# Optimizing a Trainium2 kernel written in Bass

```python
import jax, jax.numpy as jnp
from jax import lax
import numpy as np
import jax
import jax.numpy as jnp

D_MODEL = 1024
BATCH = 1
SEQ = 1024
DEPTH = 1

CTX_LEN = 256
GRID_W = 64
N_MOD = 6
EPS = 1e-6

GLA_HEADS = 4
GLA_DK = 64
GLA_DV = 128
GLA_LR = 16
GLA_TAU = 16.0
GLA_CHUNK = 64

ML_HEADS = 4
ML_DH = 128
ML_CHUNK = 64
CONV_K = 3

N_GROUPS = 4
EXP_PER_GROUP = 8
N_EXPERTS = N_GROUPS * EXP_PER_GROUP
TOP_K = 2
D_EXPERT = 512
MOE_BLOCK = 128

GLA_QK_W = GLA_HEADS * GLA_DK
GLA_V_W = GLA_HEADS * GLA_DV
ML_W = ML_HEADS * ML_DH
MIX_W = GLA_V_W + ML_W

IN_SPLITS = (GLA_QK_W, GLA_QK_W, GLA_V_W, GLA_V_W, 2 * GLA_LR, 2 * ML_W, ML_W, ML_W, 2 * ML_HEADS, 2 * ML_HEADS)
IN_W = sum(IN_SPLITS)


def rmsnorm(x, g):
    xf = x.astype(jnp.float32)
    y = xf * lax.rsqrt(jnp.mean(xf * xf, axis=-1, keepdims=True) + EPS)
    return (y * g.astype(jnp.float32)).astype(x.dtype)

def modulate(h, shift, scale):
    return h * (1 + scale) + shift

def to_heads(t, n_heads):
    b, l, w = t.shape
    return t.reshape(b, l, n_heads, w // n_heads).transpose(0, 2, 1, 3)

def from_heads(t):
    b, h, l, d = t.shape
    return t.transpose(0, 2, 1, 3).reshape(b, l, h * d)

def head_rmsnorm(t, g):
    y = t * lax.rsqrt(jnp.mean(t * t, axis=-1, keepdims=True) + EPS)
    return from_heads(y) * g.astype(jnp.float32)

def to_chunks(t, c):
    b, h, l = t.shape[:3]
    return jnp.moveaxis(t.reshape((b, h, l // c, c) + t.shape[3:]), 2, 0)

def from_chunks(t):
    n, b, h, c = t.shape[:4]
    return jnp.moveaxis(t, 0, 2).reshape((b, h, n * c) + t.shape[4:])

def flip_time(t):
    return jnp.flip(t, axis=2)

def gla_chunked(q, k, v, log_a, s0):
    mask = jnp.tril(jnp.ones((GLA_CHUNK, GLA_CHUNK), dtype=bool))

    def step(s, inp):
        qc, kc, vc, gc = inp
        b = jnp.cumsum(gc, axis=2)
        q_t = qc * jnp.exp(b)
        k_t = kc * jnp.exp(-b)
        att = jnp.where(mask, jnp.einsum('bhtd,bhsd->bhts', q_t, k_t), 0.0)
        o = jnp.einsum('bhts,bhsv->bhtv', att, vc) + jnp.einsum('bhtd,bhdv->bhtv', q_t, s)
        b_end = b[:, :, -1]
        s_new = jnp.exp(b_end)[..., None] * s + jnp.einsum(
            'bhsd,bhsv->bhdv', kc * jnp.exp(b_end[:, :, None] - b), vc)
        return s_new, o

    s_fin, o = lax.scan(step, s0, tuple(to_chunks(t, GLA_CHUNK) for t in (q, k, v, log_a)))
    return from_chunks(o), s_fin

def mlstm_chunked(q, k, v, ig, lf, state0):
    mask = jnp.tril(jnp.ones((ML_CHUNK, ML_CHUNK), dtype=bool))

    def step(state, inp):
        s, n, m = state
        qc, kc, vc, ic, fc = inp
        a = jnp.cumsum(fc, axis=-1)
        dmat = jnp.where(mask, a[..., :, None] - a[..., None, :] + ic[..., None, :], -jnp.inf)
        inter = a + m[..., None]
        m_t = jnp.maximum(inter, jnp.max(dmat, axis=-1))
        w_inter = jnp.exp(inter - m_t)
        qk = jnp.einsum('bhtd,bhsd->bhts', qc, kc) * jnp.exp(dmat - m_t[..., None])
        num = jnp.einsum('bhts,bhsv->bhtv', qk, vc) + w_inter[..., None] * jnp.einsum('bhtd,bhdv->bhtv', qc, s)
        den = jnp.sum(qk, axis=-1) + w_inter * jnp.einsum('bhtd,bhd->bht', qc, n)
        h = num / jnp.maximum(jnp.abs(den), jnp.exp(-m_t))[..., None]
        a_end = a[..., -1]
        g = a_end[..., None] - a + ic
        m_new = jnp.maximum(a_end + m, jnp.max(g, axis=-1))
        decay = jnp.exp(a_end + m - m_new)
        kw = kc * jnp.exp(g - m_new[..., None])[..., None]
        s_new = decay[..., None, None] * s + jnp.einsum('bhsd,bhsv->bhdv', kw, vc)
        n_new = decay[..., None] * n + jnp.sum(kw, axis=2)
        return (s_new, n_new, m_new), h

    state_fin, h = lax.scan(step, state0, tuple(to_chunks(t, ML_CHUNK) for t in (q, k, v, ig, lf)))
    return from_chunks(h), state_fin

def bidir(scan_fn, ctx_dirs, lat_dirs, init):
    outs_c, outs_l = [], []
    for direction in range(2):
        fl = flip_time if direction == 1 else (lambda t: t)
        oc, st = scan_fn(*[fl(t) for t in ctx_dirs[direction]], init)
        ol, _ = scan_fn(*[fl(t) for t in lat_dirs[direction]], st)
        outs_c.append(fl(oc))
        outs_l.append(fl(ol))
    return outs_c[0] + outs_c[1], outs_l[0] + outs_l[1]

def grid_conv(t, w, b, grid_w):
    bsz, l, ch = t.shape
    rows = l // grid_w
    img = t.reshape(bsz, rows, grid_w, ch)
    y = lax.conv_general_dilated(img, w.astype(t.dtype), (1, 1), 'SAME',
                                 dimension_numbers=('NHWC', 'HWIO', 'NHWC'), feature_group_count=ch)
    return y.reshape(bsz, l, ch) + b

def prepare_stream(z, grid_w, gla_up_w, gla_up_b, conv_w, conv_b, ml_i_b, ml_f_b):
    bsz, l, _ = z.shape
    zf = z.astype(jnp.float32)
    idx = np.cumsum(IN_SPLITS)[:-1].tolist()
    gq, gk, gv, gg, glr, mqk, mv, mo, mi, mf = jnp.split(zf, idx, axis=-1)
    gla_q = to_heads(gq, GLA_HEADS) * (GLA_DK ** -0.5)
    gla_k = to_heads(gk, GLA_HEADS)
    gla_v = to_heads(gv, GLA_HEADS)
    gate_logits = jnp.einsum('blrk,rkn->blrn', glr.reshape(bsz, l, 2, GLA_LR), gla_up_w) + gla_up_b
    log_a = jax.nn.log_sigmoid(gate_logits) / GLA_TAU
    gla_dirs = tuple((gla_q, gla_k, gla_v, to_heads(log_a[:, :, d], GLA_HEADS)) for d in range(2))
    qk = jax.nn.silu(grid_conv(mqk, conv_w, conv_b, grid_w))
    mq, mk = jnp.split(qk, 2, axis=-1)
    ml_q = to_heads(mq, ML_HEADS)
    ml_k = to_heads(mk, ML_HEADS) * (ML_DH ** -0.5)
    ml_v = to_heads(mv, ML_HEADS)
    ig = (mi.reshape(bsz, l, 2, ML_HEADS) + ml_i_b).transpose(2, 0, 3, 1)
    lf = jax.nn.log_sigmoid(mf.reshape(bsz, l, 2, ML_HEADS) + ml_f_b).transpose(2, 0, 3, 1)
    ml_dirs = tuple((ml_q, ml_k, ml_v, ig[d], lf[d]) for d in range(2))
    return gla_dirs, ml_dirs, gg, mo

def mixer_output(gla_h, ml_h, gg, mo, gla_norm_g, ml_norm_g, w_out, dtype):
    gla_o = head_rmsnorm(gla_h, gla_norm_g) * jax.nn.silu(gg)
    ml_o = jax.nn.sigmoid(mo) * head_rmsnorm(ml_h, ml_norm_g)
    return jnp.concatenate([gla_o, ml_o], axis=-1).astype(dtype) @ w_out

def hier_moe(h, rg_w, rg_b, re_w, re_b, e_w_in, e_w_out):
    bsz, l, d = h.shape
    t = bsz * l
    tok = h.reshape(t, d)
    g_logits = (tok @ rg_w + rg_b).astype(jnp.float32)
    p_group = jax.nn.softmax(g_logits, axis=-1)
    g_idx = jnp.argmax(g_logits, axis=-1)
    g_w = jnp.take_along_axis(p_group, g_idx[:, None], axis=-1)
    e_logits = (tok @ re_w + re_b).astype(jnp.float32).reshape(t, N_GROUPS, EXP_PER_GROUP)
    e_in_group = jnp.take_along_axis(e_logits, g_idx[:, None, None], axis=1)[:, 0]
    top_v, top_i = lax.top_k(e_in_group, TOP_K)
    weights = g_w * jax.nn.softmax(top_v, axis=-1)
    expert_ids = (g_idx[:, None] * EXP_PER_GROUP + top_i).reshape(-1)
    n_assign = t * TOP_K
    order = jnp.argsort(expert_ids)
    sorted_e = expert_ids[order]
    token_of = order // TOP_K
    counts = jnp.bincount(expert_ids, length=N_EXPERTS)
    padded = (counts + MOE_BLOCK - 1) // MOE_BLOCK * MOE_BLOCK
    pad_end = jnp.cumsum(padded)
    pad_start = pad_end - padded
    start = jnp.cumsum(counts) - counts
    dest = pad_start[sorted_e] + jnp.arange(n_assign) - start[sorted_e]
    n_blocks = (n_assign + MOE_BLOCK - 1) // MOE_BLOCK + N_EXPERTS
    buf = jnp.zeros((n_blocks * MOE_BLOCK, d), tok.dtype).at[dest].set(tok[token_of])
    block_e = jnp.minimum(jnp.searchsorted(pad_end, jnp.arange(n_blocks) * MOE_BLOCK, side='right'), N_EXPERTS - 1)

    def expert_block(args):
        xb, e = args
        gate, up = jnp.split(xb @ e_w_in[e], 2, axis=-1)
        return (jax.nn.silu(gate) * up) @ e_w_out[e]

    yb = lax.map(expert_block, (buf.reshape(n_blocks, MOE_BLOCK, d), block_e)).reshape(-1, d)
    y = yb[dest] * weights.reshape(-1)[order][:, None].astype(yb.dtype)
    out = jax.ops.segment_sum(y, token_of, num_segments=t)
    return out.reshape(bsz, l, d)

def hybrid_layer(x, ctx, c, c_ctx, ada_w, ada_b, norm1_g, w_in, gla_up_w, gla_up_b, gla_norm_g,
                 ml_conv_w, ml_conv_b, ml_i_b, ml_f_b, ml_norm_g, w_out, norm2_g,
                 rg_w, rg_b, re_w, re_b, e_w_in, e_w_out, update_ctx):
    bsz = x.shape[0]
    mod_x = (jax.nn.silu(c) @ ada_w + ada_b)[:, None, :]
    mod_c = (jax.nn.silu(c_ctx) @ ada_w + ada_b)[None, None, :]
    sh1x, sc1x, g1x, sh2x, sc2x, g2x = jnp.split(mod_x, N_MOD, axis=-1)
    sh1c, sc1c, g1c, sh2c, sc2c, g2c = jnp.split(mod_c, N_MOD, axis=-1)

    zx = modulate(rmsnorm(x, norm1_g), sh1x, sc1x) @ w_in
    zc = modulate(rmsnorm(ctx, norm1_g), sh1c, sc1c) @ w_in
    gla_c, ml_c, gg_c, mo_c = prepare_stream(zc, zc.shape[1], gla_up_w, gla_up_b, ml_conv_w, ml_conv_b, ml_i_b, ml_f_b)
    gla_x, ml_x, gg_x, mo_x = prepare_stream(zx, GRID_W, gla_up_w, gla_up_b, ml_conv_w, ml_conv_b, ml_i_b, ml_f_b)
    gla_init = jnp.zeros((bsz, GLA_HEADS, GLA_DK, GLA_DV), jnp.float32)
    ml_init = (jnp.zeros((bsz, ML_HEADS, ML_DH, ML_DH), jnp.float32),
               jnp.zeros((bsz, ML_HEADS, ML_DH), jnp.float32),
               jnp.zeros((bsz, ML_HEADS), jnp.float32))
    gla_hc, gla_hx = bidir(gla_chunked, gla_c, gla_x, gla_init)
    ml_hc, ml_hx = bidir(mlstm_chunked, ml_c, ml_x, ml_init)
    x = x + g1x * mixer_output(gla_hx, ml_hx, gg_x, mo_x, gla_norm_g, ml_norm_g, w_out, x.dtype)

    x = x + g2x * hier_moe(modulate(rmsnorm(x, norm2_g), sh2x, sc2x), rg_w, rg_b, re_w, re_b, e_w_in, e_w_out)

    if update_ctx:
        ctx = ctx + g1c * mixer_output(gla_hc, ml_hc, gg_c, mo_c, gla_norm_g, ml_norm_g, w_out, ctx.dtype)
        ctx = ctx + g2c * hier_moe(modulate(rmsnorm(ctx, norm2_g), sh2c, sc2c), rg_w, rg_b, re_w, re_b, e_w_in, e_w_out)
    return x, ctx

def first_inputs(seed: int = 0) -> dict:
    key = jax.random.key(seed)
    ks = jax.random.split(key, 26)
    nrm = lambda k, shape, s: jax.random.normal(k, shape, jnp.float32) * s
    L = DEPTH
    return {
        "x": nrm(ks[0], (BATCH, SEQ, D_MODEL), 1.0),
        "c": nrm(ks[1], (BATCH, D_MODEL), 1.0),
        "ctx": nrm(ks[2], (BATCH, CTX_LEN, D_MODEL), 1.0),
        "c_ctx": nrm(ks[3], (D_MODEL,), 1.0),
        "ada_w": nrm(ks[4], (L, D_MODEL, N_MOD * D_MODEL), D_MODEL ** -0.5),
        "ada_b": nrm(ks[5], (L, N_MOD * D_MODEL), 0.02),
        "norm1_g": 1.0 + nrm(ks[6], (L, D_MODEL), 0.02),
        "w_in": nrm(ks[7], (L, D_MODEL, IN_W), D_MODEL ** -0.5),
        "gla_up_w": nrm(ks[8], (L, 2, GLA_LR, GLA_QK_W), GLA_LR ** -0.5),
        "gla_up_b": nrm(ks[9], (L, 2, GLA_QK_W), 0.1),
        "gla_norm_g": 1.0 + nrm(ks[10], (L, GLA_V_W), 0.02),
        "ml_conv_w": nrm(ks[11], (L, CONV_K, CONV_K, 1, 2 * ML_W), 1.0 / CONV_K),
        "ml_conv_b": nrm(ks[12], (L, 2 * ML_W), 0.02),
        "ml_i_b": nrm(ks[13], (L, 2, ML_HEADS), 0.1),
        "ml_f_b": 3.0 + nrm(ks[14], (L, 2, ML_HEADS), 0.5),
        "ml_norm_g": 1.0 + nrm(ks[15], (L, ML_W), 0.02),
        "w_out": nrm(ks[16], (L, MIX_W, D_MODEL), MIX_W ** -0.5),
        "norm2_g": 1.0 + nrm(ks[17], (L, D_MODEL), 0.02),
        "router_group_w": nrm(ks[18], (L, D_MODEL, N_GROUPS), D_MODEL ** -0.5),
        "router_group_b": nrm(ks[19], (L, N_GROUPS), 0.01),
        "router_expert_w": nrm(ks[20], (L, D_MODEL, N_EXPERTS), D_MODEL ** -0.5),
        "router_expert_b": nrm(ks[21], (L, N_EXPERTS), 0.01),
        "expert_w_in": nrm(ks[22], (L, N_EXPERTS, D_MODEL, 2 * D_EXPERT), D_MODEL ** -0.5),
        "expert_w_out": nrm(ks[23], (L, N_EXPERTS, D_EXPERT, D_MODEL), D_EXPERT ** -0.5),
        "final_norm_g": 1.0 + nrm(ks[24], (D_MODEL,), 0.02),
    }

def first_block(x, c, ctx, c_ctx, ada_w, ada_b, norm1_g, w_in, gla_up_w, gla_up_b, gla_norm_g,
              ml_conv_w, ml_conv_b, ml_i_b, ml_f_b, ml_norm_g, w_out, norm2_g,
              router_group_w, router_group_b, router_expert_w, router_expert_b,
              expert_w_in, expert_w_out, final_norm_g):
    for layer in range(DEPTH):
        x, ctx = hybrid_layer(
            x, ctx, c, c_ctx, ada_w[layer], ada_b[layer], norm1_g[layer], w_in[layer],
            gla_up_w[layer], gla_up_b[layer], gla_norm_g[layer],
            ml_conv_w[layer], ml_conv_b[layer], ml_i_b[layer], ml_f_b[layer], ml_norm_g[layer],
            w_out[layer], norm2_g[layer],
            router_group_w[layer], router_group_b[layer], router_expert_w[layer], router_expert_b[layer],
            expert_w_in[layer], expert_w_out[layer], update_ctx=(layer < DEPTH - 1))
    return rmsnorm(x, final_norm_g)


D_MIX = 1024
HG_HEADS = 4
HG_KDIM = 128
HG_VDIM = 128
HG_WIDTH = HG_HEADS * HG_VDIM
HG_CHUNK = 64
SW_HEADS = 4
SW_HDIM = 64
SW_WIDTH = SW_HEADS * SW_HDIM
SW_PATTERNS = ((128, 1), (512, 4), (2048, 16))
SW_BLOCK = 128
RK_HEADS = 4
RK_HDIM = 64
RK_WIDTH = RK_HEADS * RK_HDIM
RK_DECAY_LORA = 64
RK_AAA_LORA = 64
RK_MV_LORA = 32
RK_GATE_LORA = 128
RK_GN_EPS = 64e-5
HG_IN = 4 * HG_WIDTH
SW_IN = 3 * SW_WIDTH
RK_IN = 3 * RK_WIDTH + RK_DECAY_LORA + RK_AAA_LORA + RK_GATE_LORA
N_IN = HG_IN + SW_IN + RK_IN
D_FF = 2816
CONV_W = 3
PLE_DIM = 256
NORM_EPS = 1e-6


def rmsnorm_2(x, g):
    xf = x.astype(jnp.float32)
    y = xf * lax.rsqrt(jnp.mean(xf * xf, axis=-1, keepdims=True) + NORM_EPS)
    return (y * g.astype(jnp.float32)).astype(x.dtype)

def hgrn2_mix(q_raw, f_raw, i_raw, g_raw, lower_bound, gnorm_g):
    f32 = jnp.float32
    B_, S_, _ = q_raw.shape
    nc = S_ // HG_CHUNK
    q = jax.nn.silu(q_raw.astype(f32))
    f = lower_bound + (1.0 - lower_bound) * jax.nn.sigmoid(f_raw.astype(f32))
    k = 1.0 - f
    log_f = jnp.log(f)

    def chunks(t):
        return t.reshape(B_, nc, HG_CHUNK, HG_HEADS, -1).transpose(1, 0, 3, 2, 4)

    causal = jnp.tril(jnp.ones((HG_CHUNK, HG_CHUNK), dtype=bool))

    def step(state, inp):
        qc, kc, vc, lfc = inp
        b = jnp.cumsum(lfc, axis=2)
        b_last = b[:, :, -1:, :]
        o_inter = jnp.einsum('bhck,bhkv->bhcv', qc * jnp.exp(b), state)
        rel = jnp.where(causal[:, :, None], b[:, :, :, None, :] - b[:, :, None, :, :], -jnp.inf)
        scores = jnp.einsum('bhik,bhjk,bhijk->bhij', qc, kc, jnp.exp(rel))
        o_intra = jnp.einsum('bhij,bhjv->bhiv', scores, vc)
        state = (jnp.exp(b_last[:, :, 0, :])[..., None] * state
                 + jnp.einsum('bhck,bhcv->bhkv', kc * jnp.exp(b_last - b), vc))
        return state, o_inter + o_intra

    s0 = jnp.zeros((B_, HG_HEADS, HG_KDIM, HG_VDIM), f32)
    _, o = lax.scan(step, s0, (chunks(q), chunks(k), chunks(i_raw.astype(f32)), chunks(log_f)))
    o = o.transpose(1, 0, 3, 2, 4).reshape(B_, S_, HG_HEADS, HG_VDIM)
    o = o * lax.rsqrt(jnp.mean(o * o, axis=-1, keepdims=True) + NORM_EPS)
    o = o.reshape(B_, S_, HG_WIDTH) * gnorm_g.astype(f32) * jax.nn.silu(g_raw.astype(f32))
    return o.astype(q_raw.dtype)

def banded_causal_attention(q, k, v, n_back):
    f32 = jnp.float32
    N, L, H, Dh = q.shape
    blk = SW_BLOCK
    nb = -(-L // blk)
    padw = ((0, 0), (0, nb * blk - L), (0, 0), (0, 0))
    qb = jnp.pad(q.astype(f32), padw).reshape(N, nb, blk, H, Dh)
    kb = jnp.pad(k.astype(f32), padw).reshape(N, nb, blk, H, Dh)
    vb = jnp.pad(v.astype(f32), padw).reshape(N, nb, blk, H, Dh)

    def with_prev(t):
        prev = jnp.pad(t, ((0, 0), (1, 0), (0, 0), (0, 0), (0, 0)))[:, :-1]
        return jnp.concatenate([prev, t], axis=2)

    kw, vw = with_prev(kb), with_prev(vb)
    s = jnp.einsum('nbqhd,nbkhd->nbhqk', qb, kw) * (Dh ** -0.5)
    qi = jnp.arange(blk)[:, None]
    kj = jnp.arange(2 * blk)[None, :]
    dist = qi - kj + blk
    kpos = jnp.arange(nb)[:, None, None] * blk + kj[None] - blk
    valid = (dist >= 0)[None] & (dist <= n_back)[None] & (kpos >= 0)
    s = jnp.where(valid[None, :, None], s, -jnp.inf)
    lse = jax.nn.logsumexp(s, axis=-1)
    prob = jnp.exp(s - lse[..., None])
    o = jnp.einsum('nbhqk,nbkhd->nbqhd', prob, vw).reshape(N, nb * blk, H, Dh)[:, :L]
    lse = lse.transpose(0, 1, 3, 2).reshape(N, nb * blk, H)[:, :L]
    return o, lse

def stride_gather(t, dil):
    B_, S_ = t.shape[:2]
    rest = t.shape[2:]
    return t.reshape((B_, S_ // dil, dil) + rest).swapaxes(1, 2).reshape((B_ * dil, S_ // dil) + rest)

def stride_scatter(t, B_, dil):
    L = t.shape[1]
    rest = t.shape[2:]
    return t.reshape((B_, dil, L) + rest).swapaxes(1, 2).reshape((B_, L * dil) + rest)

def dilated_window_mix(q_raw, k_raw, v_raw):
    B_, S_, _ = q_raw.shape
    q, k, v = (t.reshape(B_, S_, SW_HEADS, SW_HDIM) for t in (q_raw, k_raw, v_raw))
    outs, lses = [], []
    for window, dil in SW_PATTERNS:
        o, lse = banded_causal_attention(stride_gather(q, dil), stride_gather(k, dil),
                                         stride_gather(v, dil), window // dil)
        outs.append(stride_scatter(o, B_, dil))
        lses.append(stride_scatter(lse, B_, dil))
    wts = jax.nn.softmax(jnp.stack(lses, 0), axis=0)
    o = jnp.sum(wts[..., None] * jnp.stack(outs, 0), axis=0)
    return o.reshape(B_, S_, SW_WIDTH).astype(q_raw.dtype)

def rwkv7_mix(c, mu, w0, w2, a0, a2, g2, k_k, k_a, r_k, ln_w, ln_b, v_first, v_res):
    f32 = jnp.float32
    B_, S_, _ = c.shape
    cf = c.astype(f32)
    c_prev = jnp.pad(cf, ((0, 0), (1, 0), (0, 0)))[:, :-1]
    cm = cf + (c_prev - cf) * mu
    splits = [RK_WIDTH, 2 * RK_WIDTH, 3 * RK_WIDTH, 3 * RK_WIDTH + RK_DECAY_LORA,
              3 * RK_WIDTH + RK_DECAY_LORA + RK_AAA_LORA]
    r, k, v, wd, ad, gd = jnp.split(cm, splits, axis=-1)
    w = -jax.nn.softplus(-(w0 + jnp.tanh(wd) @ w2)) - 0.5
    decay = jnp.exp(-jnp.exp(w))
    a = jax.nn.sigmoid(a0 + ad @ a2)
    g = jax.nn.sigmoid(gd) @ g2
    if v_res is None:
        v_first = v
    else:
        v0, v1, v2 = v_res
        v = v + (v_first - v) * jax.nn.sigmoid(v0 + (v @ v1) @ v2)

    def heads(t):
        return t.reshape(B_, S_, RK_HEADS, RK_HDIM)

    kk = heads(k * k_k)
    kk = kk / jnp.maximum(jnp.linalg.norm(kk, axis=-1, keepdims=True), 1e-12)
    k = k * (1.0 + (a - 1.0) * k_a)
    rh, kh, vh, wh, ah = heads(r), heads(k), heads(v), heads(decay), heads(a)

    def step(state, inp):
        r_t, w_t, k_t, v_t, kk_t, a_t = inp
        sa = jnp.einsum('bhvk,bhk->bhv', state, -kk_t)
        state = (state * w_t[:, :, None, :] + sa[..., None] * (kk_t * a_t)[:, :, None, :]
                 + v_t[..., None] * k_t[:, :, None, :])
        return state, jnp.einsum('bhvk,bhk->bhv', state, r_t)

    s0 = jnp.zeros((B_, RK_HEADS, RK_HDIM, RK_HDIM), f32)
    xs = (rh.swapaxes(0, 1), wh.swapaxes(0, 1), kh.swapaxes(0, 1), vh.swapaxes(0, 1),
          kk.swapaxes(0, 1), ah.swapaxes(0, 1))
    _, y = lax.scan(step, s0, xs)
    y = y.swapaxes(0, 1)
    mean = jnp.mean(y, axis=-1, keepdims=True)
    var = jnp.mean((y - mean) ** 2, axis=-1, keepdims=True)
    y = ((y - mean) * lax.rsqrt(var + RK_GN_EPS)).reshape(B_, S_, RK_WIDTH) * ln_w + ln_b
    bonus = jnp.sum(rh * kh * r_k, axis=-1, keepdims=True) * vh
    y = (y + bonus.reshape(B_, S_, RK_WIDTH)) * g
    return y.astype(c.dtype), v_first

def conv_glu_ffn(hn, w_up, conv_w, conv_b, w_down):
    u = hn @ w_up
    S_ = u.shape[1]
    up = jnp.pad(u, ((0, 0), (CONV_W - 1, 0), (0, 0)))
    uc = conv_b + conv_w[0] * up[:, 0:S_]
    for j in range(1, CONV_W):
        uc = uc + conv_w[j] * up[:, j:j + S_]
    gate, val = jnp.split(uc, 2, axis=-1)
    return (jax.nn.silu(gate) * val) @ w_down

def second_inputs(seed: int = 0) -> dict:
    key = jax.random.key(seed)
    ks = iter(jax.random.split(key, 40))

    def nrm(shape, scale):
        return jax.random.normal(next(ks), shape, jnp.float32) * scale

    def unif(shape, lo, hi):
        return jax.random.uniform(next(ks), shape, jnp.float32, lo, hi)

    L = DEPTH
    return {
        'x': nrm((BATCH, SEQ, D_MODEL), 1.0),
        'p': nrm((DEPTH, BATCH, SEQ, PLE_DIM), 1.0),
        'w_in': nrm((L, D_MODEL, N_IN), D_MODEL ** -0.5),
        'w_out': nrm((L, D_MIX, D_MODEL), D_MIX ** -0.5),
        'norm_mix_g': 1.0 + nrm((L, D_MODEL), 0.02),
        'norm_ffn_g': 1.0 + nrm((L, D_MODEL), 0.02),
        'norm_ple_g': 1.0 + nrm((L, D_MODEL), 0.02),
        'final_norm_g': 1.0 + nrm((D_MODEL,), 0.02),
        'hgrn_lower_bounds': nrm((L, HG_HEADS * HG_KDIM), 0.5),
        'hgrn_gnorm_g': 1.0 + nrm((L, HG_WIDTH), 0.02),
        'rwkv_mu': unif((L, RK_IN), 0.0, 1.0),
        'rwkv_w0': unif((L, RK_WIDTH), -5.0, -0.5),
        'rwkv_w2': nrm((L, RK_DECAY_LORA, RK_WIDTH), 0.1 * RK_DECAY_LORA ** -0.5),
        'rwkv_a0': nrm((L, RK_WIDTH), 0.1),
        'rwkv_a2': nrm((L, RK_AAA_LORA, RK_WIDTH), 0.1 * RK_AAA_LORA ** -0.5),
        'rwkv_g2': nrm((L, RK_GATE_LORA, RK_WIDTH), RK_GATE_LORA ** -0.5),
        'rwkv_k_k': 0.85 + nrm((L, RK_WIDTH), 0.05),
        'rwkv_k_a': 1.0 + nrm((L, RK_WIDTH), 0.05),
        'rwkv_r_k': nrm((L, RK_HEADS, RK_HDIM), 0.1),
        'rwkv_ln_w': 1.0 + nrm((L, RK_WIDTH), 0.02),
        'rwkv_ln_b': nrm((L, RK_WIDTH), 0.02),
        'rwkv_v0': 1.0 + nrm((L - 1, RK_WIDTH), 0.1),
        'rwkv_v1': nrm((L - 1, RK_WIDTH, RK_MV_LORA), 0.1 * RK_WIDTH ** -0.5),
        'rwkv_v2': nrm((L - 1, RK_MV_LORA, RK_WIDTH), 0.1 * RK_MV_LORA ** -0.5),
        'ffn_up': nrm((L, D_MODEL, 2 * D_FF), D_MODEL ** -0.5),
        'ffn_conv_w': nrm((L, CONV_W, 2 * D_FF), CONV_W ** -0.5),
        'ffn_conv_b': nrm((L, 2 * D_FF), 0.02),
        'ffn_down': nrm((L, D_FF, D_MODEL), D_FF ** -0.5),
        'ple_proj': nrm((L, PLE_DIM, D_MODEL), PLE_DIM ** -0.5),
        'ple_gate': nrm((L, D_MODEL, D_MODEL), D_MODEL ** -0.5),
    }

def second_block(x, p, w_in, w_out, norm_mix_g, norm_ffn_g, norm_ple_g, final_norm_g,
              hgrn_lower_bounds, hgrn_gnorm_g, rwkv_mu, rwkv_w0, rwkv_w2, rwkv_a0, rwkv_a2,
              rwkv_g2, rwkv_k_k, rwkv_k_a, rwkv_r_k, rwkv_ln_w, rwkv_ln_b, rwkv_v0, rwkv_v1,
              rwkv_v2, ffn_up, ffn_conv_w, ffn_conv_b, ffn_down, ple_proj, ple_gate):
    lbs = jax.nn.softmax(hgrn_lower_bounds.astype(jnp.float32), axis=0)
    lbs = jnp.cumsum(lbs, axis=0) - lbs[0]
    splits = [HG_WIDTH, 2 * HG_WIDTH, 3 * HG_WIDTH, 4 * HG_WIDTH,
              HG_IN + SW_WIDTH, HG_IN + 2 * SW_WIDTH, HG_IN + 3 * SW_WIDTH]
    h = x
    v_first = None
    for l in range(DEPTH):
        z = rmsnorm_2(h, norm_mix_g[l]) @ w_in[l]
        a_q, a_f, a_i, a_g, b_q, b_k, b_v, c_in = jnp.split(z, splits, axis=-1)
        o_a = hgrn2_mix(a_q, a_f, a_i, a_g, lbs[l], hgrn_gnorm_g[l])
        o_b = dilated_window_mix(b_q, b_k, b_v)
        v_res = None if l == 0 else (rwkv_v0[l - 1], rwkv_v1[l - 1], rwkv_v2[l - 1])
        o_c, v_first = rwkv7_mix(c_in, rwkv_mu[l], rwkv_w0[l], rwkv_w2[l], rwkv_a0[l], rwkv_a2[l],
                                 rwkv_g2[l], rwkv_k_k[l], rwkv_k_a[l], rwkv_r_k[l], rwkv_ln_w[l],
                                 rwkv_ln_b[l], v_first, v_res)
        h = h + jnp.concatenate([o_a, o_b.astype(o_a.dtype), o_c.astype(o_a.dtype)], axis=-1) @ w_out[l]
        h = h + conv_glu_ffn(rmsnorm_2(h, norm_ffn_g[l]), ffn_up[l], ffn_conv_w[l], ffn_conv_b[l], ffn_down[l])
        gate = jax.nn.sigmoid(rmsnorm_2(h, norm_ple_g[l]) @ ple_gate[l])
        h = h + gate * (p[l] @ ple_proj[l])
    return rmsnorm_2(h, final_norm_g)


def setup_inputs(seed=0):
    out = dict(first_inputs(seed))
    for name, value in second_inputs(seed + 1).items():
        if name != "x":
            out[name + "_2"] = value
    return out


def reference(
    x, c, ctx, c_ctx, ada_w, ada_b, norm1_g, w_in, gla_up_w, gla_up_b, gla_norm_g, ml_conv_w,
    ml_conv_b, ml_i_b, ml_f_b, ml_norm_g, w_out, norm2_g, router_group_w, router_group_b,
    router_expert_w, router_expert_b, expert_w_in, expert_w_out, final_norm_g, p_2, w_in_2,
    w_out_2, norm_mix_g_2, norm_ffn_g_2, norm_ple_g_2, final_norm_g_2, hgrn_lower_bounds_2,
    hgrn_gnorm_g_2, rwkv_mu_2, rwkv_w0_2, rwkv_w2_2, rwkv_a0_2, rwkv_a2_2, rwkv_g2_2,
    rwkv_k_k_2, rwkv_k_a_2, rwkv_r_k_2, rwkv_ln_w_2, rwkv_ln_b_2, rwkv_v0_2, rwkv_v1_2,
    rwkv_v2_2, ffn_up_2, ffn_conv_w_2, ffn_conv_b_2, ffn_down_2, ple_proj_2, ple_gate_2,
):
    x = first_block(
        x, c, ctx, c_ctx, ada_w, ada_b, norm1_g, w_in, gla_up_w, gla_up_b, gla_norm_g,
        ml_conv_w, ml_conv_b, ml_i_b, ml_f_b, ml_norm_g, w_out, norm2_g, router_group_w,
        router_group_b, router_expert_w, router_expert_b, expert_w_in, expert_w_out,
        final_norm_g,
    )
    return second_block(
        x, p_2, w_in_2, w_out_2, norm_mix_g_2, norm_ffn_g_2, norm_ple_g_2, final_norm_g_2,
        hgrn_lower_bounds_2, hgrn_gnorm_g_2, rwkv_mu_2, rwkv_w0_2, rwkv_w2_2, rwkv_a0_2,
        rwkv_a2_2, rwkv_g2_2, rwkv_k_k_2, rwkv_k_a_2, rwkv_r_k_2, rwkv_ln_w_2, rwkv_ln_b_2,
        rwkv_v0_2, rwkv_v1_2, rwkv_v2_2, ffn_up_2, ffn_conv_w_2, ffn_conv_b_2, ffn_down_2,
        ple_proj_2, ple_gate_2,
    )


_drawn_inputs = setup_inputs


def setup_inputs(seed=0):
    import zlib

    import numpy as np

    out = dict(_drawn_inputs(seed))
    spreads = {}
    factors = {'ml_conv_b': 8.0,
     'ml_i_b': 32.304,
     'ml_norm_g': 3.135,
     'router_group_b': 3.39,
     'router_expert_b': 4.132,
     'norm_mix_g_2': 3.732,
     'norm_ffn_g_2': 14.378,
     'norm_ple_g_2': 200.0,
     'final_norm_g_2': 22.097,
     'hgrn_gnorm_g_2': 25.276,
     'rwkv_w2_2': 8.0,
     'rwkv_a0_2': 4.74,
     'rwkv_a2_2': 4.954,
     'rwkv_k_k_2': 17.669,
     'rwkv_k_a_2': 3.34,
     'rwkv_ln_w_2': 200.0,
     'rwkv_ln_b_2': 200.0,
     'ffn_conv_b_2': 14.155,
     'ple_gate_2': 22.36,
     'p_2': 8.0,
     'ple_proj_2': 8.0}
    for name, (base, spread) in spreads.items():
        noise = np.random.default_rng([zlib.crc32(name.encode()), seed]).standard_normal(out[name].shape)
        drawn = base * np.exp(spread * noise) if base else spread * noise
        out[name] = jnp.asarray(drawn.astype(out[name].dtype))
    for name, factor in factors.items():
        out[name] = (out[name] * factor).astype(out[name].dtype)
    return out
```

```python
from contextlib import ExitStack, contextmanager

import numpy as np

import concourse.bass as bass
from concourse import mybir

F32 = mybir.dt.float32
I32 = mybir.dt.int32
U32 = mybir.dt.uint32
ALU = mybir.AluOpType
ACT = mybir.ActivationFunctionType
AX = mybir.AxisListType

P = 128
D = 1024
KT = D // P
T = 1024
NCTX = 256
TALL = NCTX + T
TSCAN = TALL + NCTX
NCH = TALL // P
BANK = 512
EPS = 1e-6
RK_GN_EPS = 64e-5

GQ, GK, GV, GG, GLR, MQK, MV, MO, MI, MF = 0, 256, 512, 1024, 1536, 1568, 2592, 3104, 3616, 3624
NE, EPG, NG, DE = 32, 8, 4, 512
NBLK = 2 * T // P + NE
NFF = 2816


def constants():
    s, t = np.arange(P)[:, None], np.arange(P)[None, :]
    one = lambda m: m.astype(np.float32)
    mid = one(s < 64)
    parts = {
        "ident": one(s == t), "ones": np.ones((P, P), np.float32),
        "tri0": one(s <= t), "tri1": one(s >= t),
        "mid0": one(s <= t) - mid, "mid1": one(s >= t) - one(s >= 64),
        "after0": one(s > t), "after1": one(s < t),
        "neg0": -1e30 * one(s > t), "neg1": -1e30 * one(s < t),
        "selrow": one(np.arange(4 * P)[None, :] // P == s),
        "mean1024": np.full((P, P), 1.0 / 1024, np.float32),
        "mean128": np.full((P, P), 1.0 / 128, np.float32),
        "mean64": one(s // 64 == t // 64) / 64, "ones64": one(s // 64 == t // 64),
        "lt_half": one((s // 64 == t // 64) & (s < t)), "le_half": one((s // 64 == t // 64) & (s <= t)),
        "halves": one(np.arange(P)[:, None] // 64 == np.arange(2)[None, :]),
        "lt64": one((s < t) & (t < 64)), "le64": one((s <= t) & (t < 64)),
        "before": one(s < t), "iota": np.broadcast_to(np.arange(64, dtype=np.float32), (P, 64)),
    }
    for lv in (8, 16, 32, 64):
        parts[f"level{lv}"] = one((s // (2 * lv) == t // (2 * lv)) & (s % (2 * lv) < lv) & (t % (2 * lv) >= lv))
    for lv in (1, 2, 4, 8, 16, 32):
        parts[f"pair{lv}"] = one((s // (2 * lv) == t // (2 * lv)) & (s % (2 * lv) < lv) & (t % (2 * lv) >= lv))
        parts[f"pairT{lv}"] = parts[f"pair{lv}"].T
    q, k = np.arange(P)[:, None], np.arange(T)[None, :]
    dist = q + T - P - k
    mult = one((dist >= 0) & (dist <= 128)) + one((dist >= 0) & (dist % 4 == 0) & (dist <= 512)) \
        + one((dist >= 0) & (dist % 16 == 0) & (dist <= 2048))
    wide = {"mult": mult, "multneg": np.where(mult > 0, 0, -1e30)}

    def pack(parts):
        at, n = {}, 0
        for name, a in parts.items():
            at[name] = (n, a.shape[1])
            n += a.shape[1]
        return at, np.ascontiguousarray(np.concatenate(list(parts.values()), 1).astype(np.float32))
    at, const = pack(parts)
    return at, const, pack(wide)[1]


class Count:

    def __init__(self, eng, sem, base=0, n=0):
        self.eng, self.sem, self.base, self.n = eng, sem, base, n

    def __call__(self, ins):
        self.n += 1
        ins.then_inc(self.sem, 1)
        self.eng.wait_ge(self.sem, self.base + self.n)

    def mark(self, ins):
        self.n += 1
        ins.then_inc(self.sem, 1)


class Core:

    def __init__(self, nc, A, const_at, const, wide, out, stack):
        self.nc, self.A, self.out, self.stack = nc, A, out, stack
        self.const_at, self.const_dram, self.wide_dram = const_at, const, wide
        self.scratch = {}
        self.nsem = 0

    def sb(self, name, shape, dt=F32, stack=None):
        return (stack or self.stack).enter_context(self.nc.sbuf_tensor(name, shape, dt))

    def ps(self, name, shape, stack, dt=F32):
        return stack.enter_context(self.nc.psum_tensor(name + "_psum", shape, dt))

    @contextmanager
    def stage(self):
        with ExitStack() as st:
            self.held = []
            yield st
            self.nc.clear_and_free_semaphores(self.held)
            self.nc.all_engine_barrier()

    def sem(self, name):
        self.held.append(self.nc.alloc_semaphore(name))
        return self.held[-1]

    def dram(self, name, shape, dt=F32):
        self.scratch[name] = self.nc.dram_tensor(name, shape, dt, kind="Internal").ap()
        return self.scratch[name]

    def c(self, name):
        o, n = self.const_at[name]
        return self.const[:, o:o + n]

    def col(self, name, j=0):
        return self.cols[:, self.col_at[name] + j:self.col_at[name] + j + 1]


VECS = [("norm1_g", 8), ("gla_norm_g", 4), ("ml_norm_g", 4), ("ml_conv_b", 8), ("norm2_g", 8),
        ("final_norm_g", 8), ("norm_mix_g_2", 8), ("norm_ffn_g_2", 8), ("norm_ple_g_2", 8),
        ("final_norm_g_2", 8), ("hgrn_gnorm_g_2", 4), ("hgrn_lower_bounds_2", 4), ("rwkv_mu_2", 8),
        ("ml_conv_w", 72), ("ffn_conv_w_2", 132), ("ffn_conv_b_2", 44),
        ("rwkv_w0_2", 2), ("rwkv_a0_2", 2), ("rwkv_k_k_2", 2), ("rwkv_k_a_2", 2), ("rwkv_r_k_2", 2),
        ("rwkv_ln_w_2", 2), ("rwkv_ln_b_2", 2)]


def flat_rows(ap, w):
    while len(ap.shape) > 1:
        names = " ".join("abcdef"[:len(ap.shape)])
        ap = ap.rearrange(f"{names} -> ({names})")
    return ap.rearrange("(r w) -> r w", w=w)


def stage_setup(K):
    nc, A = K.nc, K.A
    nconst = K.const_dram.shape[1]
    K.const = K.sb("const", [P, nconst])
    total = sum(n for _, n in VECS)
    ntile = -(-total // P)
    K.cols = K.sb("cols", [P, ntile * P])
    K.modcols = K.sb("modcols", [P, 64])
    K.col_at, at = {}, 0
    for name, n in VECS:
        K.col_at[name] = at
        at += n
    mod = K.dram("mod", [2, 6 * D])
    with K.stage() as st:
        rows = [K.sb(f"vec_rows{i}", [P, P], stack=st) for i in range(ntile)]
        mrows = K.sb("mod_rows", [64, P], stack=st)
        crow = K.sb("cond_rows", [16, P], stack=st)
        csil = K.sb("cond_silu", [P, 8, 2], stack=st)
        brow = K.sb("ada_bias", [2, 6 * D], stack=st)
        mout = K.sb("mod_out", [2, 6 * D], stack=st)
        NW = 3
        aw = [K.sb(f"ada_w{i}", [P, 8, 512], stack=st) for i in range(NW)]
        pt = K.ps("vec_ps", [P, ntile * P], st)
        pm = [K.ps(f"mod_ps{i}", [2, 512], st) for i in range(2)]
        s_const, s_rows, s_cond, s_bias = (K.sem(f"setup_{x}") for x in ("const", "rows", "cond", "bias"))
        s_aw = [K.sem(f"setup_ada{i}") for i in range(NW)]
        s_mm, s_ev, s_t, s_tc, s_zero, s_mod, s_modrows, s_sil = (
            K.sem(f"setup_{x}") for x in ("mod_mm", "mod_ev", "turned", "copied", "zero", "mod_out", "mod_rows", "silu"))
        pieces = []
        for name, n in VECS:
            src, r = flat_rows(A[name], P), 0
            while r < n:
                g = K.col_at[name] + r
                k = min(n - r, P - g % P)
                pieces.append((g // P, g % P, k, src[r:r + k, :]))
                r += k
        last = total % P
        with nc.Block() as block:
            @block.sync
            def _(sp):
                sp.dma_start(K.const[:], K.const_dram).then_inc(s_const, 16)
                sp.dma_start(crow[0:8, :], flat_rows(A["c"], P)).then_inc(s_cond, 16)
                sp.dma_start(crow[8:16, :], flat_rows(A["c_ctx"], P)).then_inc(s_cond, 16)
                for r in range(2):
                    sp.dma_start(brow[r:r + 1, :], A["ada_b"]).then_inc(s_bias, 16)
                for n in range(12):
                    if n >= NW:
                        sp.wait_ge(s_mm, n - NW + 1)
                    sp.dma_start(aw[n % NW][:], A["ada_w"][0, :, n * 512:(n + 1) * 512].rearrange("(k p) n -> p k n", p=P)) \
                        .then_inc(s_aw[n % NW], 16)
                sp.wait_ge(s_ev, 12)
                sp.dma_start(mod, mout[:]).then_inc(s_mod, 16)
                sp.wait_ge(s_mod, 16)
                sp.dma_start(mrows[0:48, :], flat_rows(mod[0:1, :], P)).then_inc(s_modrows, 16)
                sp.dma_start(mrows[48:64, :], flat_rows(mod[1:2, 0:2 * D], P)).then_inc(s_modrows, 16)

            @block.gpsimd
            def _(pool):
                if last:
                    nc.gpsimd.memset(rows[-1][:], 0.0).then_inc(s_zero, 1)
                    pool.wait_ge(s_zero, 1)
                for i, r, k, src in pieces:
                    pool.dma_start(rows[i][r:r + k, :], src).then_inc(s_rows, 16)

            @block.scalar
            def _(act):
                act.wait_ge(s_t, 1)
                act.activation(csil[:].rearrange("p k r -> p r k"), pt[:, 0:16].rearrange("p (r k) -> p r k", r=2),
                               ACT.Silu).then_inc(s_sil, 1)

            @block.tensor
            def _(pe):
                pe.wait_ge(s_const, 16)
                pe.wait_ge(s_cond, 32)
                pe.transpose(pt[:, 0:16], crow[:], K.c("ident")[0:16, 0:16]).then_inc(s_t, 1)
                pe.wait_ge(s_sil, 1)
                for n in range(12):
                    pe.wait_ge(s_aw[n % NW], 16 * (n // NW + 1))
                    if n >= 2:
                        pe.wait_ge(s_ev, n - 1)
                    for k in range(8):
                        mm = pe.matmul(pm[n % 2][:], csil[:, k, :], aw[n % NW][:, k, :], start=k == 0, stop=k == 7)
                    mm.then_inc(s_mm, 1)
                pe.wait_ge(s_rows, 16 * len(pieces))
                for i in range(ntile):
                    mm = pe.transpose(pt[:, i * P:(i + 1) * P], rows[i][:], K.c("ident"))
                mm.then_inc(s_t, 1)
                pe.wait_ge(s_tc, 1)
                pe.wait_ge(s_modrows, 32)
                pe.transpose(pt[:, 0:64], mrows[:], K.c("ident")[0:64, 0:64]).then_inc(s_t, 1)

            @block.vector
            def _(dve):
                dve.wait_ge(s_bias, 32)
                for n in range(12):
                    dve.wait_ge(s_mm, n + 1)
                    dve.tensor_tensor(mout[:, n * 512:(n + 1) * 512], pm[n % 2][:], brow[:, n * 512:(n + 1) * 512],
                                      ALU.add).then_inc(s_ev, 1)
                dve.wait_ge(s_t, 2)
                dve.tensor_copy(K.cols[:], pt[:]).then_inc(s_tc, 1)
                dve.wait_ge(s_t, 3)
                dve.tensor_copy(K.modcols[:], pt[:, 0:64]).then_inc(s_tc, 1)
                dve.wait_ge(s_tc, 2)
                for o in (8, 32, 56):
                    dve.tensor_scalar(K.modcols[:, o:o + 8], K.modcols[:, o:o + 8], 1.0, None, ALU.add)


def stage_turn_in(K):
    nc, A = K.nc, K.A
    ctxF = K.ctxF
    with K.stage() as st:
        xin = [K.sb(f"x_rows{i}", [P, D], stack=st) for i in range(4)]
        pt = [K.ps(f"turn_ps{i}", [P, 2, 512], st) for i in range(3)]
        s_x = [K.sem(f"turn_x{i}") for i in range(4)]
        s_t, s_c = K.sem("turn_done"), K.sem("turn_copied")
        tiles = [("c", i) for i in range(NCTX // P)] + [("x", i) for i in range(T // P)]
        with nc.Block() as block:
            @block.sync
            def _(sp):
                for n, (w, i) in enumerate(tiles):
                    if n >= 4:
                        sp.wait_ge(s_t, n - 3)
                    src = A["x" if w == "x" else "ctx"][0, i * P:(i + 1) * P, :]
                    sp.dma_start(xin[n % 4][:], src).then_inc(s_x[n % 4], 16)

            @block.tensor
            def _(pe):
                for n in range(len(tiles)):
                    pe.wait_ge(s_x[n % 4], 16 * (n // 4 + 1))
                    if n >= 3:
                        pe.wait_ge(s_c, n - 2)
                    for k in range(8):
                        mm = pe.transpose(pt[n % 3][:, k // 4, (k % 4) * P:(k % 4 + 1) * P],
                                          xin[n % 4][:, k * P:(k + 1) * P], K.c("ident"))
                    mm.then_inc(s_t, 1)

            @block.vector
            def _(dve):
                for n, (w, i) in enumerate(tiles):
                    dve.wait_ge(s_t, n + 1)
                    dst = (K.hF if w == "x" else ctxF)[:, :, i * P:(i + 1) * P]
                    dve.tensor_copy(dst, pt[n % 3][:].rearrange("p a (b t) -> p (a b) t", b=4)).then_inc(s_c, 1)


def stage_norm(K, name, src, dst, ntok, gain, shift=None, scale=None):
    nc = K.nc
    W = min(512, ntok)
    with K.stage() as st:
        sq = [K.sb(f"{name}_sq{i}", [P, W], stack=st) for i in range(4)]
        rstd = [K.sb(f"{name}_rstd{i}", [P, W], stack=st) for i in range(2)]
        gm = K.sb(f"{name}_gain", [P, 8], stack=st)
        pm = [K.ps(f"{name}_ps{i}", [P, W], st) for i in range(2)]
        s_sq, s_used, s_ms, s_v, s_rt, s_n, s_g, s_out = (
            K.sem(f"{name}_{x}") for x in ("sq", "sq_used", "ms", "var", "root", "normed", "gain", "out"))
        nh = ntok // W
        with nc.Block() as block:
            @block.scalar
            def _(act):
                def squares(h):
                    for k in range(8):
                        n = 8 * h + k
                        if n >= 4:
                            act.wait_ge(s_used, n - 3)
                        act.activation(sq[n % 4][:], src[:, k, h * W:(h + 1) * W], ACT.Square).then_inc(s_sq, 1)

                def root(h):
                    act.wait_ge(s_v, 2 * h + 1)
                    act.activation(rstd[h][:], rstd[h][:], ACT.Sqrt).then_inc(s_rt, 1)

                def affine(h):
                    if h == 0:
                        act.wait_ge(s_g, 1)
                    for k in range(8):
                        act.wait_ge(s_n, 8 * h + k + 1)
                        t = dst[:, k, h * W:(h + 1) * W]
                        act.activation(t, t, ACT.Identity, bias=shift[:, k:k + 1], scale=gm[:, k:k + 1]).then_inc(s_out, 1)
                for h in range(nh):
                    squares(h)
                for h in range(nh):
                    root(h)
                if shift is not None:
                    for h in range(nh):
                        affine(h)

            @block.tensor
            def _(pe):
                for h in range(nh):
                    for k in range(8):
                        pe.wait_ge(s_sq, 8 * h + k + 1)
                        mm = pe.matmul(pm[h][:], K.c("mean1024"), sq[(8 * h + k) % 4][:], start=k == 0, stop=k == 7)
                        mm.then_inc(s_used, 1)

            @block.vector
            def _(dve):
                if shift is not None:
                    dve.tensor_tensor(gm[:], gain, scale, ALU.mult).then_inc(s_g, 1)
                for h in range(nh):
                    dve.wait_ge(s_used, 8 * h + 8)
                    dve.tensor_scalar(rstd[h][:], pm[h][:], EPS, None, ALU.add).then_inc(s_v, 1)
                    dve.wait_ge(s_rt, h + 1)
                    dve.reciprocal(rstd[h][:], rstd[h][:]).then_inc(s_v, 1)
                    dve.wait_ge(s_v, 2 * h + 2)
                    for k in range(8):
                        s, d = src[:, k, h * W:(h + 1) * W], dst[:, k, h * W:(h + 1) * W]
                        if shift is not None:
                            dve.tensor_tensor(d, s, rstd[h][:], ALU.mult).then_inc(s_n, 1)
                        else:
                            dve.scalar_tensor_tensor(d, s, gain[:, k:k + 1], rstd[h][:], ALU.mult, ALU.mult).then_inc(s_n, 1)


def stage_gemm_f(K, name, w, ncol, src, ntok, dst, func=None, scale=1.0, residual=None, gcol=None, kt=KT, ctx=None):
    nc = K.nc
    npair = ncol // (2 * P)
    NT = ntok // BANK
    with K.stage() as st:
        wt = [K.sb(f"{name}_w{i}", [P, kt, P], stack=st) for i in range(2)]
        nps = NT + (1 if ctx is not None else 0)
        pm = [K.ps(f"{name}_ps{i}", [P, nps, BANK], st) for i in range(2)]
        ob = [K.sb(f"{name}_out{i}", [P, nps * BANK], stack=st) for i in range(2)]
        s_w = [K.sem(f"{name}_w{i}") for i in range(2)]
        s_o = [K.sem(f"{name}_o{i}") for i in range(2)]
        s_mm = [K.sem(f"{name}_mm{i}") for i in range(2)]
        s_ev = [K.sem(f"{name}_ev{i}") for i in range(2)]
        ndma = 3 if ctx is not None else 1
        with nc.Block() as block:
            @block.sync
            def _(sp):
                with sp.Fori(0, npair) as i:
                    for u in range(2):
                        sp.wait_ge(s_mm[u], i)
                        sp.dma_start(wt[u][:], w[:, bass.ds(i * 2 * P + u * P, P)].rearrange("(k p) n -> p k n", p=P)) \
                            .then_inc(s_w[u], 16)

            @block.tensor
            def _(pe):
                with pe.Fori(0, npair) as i:
                    for u in range(2):
                        pe.wait_ge(s_w[u], (i + 1) * 16)
                        pe.wait_ge(s_ev[u], i)
                        for h in range(nps):
                            for k in range(kt):
                                if h < NT:
                                    o, r = pm[u][:, h, :], src[:, k, h * BANK:(h + 1) * BANK]
                                else:
                                    o, r = pm[u][:, h, 0:NCTX], ctx[:, k, :]
                                mm = pe.matmul(o, wt[u][:, k, :], r, start=k == 0, stop=k == kt - 1)
                        mm.then_inc(s_mm[u], 1)

            if residual is None:
                @block.scalar
                def _(act):
                    with act.Fori(0, npair) as i:
                        for u in range(2):
                            act.wait_ge(s_mm[u], i + 1)
                            act.wait_ge(s_o[u], i * 16 * ndma)
                            n = T + NCTX if ctx is not None else ntok
                            act.activation(ob[u][:, 0:n], pm[u][:].rearrange("p a b -> p (a b)")[:, 0:n], func, scale=scale) \
                                .then_inc(s_ev[u], 1)
                            act.wait_ge(s_ev[u], i + 1)
                            rows = bass.ds(i * 2 * P + u * P, P)
                            if ctx is not None:
                                act.dma_start(dst[rows, NCTX:NCTX + T], ob[u][:, 0:T]).then_inc(s_o[u], 16)
                                act.dma_start(dst[rows, 0:NCTX], ob[u][:, T:n]).then_inc(s_o[u], 16)
                                act.dma_start(dst[rows, NCTX + T:TSCAN], ob[u][:, T:n]).then_inc(s_o[u], 16)
                            else:
                                act.dma_start(dst[rows, :], ob[u][:, 0:n]).then_inc(s_o[u], 16)
                    for u in range(2):
                        act.wait_ge(s_o[u], npair * 16 * ndma)
            else:
                @block.vector
                def _(dve):
                    flat = residual[:].rearrange("p k t -> p (k t)")
                    with dve.Fori(0, npair) as i:
                        for u in range(2):
                            dve.wait_ge(s_mm[u], i + 1)
                            h = flat[:, bass.ds(i * 2 * ntok + u * ntok, ntok)]
                            if gcol is None:
                                dve.tensor_tensor(h, pm[u][:].rearrange("p a b -> p (a b)"), h, ALU.add).then_inc(s_ev[u], 1)
                            else:
                                dve.scalar_tensor_tensor(h, pm[u][:].rearrange("p a b -> p (a b)"),
                                                         gcol[:, bass.ds(i * 2 + u, 1)], h, ALU.mult, ALU.add).then_inc(s_ev[u], 1)


def stage_gemm_t(K, name, groups, toks):
    nc = K.nc
    NB = 4
    with K.stage() as st:
        wt = [K.sb(f"{name}_w{i}", [P, KT, BANK], stack=st) for i in range(2)]
        pm = [K.ps(f"{name}_ps{i}", [P, BANK], st) for i in range(NB)]
        ob = [K.sb(f"{name}_out{i}", [P, BANK], stack=st) for i in range(NB)]
        s_w = [K.sem(f"{name}_w{i}") for i in range(2)]
        s_o = [K.sem(f"{name}_o{i}") for i in range(NB)]
        s_mm, s_ev = K.sem(f"{name}_mm"), K.sem(f"{name}_ev")
        nt = len(toks)
        stored = [0] * NB
        with nc.Block() as block:
            @block.sync
            def _(sp):
                for g, (w, dst, c0) in enumerate(groups):
                    n = w.shape[1]
                    if g >= 2:
                        sp.wait_ge(s_mm, nt * (g - 1))
                    sp.dma_start(wt[g % 2][:, :, 0:n], w.rearrange("(k p) n -> p k n", p=P)).then_inc(s_w[g % 2], 16)

            @block.tensor
            def _(pe):
                for g, (w, dst, c0) in enumerate(groups):
                    n = w.shape[1]
                    pe.wait_ge(s_w[g % 2], 16 * (g // 2 + 1))
                    for i, (src, t0, _) in enumerate(toks):
                        m = g * nt + i
                        if m >= NB:
                            pe.wait_ge(s_ev, m - NB + 1)
                        for k in range(KT):
                            mm = pe.matmul(pm[m % NB][:, 0:n], src[:, k, t0:t0 + P], wt[g % 2][:, k, 0:n],
                                           start=k == 0, stop=k == KT - 1)
                        mm.then_inc(s_mm, 1)

            @block.scalar
            def _(act):
                for g, (w, dst, c0) in enumerate(groups):
                    n = w.shape[1]
                    for i, (_, _, rows) in enumerate(toks):
                        m = g * nt + i
                        b = m % NB
                        act.wait_ge(s_mm, m + 1)
                        if stored[b]:
                            act.wait_ge(s_o[b], stored[b])
                        act.activation(ob[b][:, 0:n], pm[b][:, 0:n], ACT.Copy).then_inc(s_ev, 1)
                        act.wait_ge(s_ev, m + 1)
                        for r in rows:
                            act.dma_start(dst[r:r + P, c0:c0 + n], ob[b][:, 0:n]).then_inc(s_o[b], 16)
                            stored[b] += 16
                for b in range(NB):
                    act.wait_ge(s_o[b], stored[b])




def stage_misc(K):
    nc, A = K.nc, K.A
    misc = K.dram("miscF", [P, TALL])
    with K.stage() as st:
        wm = K.sb("misc_w", [P, KT, P], stack=st)
        ob = K.sb("misc_out", [P, TALL], stack=st)
        pm = K.ps("misc_ps", [P, 3, BANK], st)
        s_z, s_w, s_mm, s_cp, s_st = (K.sem(f"misc_{x}") for x in ("zero", "w", "mm", "copied", "stored"))
        with nc.Block() as block:
            @block.gpsimd
            def _(pool):
                pool.memset(wm[:], 0.0).then_inc(s_z, 1)

            @block.sync
            def _(sp):
                sp.wait_ge(s_z, 1)
                w = A["w_in"][0].rearrange("(k p) n -> p k n", p=P)
                for o, c, n in ((0, GLR, 16), (32, GLR + 16, 16), (64, MI, 8), (96, MF, 8)):
                    sp.dma_start(wm[:, :, o:o + n], w[:, :, c:c + n]).then_inc(s_w, 16)
                sp.wait_ge(s_cp, 2)
                sp.dma_start(misc, ob[:]).then_inc(s_st, 16)
                sp.wait_ge(s_st, 16)

            @block.tensor
            def _(pe):
                pe.wait_ge(s_w, 64)
                for h in range(3):
                    for k in range(KT):
                        r = K.ctxN[:, k, :] if h == 2 else K.hN[:, k, h * BANK:(h + 1) * BANK]
                        mm = pe.matmul(pm[:, h, 0:r.shape[1]], wm[:, k, :], r, start=k == 0, stop=k == KT - 1)
                mm.then_inc(s_mm, 1)

            @block.vector
            def _(dve):
                dve.wait_ge(s_mm, 1)
                flat = pm[:].rearrange("p a b -> p (a b)")
                dve.tensor_copy(ob[:, NCTX:TALL], flat[:, 0:T]).then_inc(s_cp, 1)
                dve.tensor_copy(ob[:, 0:NCTX], flat[:, T:TALL]).then_inc(s_cp, 1)


def stage_gates(K):
    nc, A = K.nc, K.A
    misc = K.scratch["miscF"]
    la_dram = K.dram("laT", [TSCAN, 512])
    K.rows5 = [K.sb(f"ml_rows{d}", [4, NCH, 5, P], stack=K.mixstack) for d in range(2)]
    K.kwcol = [K.sb(f"ml_kwcol{d}", [P, NCH, 4], stack=K.mixstack) for d in range(2)]
    U_, W_, M_, C_, G_ = range(5)
    with K.stage() as st:
        glr = [K.sb(f"glr{d}", [16, TALL], stack=st) for d in range(2)]
        upw = [K.sb(f"gla_up{d}", [16, 256], stack=st) for d in range(2)]
        upb = K.sb("gla_up_b", [P, 512], stack=st)
        gate = [[K.sb(f"gate{n}_{d}", [4, TALL], stack=st) for d in range(2)] for n in range(2)]
        bias = [[K.sb(f"gbias{n}_{d}", [4, 1], stack=st) for d in range(2)] for n in range(2)]
        reset = K.sb("reset", [4, TALL], stack=st)
        tmp = [K.sb(f"gtmp{d}", [4, TALL], stack=st) for d in range(2)]
        acum = tmp
        mrun = [K.sb(f"mrun{d}", [4, TALL], stack=st) for d in range(2)]
        mprev = [K.sb(f"mprev{d}", [4, NCH], stack=st) for d in range(2)]
        lx = K.sb("gla_logit", [P, NCH, 512], stack=st)
        le = K.sb("gla_exp", [P, NCH, 512], stack=st)
        pl = [K.ps(f"logit_ps{i}", [P, 512], st) for i in range(2)]
        pg = K.ps("kwcol_ps", [P, 2, NCH, 4], st)
        s_z, s_8, s_in, s_lg, s_lb, s_a, s_la, s_g, s_ge, s_row, s_col, s_st = (
            K.sem(f"gates_{x}") for x in ("zero", "rows", "in", "logits", "biased", "act",
                                          "logsig", "row", "rowact", "rowdone", "col", "stored"))
        with nc.Block() as block:
            @block.gpsimd
            def _(pool):
                pool.memset(reset[:], 1.0).then_inc(s_z, 1)
                pool.wait_ge(s_z, 1)
                pool.memset(reset[:].rearrange("r (c t) -> r c t", t=P)[:, :, 0:1], 0.0).then_inc(s_z, 1)

            @block.sync
            def _(sp):
                for d in range(2):
                    sp.dma_start(upw[d][:], A["gla_up_w"][0, d]).then_inc(s_in, 16)
                    sp.dma_start(upb[:, d * 256:(d + 1) * 256], A["gla_up_b"][0, d].partition_broadcast(P)).then_inc(s_in, 16)
                    sp.dma_start(bias[0][d][:], A["ml_i_b"][0, d].rearrange("(h a) -> h a", a=1)).then_inc(s_in, 16)
                    sp.dma_start(bias[1][d][:], A["ml_f_b"][0, d].rearrange("(h a) -> h a", a=1)).then_inc(s_in, 16)
                for d in range(2):
                    sp.dma_start(glr[d][:], misc[32 * d:32 * d + 16, :]).then_inc(s_in, 16)
                    for n in range(2):
                        r = misc[64 + 32 * n + 4 * d:64 + 32 * n + 4 * d + 4, :]
                        if d == 0:
                            sp.dma_start(gate[n][d][:], r).then_inc(s_8, 16)
                        else:
                            sp.dma_start(gate[n][d][:, 0:T], r[:, NCTX:TALL]).then_inc(s_8, 16)
                            sp.dma_start(gate[n][d][:, T:TALL], r[:, 0:NCTX]).then_inc(s_8, 16)
                sp.wait_ge(s_la, 1)
                tok = lambda ap: ap.rearrange("(c p) n -> p c n", p=P)
                sp.dma_start(tok(la_dram[0:TALL, :]), lx[:]).then_inc(s_st, 16)
                sp.dma_start(tok(la_dram[TALL:TSCAN, :]), lx[:, 0:2, :]).then_inc(s_st, 16)
                sp.wait_ge(s_st, 32)

            @block.tensor
            def _(pe):
                pe.wait_ge(s_in, 160)
                for n in range(NCH):
                    if n >= 2:
                        pe.wait_ge(s_lb, n - 1)
                    for d in range(2):
                        mm = pe.matmul(pl[n % 2][:, d * 256:(d + 1) * 256], glr[d][:, n * P:(n + 1) * P], upw[d][:],
                                       start=True, stop=True)
                    mm.then_inc(s_lg, 1)
                pe.wait_ge(s_row, 2)
                for d in range(2):
                    for n in range(NCH):
                        mm = pe.transpose(pg[:, d, n, :], K.rows5[d][:, n, G_, :], K.c("ident")[0:4, 0:4])
                mm.then_inc(s_col, 1)

            @block.vector
            def _(dve):
                dve.wait_ge(s_in, 160)
                for n in range(NCH):
                    dve.wait_ge(s_lg, n + 1)
                    dve.tensor_tensor(lx[:, n, :], pl[n % 2][:], upb[:], ALU.add).then_inc(s_lb, 1)
                dve.wait_ge(s_a, 3)
                dve.scalar_tensor_tensor(lx[:], lx[:], 0.0, le[:], ALU.min, ALU.subtract).then_inc(s_la, 1)
                dve.wait_ge(s_8, 96)
                dve.wait_ge(s_z, 2)
                step = Count(dve, s_g)
                for d in range(2):
                    gi, gf, r5 = gate[0][d], gate[1][d], K.rows5[d]
                    run = (lambda t: t[:]) if d == 0 else (lambda t: backwards(t, 4, TALL))
                    chunks = lambda t: t[:].rearrange("r (c t) -> r c t", t=P)
                    end = P - 1 if d == 0 else 0
                    step(dve.tensor_scalar(gi[:], gi[:], bias[0][d][:], None, ALU.add))
                    step(dve.tensor_scalar(gf[:], gf[:], bias[1][d][:], None, ALU.add))
                    dve.wait_ge(s_ge, 4 * d + 3)
                    step(dve.scalar_tensor_tensor(gf[:], gf[:], 0.0, tmp[d][:], ALU.min, ALU.subtract))
                    step(dve.tensor_tensor_scan(run(acum[d]), reset[:], run(gf), 0.0, ALU.mult, ALU.add))
                    step(dve.tensor_tensor_scan(run(mrun[d]), run(gf), run(gi), 0.0, ALU.add, ALU.max))
                    step(dve.memset(mprev[d][:], 0.0))
                    m = chunks(mrun[d])
                    if d == 0:
                        step(dve.tensor_copy(mprev[d][:, 1:NCH], m[:, 0:NCH - 1, end]))
                    else:
                        step(dve.tensor_copy(mprev[d][:, 0:NCH - 1], m[:, 1:NCH, end]))
                    step(dve.tensor_tensor(r5[:, :, U_, :], chunks(acum[d]), m, ALU.subtract))
                    step(dve.tensor_tensor(r5[:, :, C_, :], chunks(gi), chunks(acum[d]), ALU.subtract))
                    step(dve.tensor_scalar(r5[:, :, M_, :], m, -1.0, None, ALU.mult))
                    step(dve.tensor_tensor(r5[:, :, W_, :], r5[:, :, U_, :], mprev[d][:].unsqueeze(2).to_broadcast([4, NCH, P]), ALU.add))
                    step(dve.tensor_tensor(r5[:, :, G_, :], r5[:, :, C_, :],
                                           r5[:, :, U_, end:end + 1].to_broadcast([4, NCH, P]), ALU.add))
                dve.wait_ge(s_col, 1)
                for d in range(2):
                    dve.tensor_copy(K.kwcol[d][:], pg[:, d])

            @block.scalar
            def _(act):
                act.wait_ge(s_lb, NCH)
                act.activation(le[:], lx[:], ACT.Abs).then_inc(s_a, 1)
                act.wait_ge(s_a, 1)
                act.activation(le[:], le[:], ACT.Exp, scale=-1.0).then_inc(s_a, 1)
                act.wait_ge(s_a, 2)
                act.activation(le[:], le[:], ACT.Ln, bias=1.0).then_inc(s_a, 1)
                for d in range(2):
                    act.wait_ge(s_g, 12 * d + 2)
                    act.activation(tmp[d][:], gate[1][d][:], ACT.Abs).then_inc(s_ge, 1)
                    act.wait_ge(s_ge, 4 * d + 1)
                    act.activation(tmp[d][:], tmp[d][:], ACT.Exp, scale=-1.0).then_inc(s_ge, 1)
                    act.wait_ge(s_ge, 4 * d + 2)
                    act.activation(tmp[d][:], tmp[d][:], ACT.Ln, bias=1.0).then_inc(s_ge, 1)
                    act.wait_ge(s_g, 12 * d + 12)
                    g = K.rows5[d][:, :, G_, :]
                    act.activation(g, g, ACT.Exp).then_inc(s_ge, 1)
                    act.wait_ge(s_ge, 4 * d + 4)
                    act.sem_inc(s_row, 1)


def backwards(t, parts, n):
    a = t[:]
    return bass.AP(a.tensor, a.offset + n - 1, [a.ap[0], [-1, n]])


def stage_conv(K):
    nc = K.nc
    raw, out = K.scratch["mqk_raw"], K.dram("mqkF", [1024, TSCAN])
    R, W = 16, 64
    with K.stage() as st:
        img = [K.sb(f"img{u}", [P, R + 2, W + 2], stack=st) for u in range(2)]
        row = [K.sb(f"ctxrow{u}", [P, NCTX + 2], stack=st) for u in range(2)]
        acc = [K.sb(f"conv_acc{u}", [P, TALL], stack=st) for u in range(2)]
        s_z = K.sem("conv_zero")
        s_in, s_tap, s_act, s_out = ([K.sem(f"conv_{x}{u}") for u in range(2)] for x in ("in", "taps", "act", "out"))
        cw, cb = K.col_at["ml_conv_w"], K.col_at["ml_conv_b"]
        NTAP = 12
        with nc.Block() as block:
            @block.gpsimd
            def _(pool):
                for u in range(2):
                    pool.memset(img[u][:], 0.0).then_inc(s_z, 1)
                    pool.memset(row[u][:], 0.0).then_inc(s_z, 1)

            @block.sync
            def _(sp):
                sp.wait_ge(s_z, 4)
                with sp.Fori(0, 4) as i:
                    for u in range(2):
                        sp.wait_ge(s_tap[u], i * NTAP)
                        rows = bass.ds(i * 2 * P + u * P, P)
                        sp.dma_start(img[u][:, 1:R + 1, 1:W + 1],
                                     raw[rows, NCTX:NCTX + T].rearrange("p (r w) -> p r w", w=W)).then_inc(s_in[u], 16)
                        sp.dma_start(row[u][:, 1:NCTX + 1], raw[rows, 0:NCTX]).then_inc(s_in[u], 16)

            @block.vector
            def _(dve):
                with dve.Fori(0, 4) as i:
                    for u in range(2):
                        dve.wait_ge(s_in[u], (i + 1) * 32)
                        dve.wait_ge(s_out[u], i * 32)
                        step = Count(dve, s_tap[u], i * NTAP)
                        ax = acc[u][:, NCTX:TALL].rearrange("p (r w) -> p r w", w=W)
                        ac = acc[u][:, 0:NCTX]
                        for n in range(9):
                            dy, dx = n // 3, n % 3
                            wcol = K.cols[:, bass.ds(i * 2 + (cw + 8 * n + u), 1)]
                            src = img[u][:, dy:dy + R, dx:dx + W]
                            if n == 0:
                                step(dve.tensor_scalar(ax, src, wcol, None, ALU.mult))
                            else:
                                step(dve.scalar_tensor_tensor(ax, src, wcol, ax, ALU.mult, ALU.add))
                        for dx in range(3):
                            wcol = K.cols[:, bass.ds(i * 2 + (cw + 8 * (3 + dx) + u), 1)]
                            src = row[u][:, dx:dx + NCTX]
                            if dx == 0:
                                step(dve.tensor_scalar(ac, src, wcol, None, ALU.mult))
                            else:
                                step(dve.scalar_tensor_tensor(ac, src, wcol, ac, ALU.mult, ALU.add))
                        assert step.n == NTAP

            @block.scalar
            def _(act):
                with act.Fori(0, 4) as i:
                    for u in range(2):
                        act.wait_ge(s_tap[u], (i + 1) * NTAP)
                        act.activation(acc[u][:], acc[u][:], ACT.Silu,
                                       bias=K.cols[:, bass.ds(i * 2 + (cb + u), 1)]).then_inc(s_act[u], 1)
                        act.wait_ge(s_act[u], i + 1)
                        rows = bass.ds(i * 2 * P + u * P, P)
                        act.dma_start(out[rows, 0:TALL], acc[u][:]).then_inc(s_out[u], 16)
                        act.dma_start(out[rows, TALL:TSCAN], acc[u][:, 0:NCTX]).then_inc(s_out[u], 16)
                for u in range(2):
                    act.wait_ge(s_out[u], 4 * 32)


def stage_turn_rows(K, name, src, ncols, dst, src0=0):
    nc = K.nc
    nt = ncols // P
    with K.stage() as st:
        f = K.sb(f"{name}_f", [P, nt, TSCAN], stack=st)
        t = [K.sb(f"{name}_t{u}", [P, nt, P], stack=st) for u in range(2)]
        pt = [K.ps(f"{name}_ps{u}", [P, nt, P], st) for u in range(2)]
        s_in, s_t = K.sem(f"{name}_in"), K.sem(f"{name}_turned")
        s_c = K.sem(f"{name}_copied")
        s_o = [K.sem(f"{name}_out{u}") for u in range(2)]
        n_ch = TSCAN // P
        with nc.Block() as block:
            @block.sync
            def _(sp):
                sp.dma_start(f[:], src[src0:src0 + ncols, :].rearrange("(k p) t -> p k t", p=P)).then_inc(s_in, 16)
                for n in range(n_ch):
                    sp.wait_ge(s_c, n + 1)
                    sp.dma_start(dst[n * P:(n + 1) * P, :].rearrange("t (k p) -> t k p", p=P), t[n % 2][:]).then_inc(s_o[n % 2], 16)
                for u in range(2):
                    sp.wait_ge(s_o[u], n_ch // 2 * 16)

            @block.tensor
            def _(pe):
                pe.wait_ge(s_in, 16)
                for n in range(n_ch):
                    if n >= 2:
                        pe.wait_ge(s_c, n - 1)
                    for k in range(nt):
                        mm = pe.transpose(pt[n % 2][:, k, :], f[:, k, n * P:(n + 1) * P], K.c("ident"))
                    mm.then_inc(s_t, 1)

            @block.vector
            def _(dve):
                for n in range(n_ch):
                    dve.wait_ge(s_t, n + 1)
                    if n >= 2:
                        dve.wait_ge(s_o[n % 2], n // 2 * 16)
                    dve.tensor_copy(t[n % 2][:], pt[n % 2][:]).then_inc(s_c, 1)


def stage_gla(K):
    nc = K.nc
    qk, vT, kT, la = K.scratch["gqkF"], K.scratch["vT"], K.scratch["gkT"], K.scratch["laT"]
    out = K.dram("gla_o", [2, 512, TALL])
    TAU = 1.0 / 16
    with K.stage() as st:
        D2 = range(2)
        sb2 = lambda n, shape: [K.sb(f"gla_{n}{d}", shape, stack=st) for d in D2]
        q, k = sb2("q", [P, 2, P]), sb2("k", [P, 2, P])
        kt, v, lat = sb2("kT", [P, 256]), sb2("v", [P, 4, P]), sb2("la", [P, 256])
        e1, e2, e3, e4 = sb2("e_mid", [P, 2, P]), sb2("e_inv", [P, 2, P]), sb2("e_cum", [P, 2, P]), sb2("e_end", [P, 256])
        qa, qs, ke = sb2("qa", [P, 2, P]), sb2("qs", [P, 2, P]), sb2("ke", [P, 256])
        ka, S = sb2("ka", [P, 4, P]), sb2("S", [P, 4, P])
        att, ob = sb2("att", [P, 4, P]), sb2("o", [P, 4, P])
        mask = [K.sb(f"gla_mask{d}", [P, 4, P], mybir.dt.int32, stack=st) for d in D2]
        pb = [K.ps(f"gla_decay{d}", [P, 2, 2, P], st) for d in D2]
        pe_ = [K.ps(f"gla_end{d}", [P, 256], st) for d in D2]
        pa = [K.ps(f"gla_att{d}", [P, 4, P], st) for d in D2]
        po = [K.ps(f"gla_out{d}", [P, 4, P], st) for d in D2]
        sem2 = lambda n: [K.sem(f"gla_{n}{d}") for d in D2]
        s_in, s_dec, s_exp, s_q, s_att, s_m, s_o, s_su, s_S, s_ob, s_st = (
            sem2(x) for x in ("in", "decay", "exp", "scaled", "att", "masked", "o", "su", "S", "evac", "stored"))
        s_init = K.sem("gla_init")
        with nc.Block() as block:
            @block.sync
            def _(sp):
                with sp.Fori(0, NCH) as j:
                    for d in D2:
                        at = j * P if d == 0 else (TSCAN // P - 1) * P - j * P
                        sp.wait_ge(s_init, 8)
                        sp.wait_ge(s_o[d], j)
                        f = qk[:, bass.ds(at, P)].rearrange("(a p) t -> p a t", p=P)
                        sp.dma_start(q[d][:], f[:, 0:2, :]).then_inc(s_in[d], 16)
                        sp.dma_start(k[d][:], f[:, 2:4, :]).then_inc(s_in[d], 16)
                        sp.dma_start(kt[d][:], kT[bass.ds(at, P), :]).then_inc(s_in[d], 16)
                        sp.dma_start(v[d][:], vT[bass.ds(at, P), 0:512].rearrange("t (h p) -> t h p", p=P)).then_inc(s_in[d], 16)
                        sp.dma_start(lat[d][:], la[bass.ds(at, P), d * 256:(d + 1) * 256]).then_inc(s_in[d], 16)

            @block.tensor
            def _(pe):
                pe.wait_ge(s_init, 8)
                with pe.Fori(0, NCH) as j:
                    for d in D2:
                        pe.wait_ge(s_in[d], (j + 1) * 80)
                        pe.wait_ge(s_S[d], j * 4)
                        for p in range(2):
                            for m, w in enumerate((f"mid{d}", f"tri{d}")):
                                pe.matmul(pb[d][:, p, m, :], lat[d][:, p * P:(p + 1) * P], K.c(w), start=True, stop=True)
                        pe.matmul(pe_[d][:], K.c(f"after{d}"), lat[d][:], start=True, stop=True).then_inc(s_dec[d], 1)
                    for d in D2:
                        pe.wait_ge(s_q[d], (j + 1) * 5)
                        pe.wait_ge(s_m[d], j)
                        for h in range(4):
                            mm = pe.matmul(pa[d][:, h, :], ka[d][:, h, :], qa[d][:, h // 2, :], start=True, stop=True)
                        mm.then_inc(s_att[d], 1)
                        for h in range(4):
                            p = h // 2
                            mm = pe.matmul(pb[d][:, p, h % 2, :], ke[d][:, p * P:(p + 1) * P], v[d][:, h, :], start=True, stop=True)
                        mm.then_inc(s_su[d], 1)
                    for d in D2:
                        pe.wait_ge(s_m[d], j + 1)
                        pe.wait_ge(s_ob[d], j)
                        for h in range(4):
                            pe.matmul(po[d][:, h, :], v[d][:, h, :], att[d][:, h, :], start=True, stop=False)
                            mm = pe.matmul(po[d][:, h, :], S[d][:, h, :], qs[d][:, h // 2, :], start=False, stop=True)
                        mm.then_inc(s_o[d], 1)

            @block.scalar
            def _(act):
                with act.Fori(0, NCH) as j:
                    for d in D2:
                        act.wait_ge(s_dec[d], j + 1)
                        act.wait_ge(s_o[d], j)
                        act.activation(e1[d][:], pb[d][:, :, 0, :], ACT.Exp, scale=TAU).then_inc(s_exp[d], 1)
                        act.activation(e2[d][:], pb[d][:, :, 0, :], ACT.Exp, scale=-TAU).then_inc(s_exp[d], 1)
                        act.activation(e3[d][:], pb[d][:, :, 1, :], ACT.Exp, scale=TAU).then_inc(s_exp[d], 1)
                        act.activation(e4[d][:], pe_[d][:], ACT.Exp, scale=TAU).then_inc(s_exp[d], 1)
                    for d in D2:
                        act.wait_ge(s_o[d], j + 1)
                        act.wait_ge(s_st[d], j * 16)
                        act.activation(ob[d][:], po[d][:], ACT.Copy).then_inc(s_ob[d], 1)
                        act.wait_ge(s_ob[d], j + 1)
                        at = j * P if d == 0 else (NCH - 1) * P - j * P
                        act.dma_start(out[d, :, bass.ds(at, P)].rearrange("(h p) t -> p h t", p=P), ob[d][:]).then_inc(s_st[d], 16)
                for d in D2:
                    act.wait_ge(s_st[d], NCH * 16)

            @block.vector
            def _(dve):
                for d in D2:
                    dve.memset(S[d][:], 0.0).then_inc(s_init, 1)
                    dve.memset(att[d][:], 0.0).then_inc(s_init, 1)
                    dve.memset(ka[d][:], 0.0).then_inc(s_init, 1)
                    m = K.c(f"tri{d}").unsqueeze(1).to_broadcast([P, 4, P])
                    dve.tensor_copy(mask[d][:], m).then_inc(s_init, 1)
                dve.wait_ge(s_init, 8)
                with dve.Fori(0, NCH) as j:
                    for d in D2:
                        dve.wait_ge(s_exp[d], (j + 1) * 4)
                        dve.tensor_tensor(qa[d][:], q[d][:], e1[d][:], ALU.mult).then_inc(s_q[d], 1)
                        for r in (slice(0, 64), slice(64, P)):
                            own = ka[d][r].rearrange("p (a b) t -> p a b t", b=2)[:, :, r.start // 64, :]
                            dve.tensor_tensor(own, k[d][r], e2[d][r], ALU.mult).then_inc(s_q[d], 1)
                        dve.tensor_tensor(qs[d][:], q[d][:], e3[d][:], ALU.mult).then_inc(s_q[d], 1)
                        dve.tensor_tensor(ke[d][:], kt[d][:], e4[d][:], ALU.mult).then_inc(s_q[d], 1)
                    for d in D2:
                        dve.wait_ge(s_init, 8)
                        dve.wait_ge(s_att[d], j + 1)
                        dve.copy_predicated(att[d][:], mask[d][:], pa[d][:]).then_inc(s_m[d], 1)
                    for d in D2:
                        dve.wait_ge(s_su[d], j + 1)
                        dve.wait_ge(s_o[d], j + 1)
                        end = P - 1 if d == 0 else 0
                        for h in range(4):
                            p, r = h // 2, slice(64 * (h % 2), 64 * (h % 2) + 64)
                            dve.scalar_tensor_tensor(S[d][r, h, :], S[d][r, h, :], e3[d][r, p, end:end + 1],
                                                     pb[d][r, p, h % 2, :], ALU.mult, ALU.add).then_inc(s_S[d], 1)


def stage_mlstm(K):
    nc = K.nc
    qk, vT, kT = K.scratch["mqkF"], K.scratch["vT"], K.scratch["mkT"]
    out = K.dram("ml_o", [2, 512, TALL])
    QS = float(P) ** -0.5
    U_, W_, M_, C_, G_ = range(5)
    with K.stage() as st:
        D2 = range(2)
        sb2 = lambda n, shape: [K.sb(f"ml_{n}{d}", shape, stack=st) for d in D2]
        q, k, kt, va = sb2("q", [P, 4, P]), sb2("k", [P, 4, P]), sb2("kT", [P, 4, P]), sb2("v_ones", [P, 4, 2 * P])
        rb = sb2("rows_now", [4, 5, P])
        dx, wx, mx = sb2("exp_pair", [P, 4, P]), sb2("exp_inter", [P, 4, P]), sb2("exp_negm", [P, 4, P])
        pr, qw, kw = sb2("probs", [P, 4, P]), sb2("qw", [P, 4, P]), sb2("kw", [P, 4, P])
        den, ob, S = sb2("den", [P, 4, P]), sb2("o", [P, 4, P]), sb2("S", [P, 4, 2 * P])
        b0 = [K.ps(f"ml_exp_num{d}", [P, 4, P], st) for d in D2]
        b1 = [K.ps(f"ml_inter_den{d}", [P, 4, P], st) for d in D2]
        b23 = [K.ps(f"ml_m_qk_state{d}", [P, 2, 4, P], st) for d in D2]
        sem2 = lambda n: [K.sem(f"ml_{n}{d}") for d in D2]
        s_in, s_rb, s_e, s_x, s_p, s_nd, s_su, s_S, s_dn, s_h, s_st = (sem2(x) for x in (
            "in", "rows", "exponents", "exp", "weighted", "num_den", "su", "S", "den", "h", "stored"))
        s_init = K.sem("ml_init")
        with nc.Block() as block:
            @block.sync
            def _(sp):
                sp.wait_ge(s_init, 4)
                with sp.Fori(0, NCH) as j:
                    for d in D2:
                        at = j * P if d == 0 else (TSCAN // P - 1) * P - j * P
                        sp.wait_ge(s_init, 4)
                        sp.wait_ge(s_su[d], j)
                        f = qk[:, bass.ds(at, P)].rearrange("(a p) t -> p a t", p=P)
                        sp.dma_start(q[d][:], f[:, 0:4, :]).then_inc(s_in[d], 16)
                        sp.dma_start(k[d][:], f[:, 4:8, :]).then_inc(s_in[d], 16)
                        sp.dma_start(kt[d][:], kT[bass.ds(at, P), :].rearrange("t (h p) -> t h p", p=P)).then_inc(s_in[d], 16)
                        sp.dma_start(va[d][:, :, 0:P], vT[bass.ds(at, P), 512:1024].rearrange("t (h p) -> t h p", p=P)) \
                            .then_inc(s_in[d], 16)

            @block.gpsimd
            def _(pool):
                for d in D2:
                    pool.memset(S[d][:], 0.0).then_inc(s_init, 1)
                    pool.memset(va[d][:, :, P:2 * P], 1.0).then_inc(s_init, 1)
                with pool.Fori(0, NCH) as j:
                    for d in D2:
                        at = j * (5 * P) if d == 0 else (NCH - 1) * (5 * P) - j * (5 * P)
                        pool.wait_ge(s_init, 4)
                        pool.wait_ge(s_e[d], j)
                        pool.tensor_copy(rb[d][:].rearrange("r a t -> r (a t)"),
                                         K.rows5[d][:].rearrange("r c a t -> r (c a t)")[:, bass.ds(at, 5 * P)]).then_inc(s_rb[d], 1)

            @block.tensor
            def _(pe):
                pe.wait_ge(s_init, 4)
                with pe.Fori(0, NCH) as j:
                    for d in D2:
                        sel = K.c("selrow")
                        pe.wait_ge(s_in[d], (j + 1) * 64)
                        pe.wait_ge(s_h[d], j)
                        pe.wait_ge(s_S[d], j * 4)
                        neg = K.c(f"neg{d}").unsqueeze(1).to_broadcast([P, 4, P])
                        pe.matmul(b0[d][:], K.c("ident"), neg, start=True, stop=False)
                        pe.wait_ge(s_rb[d], j + 1)
                        pe.matmul(b0[d][:], rb[d][:, C_, :], sel[0:4, :], start=False, stop=False)
                        for h in range(4):
                            one = sel[0:4, h * P:(h + 1) * P]
                            pe.matmul(b0[d][:, h, :], one, rb[d][:, U_, :], start=False, stop=h == 3)
                        for h in range(4):
                            one = sel[0:4, h * P:(h + 1) * P]
                            pe.matmul(b1[d][:, h, :], one, rb[d][:, W_, :], start=True, stop=True)
                            pe.matmul(b23[d][:, 0, h, :], one, rb[d][:, M_, :], start=True, stop=True)
                        for h in range(4):
                            mm = pe.matmul(b23[d][:, 1, h, :], k[d][:, h, :], q[d][:, h, :], start=True, stop=True)
                        mm.then_inc(s_e[d], 1)
                    for d in D2:
                        pe.wait_ge(s_p[d], (j + 1) * 3)
                        for h in range(4):
                            pe.matmul(b0[d][:, h, :], va[d][:, h, 0:P], pr[d][:, h, :], start=True, stop=False)
                            pe.matmul(b0[d][:, h, :], S[d][:, h, 0:P], qw[d][:, h, :], start=False, stop=True)
                        for h in range(4):
                            pe.matmul(b1[d][:, h, :], K.c("ones"), pr[d][:, h, :], start=True, stop=False)
                            mm = pe.matmul(b1[d][:, h, :], S[d][:, h, P:2 * P], qw[d][:, h, :], start=False, stop=True)
                        mm.then_inc(s_nd[d], 1)
                        for h in range(4):
                            o = b23[d][:, h // 2, 2 * (h % 2):2 * (h % 2) + 2, :].rearrange("p a b -> p (a b)")
                            mm = pe.matmul(o, kw[d][:, h, :], va[d][:, h, :], start=True, stop=True)
                        mm.then_inc(s_su[d], 1)

            @block.scalar
            def _(act):
                with act.Fori(0, NCH) as j:
                    for d in D2:
                        act.wait_ge(s_e[d], j + 1)
                        act.wait_ge(s_S[d], j * 4)
                        act.activation(dx[d][:], b0[d][:], ACT.Exp).then_inc(s_x[d], 1)
                        act.activation(wx[d][:], b1[d][:], ACT.Exp).then_inc(s_x[d], 1)
                        act.activation(mx[d][:], b23[d][:, 0], ACT.Exp).then_inc(s_x[d], 1)
                    for d in D2:
                        act.wait_ge(s_h[d], j + 1)
                        at = j * P if d == 0 else (NCH - 1) * P - j * P
                        act.dma_start(out[d, :, bass.ds(at, P)].rearrange("(h p) t -> p h t", p=P), ob[d][:]).then_inc(s_st[d], 16)
                for d in D2:
                    act.wait_ge(s_st[d], NCH * 16)

            @block.vector
            def _(dve):
                with dve.Fori(0, NCH) as j:
                    for d in D2:
                        at = j * 4 if d == 0 else (NCH - 1) * 4 - j * 4
                        dve.wait_ge(s_x[d], (j + 1) * 3)
                        dve.scalar_tensor_tensor(pr[d][:], b23[d][:, 1], QS, dx[d][:], ALU.mult, ALU.mult).then_inc(s_p[d], 1)
                        dve.scalar_tensor_tensor(qw[d][:], q[d][:], QS, wx[d][:], ALU.mult, ALU.mult).then_inc(s_p[d], 1)
                        kc = K.kwcol[d][:].rearrange("p c h -> p (c h)")[:, bass.ds(at, 4)].unsqueeze(2).to_broadcast([P, 4, P])
                        dve.tensor_tensor(kw[d][:], kt[d][:], kc, ALU.mult).then_inc(s_p[d], 1)
                    for d in D2:
                        dve.wait_ge(s_nd[d], j + 1)
                        step = Count(dve, s_dn[d], j * 3)
                        step(dve.scalar_tensor_tensor(den[d][:], b1[d][:], -1.0, mx[d][:], ALU.mult, ALU.max))
                        step(dve.tensor_tensor(den[d][:], b1[d][:], den[d][:], ALU.max))
                        step(dve.reciprocal(den[d][:], den[d][:]))
                        dve.wait_ge(s_st[d], j * 16)
                        dve.tensor_tensor(ob[d][:], b0[d][:], den[d][:], ALU.mult).then_inc(s_h[d], 1)
                        dve.wait_ge(s_su[d], j + 1)
                        end = P - 1 if d == 0 else 0
                        for h in range(4):
                            o = b23[d][:, h // 2, 2 * (h % 2):2 * (h % 2) + 2, :].rearrange("p a b -> p (a b)")
                            dve.scalar_tensor_tensor(S[d][:, h, :], S[d][:, h, :], wx[d][:, h, end:end + 1], o,
                                                     ALU.mult, ALU.add).then_inc(s_S[d], 1)


def stage_join(K, name, parts, mixF):
    nc = K.nc
    with K.stage() as st:
        a, b, g = ([K.sb(f"{name}_{x}{u}", [P, T], stack=st) for u in range(2)] for x in ("fwd", "bwd", "gate"))
        sq, rs = ([K.sb(f"{name}_{x}{u}", [P, T], stack=st) for u in range(2)] for x in ("sq", "rstd"))
        pm = [K.ps(f"{name}_ps{u}", [P, 2, BANK], st) for u in range(2)]
        s_in, s_a, s_mm, s_v, s_x = ([K.sem(f"{name}_{x}{u}") for u in range(2)] for x in ("in", "act", "mean", "vec", "sum"))
        mix = mixF[:].rearrange("p k t -> p (k t)")
        two = len(parts[0][0].shape) == 3
        nin = 48 if two else 32
        with nc.Block() as block:
            @block.sync
            def _(sp):
                for r, (src, _, gate, _) in enumerate(parts):
                    with sp.Fori(0, 2) as i:
                        for u in range(2):
                            n = i + 2 * r
                            sp.wait_ge(s_v[u], n * 4)
                            rows = bass.ds(i * 2 * P + u * P, P)
                            if two:
                                sp.dma_start(a[u][:], src[0, rows, NCTX:TALL]).then_inc(s_in[u], 16)
                                sp.dma_start(b[u][:], src[1, rows, 0:T]).then_inc(s_in[u], 16)
                            else:
                                sp.dma_start(a[u][:], src[rows, :]).then_inc(s_in[u], 16)
                            sp.dma_start(g[u][:], gate[rows, :]).then_inc(s_in[u], 16)

            @block.vector
            def _(dve):
                for r, (_, gain, _, tile) in enumerate(parts):
                    with dve.Fori(0, 2) as i:
                        for u in range(2):
                            n = i + 2 * r
                            if two:
                                dve.wait_ge(s_in[u], (n + 1) * nin)
                                dve.tensor_tensor(a[u][:], a[u][:], b[u][:], ALU.add).then_inc(s_x[u], 1)
                            dve.wait_ge(s_mm[u], n + 1)
                            step = Count(dve, s_v[u], n * 4)
                            step(dve.tensor_scalar(rs[u][:], pm[u][:].rearrange("p a b -> p (a b)"), EPS, None, ALU.add))
                            dve.wait_ge(s_a[u], n * 2 + 2)
                            step(dve.reciprocal(rs[u][:], rs[u][:]))
                            gc = K.cols[:, bass.ds(i * 2 + (K.col_at[gain] + u), 1)]
                            step(dve.scalar_tensor_tensor(rs[u][:], rs[u][:], gc, g[u][:], ALU.mult, ALU.mult))
                            step(dve.tensor_tensor(mix[:, bass.ds(i * 2 * T + (tile + u) * T, T)], a[u][:], rs[u][:], ALU.mult))

            @block.scalar
            def _(act):
                for r in range(len(parts)):
                    with act.Fori(0, 2) as i:
                        for u in range(2):
                            n = i + 2 * r
                            act.wait_ge(s_x[u] if two else s_in[u], n + 1 if two else (n + 1) * nin)
                            act.activation(sq[u][:], a[u][:], ACT.Square).then_inc(s_a[u], 1)
                            act.wait_ge(s_v[u], n * 4 + 1)
                            act.activation(rs[u][:], rs[u][:], ACT.Sqrt).then_inc(s_a[u], 1)

            @block.tensor
            def _(pe):
                for r in range(len(parts)):
                    with pe.Fori(0, 2) as i:
                        for u in range(2):
                            n = i + 2 * r
                            pe.wait_ge(s_a[u], n * 2 + 1)
                            for h in range(2):
                                mm = pe.matmul(pm[u][:, h, :], K.c("mean128"), sq[u][:, h * BANK:(h + 1) * BANK], start=True, stop=True)
                            mm.then_inc(s_mm[u], 1)


def mixer_one(K):
    nc, A = K.nc, K.A
    w_in = A["w_in"][0]
    mc = K.modcols
    with ExitStack() as norm:
        K.hN = K.sb("hN", [P, KT, T], stack=norm)
        K.ctxN = K.sb("ctxN", [P, KT, NCTX], stack=norm)
        g1 = K.cols[:, K.col_at["norm1_g"]:K.col_at["norm1_g"] + 8]
        with ExitStack() as c:
            K.ctxF = K.sb("ctxF", [P, KT, NCTX], stack=c)
            stage_turn_in(K)
            stage_norm(K, "n1x", K.hF, K.hN, T, g1, shift=mc[:, 0:8], scale=mc[:, 8:16])
            stage_norm(K, "n1c", K.ctxF, K.ctxN, NCTX, g1, shift=mc[:, 48:56], scale=mc[:, 56:64])
        ctx = K.ctxN
        gqk, mqk = K.dram("gqkF", [512, TSCAN]), K.dram("mqk_raw", [1024, TSCAN])
        ggF, moF = K.dram("ggF", [512, T]), K.dram("moF", [512, T])
        vT, gkT = K.dram("vT", [TSCAN, 1024]), K.dram("gkT", [TSCAN, 256])
        stage_gemm_f(K, "gq", w_in[:, GQ:GQ + 256], 256, K.hN, T, gqk[0:256], ACT.Copy, scale=0.125, ctx=ctx)
        stage_gemm_f(K, "gk", w_in[:, GK:GK + 256], 256, K.hN, T, gqk[256:512], ACT.Copy, ctx=ctx)
        stage_gemm_f(K, "mqk", w_in[:, MQK:MQK + 1024], 1024, K.hN, T, mqk, ACT.Copy, ctx=ctx)
        stage_gemm_f(K, "gg", w_in[:, GG:GG + 512], 512, K.hN, T, ggF, ACT.Silu)
        stage_gemm_f(K, "mo", w_in[:, MO:MO + 512], 512, K.hN, T, moF, ACT.Sigmoid)
        toks = [(K.ctxN, i * P, (i * P, TALL + i * P)) for i in range(NCTX // P)] +                [(K.hN, i * P, (NCTX + i * P,)) for i in range(T // P)]
        stage_gemm_t(K, "vT", [(w_in[:, GV:GV + 512], vT, 0), (w_in[:, MV:MV + 512], vT, 512), (w_in[:, GK:GK + 256], gkT, 0)], toks)
        stage_misc(K)
    K.mixstack = K.stack.enter_context(ExitStack())
    stage_gates(K)
    stage_conv(K)
    stage_turn_rows(K, "mkT", K.scratch["mqkF"], 512, K.dram("mkT", [TSCAN, 512]), src0=512)
    stage_gla(K)
    stage_mlstm(K)
    K.mixstack.close()
    with ExitStack() as st:
        mixF = K.sb("mixF", [P, KT, T], stack=st)
        stage_join(K, "join1", [(K.scratch["gla_o"], "gla_norm_g", ggF, 0), (K.scratch["ml_o"], "ml_norm_g", moF, 4)], mixF)
        stage_gemm_f(K, "wout1", A["w_out"][0], D, mixF, T, None, residual=K.hF, gcol=mc[:, 16:24])


def stage_route(K):
    nc, A = K.nc, K.A
    rows, slot_tok = K.dram("moe_rows", [T, D]), K.dram("slot_tok", [NBLK * P, 1], I32)
    NT, NU = T // P, 2 * T // P
    NL = NG + NE
    with K.stage() as st:
        sb = lambda n, shape, dt=F32: K.sb(f"route_{n}", shape, dt, stack=st)
        rw, rb, lg = sb("w", [P, KT, NL]), sb("b", [P, NL]), sb("logits", [P, NT, NL])
        trow = [sb(f"rows{i}", [P, D]) for i in range(3)]
        tok, zero = sb("tok", [P, NT], I32), sb("zero", [P, NBLK], I32)
        gmax, ge, gsum, idx = sb("gmax", [P, NT]), sb("gexp", [P, NT, NG]), sb("gsum", [P, NT]), sb("idx", [P, NT])
        oh4, em, cand = sb("group", [P, NT, NG]), sb("masked", [P, NT, NE]), sb("cand", [P, NT, NE])
        v = sb("top", [P, 2, NT])
        oh, pre = sb("onehot", [P, NU, NE]), sb("prefix", [P, NU, NE])
        cnt, cnti = sb("count", [P, NE]), sb("count_i", [P, NE], I32)
        nb, bend, base = sb("blocks", [P, NE]), sb("blk_end", [P, NE]), sb("base", [P, NE])
        dest, bidx, bcmp = sb("dest", [P, NU]), sb("blk_cmp", [P, NBLK, NE]), sb("blk_e", [P, NBLK])
        pt = [K.ps(f"route_turn{i}", [P, 2, BANK], st) for i in range(2)]
        pl = K.ps("route_logits", [P, NT, NL], st)
        pr = K.ps("route_rank", [P, NU, NE], st)
        pc = K.ps("route_count", [P, NE], st)
        s_in, s_lg, s_t, s_tc, s_step, s_ex, s_oh, s_rank, s_tot, s_iota, s_zero, s_dest, s_sc = (
            K.sem(f"route_{x}") for x in ("in", "logits", "turned", "copied", "step", "exp", "onehot", "rank",
                                          "count", "iota", "zero", "dest", "scattered"))
        s_row = [K.sem(f"route_row{i}") for i in range(3)]
        iota32 = K.c("iota")[:, 0:NE]
        bc = lambda ap, n: ap.unsqueeze(2).to_broadcast([P, ap.shape[1], n])
        with nc.Block() as block:
            @block.sync
            def _(sp):
                gw, ew = A["router_group_w"][0], A["router_expert_w"][0]
                sp.dma_start(rw[:, :, 0:NG], gw.rearrange("(k p) n -> p k n", p=P)).then_inc(s_in, 16)
                sp.dma_start(rw[:, :, NG:NL], ew.rearrange("(k p) n -> p k n", p=P)).then_inc(s_in, 16)
                sp.dma_start(rb[:, 0:NG], A["router_group_b"][0].partition_broadcast(P)).then_inc(s_in, 16)
                sp.dma_start(rb[:, NG:NL], A["router_expert_b"][0].partition_broadcast(P)).then_inc(s_in, 16)
                sp.wait_ge(s_iota, 2)
                sp.dma_start(slot_tok.rearrange("(p a) o -> p (a o)", a=NBLK), zero[:]).then_inc(s_zero, 16)
                for i in range(NT):
                    sp.wait_ge(s_tc, i + 1)
                    sp.dma_start(rows[i * P:(i + 1) * P, :], trow[i % 3][:]).then_inc(s_row[i % 3], 16)
                for n in range(3):
                    sp.wait_ge(s_row[n], 16 * len(range(n, NT, 3)))

            @block.gpsimd
            def _(pool):
                pool.iota(tok[:], pattern=[[P, NT]], base=0, channel_multiplier=1).then_inc(s_iota, 1)
                pool.memset(zero[:], 0).then_inc(s_iota, 1)
                pool.wait_ge(s_iota, 2)
                pool.wait_ge(s_zero, 16)
                pool.wait_ge(s_dest, 1)
                for u in range(NU):
                    pool.indirect_dma_start(slot_tok, bass.IndirectOffsetOnAxis(ap=K.moe_dest[:, u:u + 1], axis=0),
                                            tok[:, u % NT:u % NT + 1], None).then_inc(s_sc, 16)
                pool.wait_ge(s_sc, 16 * NU)

            @block.tensor
            def _(pe):
                pe.wait_ge(s_in, 64)
                for i in range(NT):
                    for k in range(KT):
                        mm = pe.matmul(pl[:, i, :], K.hN[:, k, i * P:(i + 1) * P], rw[:, k, :], start=k == 0, stop=k == KT - 1)
                mm.then_inc(s_lg, 1)
                for i in range(NT):
                    if i >= 2:
                        pe.wait_ge(s_tc, i - 1)
                    for k in range(KT):
                        mm = pe.transpose(pt[i % 2][:, k // 4, (k % 4) * P:(k % 4 + 1) * P], K.hN[:, k, i * P:(i + 1) * P], K.c("ident"))
                    mm.then_inc(s_t, 1)
                pe.wait_ge(s_oh, 2)
                pe.matmul(pr[:].rearrange("p u e -> p (u e)"), K.c("before"), oh[:].rearrange("p u e -> p (u e)"), start=True, stop=False)
                pe.matmul(pr[:].rearrange("p u e -> p (u e)"), K.c("ones"), pre[:].rearrange("p u e -> p (u e)"),
                          start=False, stop=True).then_inc(s_rank, 1)
                pe.matmul(pc[:], K.c("ones"), pre[:, NU - 1, :], start=True, stop=False)
                pe.matmul(pc[:], K.c("ones"), oh[:, NU - 1, :], start=False, stop=True).then_inc(s_tot, 1)

            @block.scalar
            def _(act):
                for i in range(NT):
                    act.wait_ge(s_t, i + 1)
                    if i >= 3:
                        act.wait_ge(s_row[i % 3], 16 * (i // 3))
                    act.activation(trow[i % 3][:], pt[i % 2][:].rearrange("p a b -> p (a b)"), ACT.Copy).then_inc(s_tc, 1)
                    if i == 0:
                        act.wait_ge(s_step, 3)
                        act.activation(ge[:], ge[:], ACT.Exp).then_inc(s_ex, 1)
                act.wait_ge(s_ex, 2)
                act.activation(v[:, 1, :], v[:, 1, :], ACT.Exp).then_inc(s_ex, 1)

            @block.vector
            def _(dve):
                step = Count(dve, s_step)

                def first_of(hits, n, onehot):
                    io = K.c("iota")[:, 0:n].unsqueeze(1).to_broadcast([P, NT, n])
                    c = cand[:, :, 0:n]
                    step(dve.tensor_scalar(c, hits, -1e6, 1e6, ALU.mult, ALU.add))
                    step(dve.tensor_tensor(c, c, io, ALU.add))
                    step(dve.tensor_reduce(idx[:], c, AX.X, ALU.min))
                    step(dve.tensor_tensor(onehot, io, bc(idx[:], n), ALU.is_equal))

                dve.wait_ge(s_in, 64)
                dve.wait_ge(s_lg, 1)
                step(dve.tensor_tensor(lg[:], pl[:], rb[:].unsqueeze(1).to_broadcast([P, NT, NL]), ALU.add))
                gl, el = lg[:, :, 0:NG], lg[:, :, NG:NL]
                step(dve.tensor_reduce(gmax[:], gl, AX.X, ALU.max))
                step(dve.tensor_tensor(ge[:], gl, bc(gmax[:], NG), ALU.subtract))
                step(dve.tensor_tensor(oh4[:], gl, bc(gmax[:], NG), ALU.is_equal))
                first_of(oh4[:], NG, oh4[:])
                e4 = em[:].rearrange("p t (g e) -> p (t g) e", g=NG)
                ohg = oh4[:].rearrange("p t g -> p (t g)").unsqueeze(2).to_broadcast([P, NT * NG, EPG])
                step(dve.tensor_copy(em[:], el))
                step(dve.tensor_tensor(e4, e4, ohg, ALU.mult))
                step(dve.tensor_scalar(oh4[:], oh4[:], 1e30, -1e30, ALU.mult, ALU.add))
                step(dve.tensor_tensor(e4, e4, ohg, ALU.add))
                for k in range(2):
                    o = oh[:, k * NT:(k + 1) * NT, :]
                    step(dve.tensor_reduce(v[:, k, :], em[:], AX.X, ALU.max))
                    step(dve.tensor_tensor(o, em[:], bc(v[:, k, :], NE), ALU.is_equal))
                    first_of(o, NE, o)
                    if k == 0:
                        step(dve.scalar_tensor_tensor(em[:].rearrange("p t e -> p (t e)"), o.rearrange("p t e -> p (t e)"), -2e30,
                                                      em[:].rearrange("p t e -> p (t e)"), ALU.mult, ALU.add))
                step(dve.memset(pre[:, 0, :], 0.0))
                for u in range(1, NU):
                    step(dve.tensor_tensor(pre[:, u, :], pre[:, u - 1, :], oh[:, u - 1, :], ALU.add))
                dve.sem_inc(s_oh, 2)
                dve.wait_ge(s_ex, 1)
                step(dve.tensor_reduce(gsum[:], ge[:], AX.X, ALU.add))
                step(dve.reciprocal(gsum[:], gsum[:]))
                step(dve.tensor_tensor(v[:, 1, :], v[:, 1, :], v[:, 0, :], ALU.subtract))
                dve.sem_inc(s_ex, 1)
                dve.wait_ge(s_ex, 3)
                step(dve.tensor_scalar(v[:, 0, :], v[:, 1, :], 1.0, None, ALU.add))
                step(dve.reciprocal(v[:, 0, :], v[:, 0, :]))
                step(dve.tensor_tensor(K.moe_w[:, 0, :], v[:, 0, :], gsum[:], ALU.mult))
                step(dve.tensor_tensor(K.moe_w[:, 1, :], K.moe_w[:, 0, :], v[:, 1, :], ALU.mult))
                dve.wait_ge(s_tot, 1)
                step(dve.tensor_scalar(cnt[:], pc[:], float(P - 1), None, ALU.add))
                step(dve.tensor_copy(cnti[:], cnt[:]))
                step(dve.tensor_scalar(cnti[:], cnti[:], 7, None, ALU.arith_shift_right))
                step(dve.tensor_copy(nb[:], cnti[:]))
                step(dve.tensor_tensor_scan(bend[:], K.c("ones")[:, 0:NE], nb[:], 0.0, ALU.mult, ALU.add))
                step(dve.tensor_tensor(base[:], bend[:], nb[:], ALU.subtract))
                step(dve.tensor_scalar(base[:], base[:], float(P), None, ALU.mult))
                dve.wait_ge(s_rank, 1)
                step(dve.tensor_tensor(pre[:], pr[:], base[:].unsqueeze(1).to_broadcast([P, NU, NE]), ALU.add))
                step(dve.tensor_tensor(pre[:], pre[:], oh[:], ALU.mult))
                step(dve.tensor_reduce(dest[:], pre[:], AX.X, ALU.add))
                step(dve.tensor_copy(K.moe_dest[:], dest[:]))
                dve.sem_inc(s_dest, 1)
                io = K.c("iota")[:, 0:NBLK].unsqueeze(2).to_broadcast([P, NBLK, NE])
                step(dve.tensor_tensor(bidx[:], bend[:].unsqueeze(1).to_broadcast([P, NBLK, NE]), io, ALU.is_le))
                step(dve.tensor_reduce(bcmp[:], bidx[:], AX.X, ALU.add))
                step(dve.tensor_scalar(bcmp[:], bcmp[:], float(NE - 1), None, ALU.min))
                step(dve.tensor_copy(K.blk_e[:], bcmp[:]))
                step(dve.tensor_copy(K.nblk[:], bend[:, NE - 1:NE]))


def stage_experts(K):
    nc, A = K.nc, K.A
    rows, slot_tok, yb = K.scratch["moe_rows"], K.scratch["slot_tok"], K.dram("moe_y", [NBLK * P, D])
    w1, w2 = A["expert_w_in"][0].rearrange("e k n -> (e k) n"), A["expert_w_out"][0].rearrange("e k n -> (e k) n")
    KE = DE // P
    with K.stage() as st:
        U = range(2)
        sb2 = lambda n, shape, dt=F32: [K.sb(f"exp_{n}{u}", shape, dt, stack=st) for u in U]
        ids, xr, xT = sb2("ids", [P, 1], I32), sb2("rows", [P, D]), sb2("xT", [P, KT, P])
        wi, wo = sb2("w_in", [P, KT, 2 * DE]), sb2("w_out", [P, KE, D])
        sg, h, y = sb2("silu", [P, KE, P]), sb2("h", [P, KE, P]), sb2("y", [P, D])
        pt = K.ps("exp_turn", [P, 2, 4, P], st)
        pg = [K.ps(f"exp_up{u}", [P, 2, KE, P], st) for u in U]
        py = K.ps("exp_y", [P, 2, BANK], st)
        sem2 = lambda n: [K.sem(f"exp_{n}{u}") for u in U]
        s_ids, s_rows, s_wi, s_wo, s_t, s_xT, s_up, s_sg, s_h, s_y, s_ye, s_st = (sem2(x) for x in (
            "ids", "rows", "w_in", "w_out", "turned", "xT", "up", "silu", "h", "y", "y_out", "stored"))
        NI = NBLK // 2
        with nc.Block() as block:
            @block.sync
            def _(sp):
                with sp.Fori(0, NI) as i:
                    for u in U:
                        b = i * 2 + u
                        e = sp.value_load(K.blk_e[0:1, bass.ds(b, 1)], min_val=0, max_val=NE - 1)
                        sp.wait_ge(s_up[u], i)
                        sp.dma_start(wi[u][:], w1[bass.ds(e * D, D), :].rearrange("(k p) n -> p k n", p=P)).then_inc(s_wi[u], 16)
                        sp.wait_ge(s_y[u], i)
                        sp.dma_start(wo[u][:], w2[bass.ds(e * DE, DE), :].rearrange("(k p) n -> p k n", p=P)).then_inc(s_wo[u], 16)

            @block.gpsimd
            def _(pool):
                with pool.Fori(1, NI + 1) as n:
                    for u in U:
                        pool.wait_ge(s_rows[u], n * 16 - 16)
                        pool.wait_ge(s_t[u], n - 1)
                        pool.dma_start(ids[u][:], slot_tok[bass.ds(n * 2 * P + (u - 2) * P, P), :]).then_inc(s_ids[u], 16)
                        pool.wait_ge(s_ids[u], 16)
                        pool.wait_ge(s_ids[u], n * 16)
                        pool.indirect_dma_start(xr[u][:], None, rows, bass.IndirectOffsetOnAxis(ap=ids[u][:, 0:1], axis=0)) \
                            .then_inc(s_rows[u], 16)

            @block.tensor
            def _(pe):
                with pe.Fori(0, NI) as i:
                    for u in U:
                        pe.wait_ge(s_rows[u], (i + 1) * 16)
                        if u == 0:
                            pe.wait_ge(s_xT[1], i)
                        else:
                            pe.wait_ge(s_xT[0], i + 1)
                        for k in range(KT):
                            mm = pe.transpose(pt[:, k // 4, k % 4, :], xr[u][:, k * P:(k + 1) * P], K.c("ident"))
                        mm.then_inc(s_t[u], 1)
                        pe.wait_ge(s_xT[u], i + 1)
                        pe.wait_ge(s_wi[u], (i + 1) * 16)
                        for g in range(2):
                            for f in range(KE):
                                c = g * DE + f * P
                                for k in range(KT):
                                    mm = pe.matmul(pg[u][:, g, f, :], wi[u][:, k, c:c + P], xT[u][:, k, :], start=k == 0, stop=k == KT - 1)
                        mm.then_inc(s_up[u], 1)
                        pe.wait_ge(s_h[u], i + 1)
                        pe.wait_ge(s_wo[u], (i + 1) * 16)
                        if u == 0:
                            pe.wait_ge(s_ye[1], i)
                        else:
                            pe.wait_ge(s_ye[0], i + 1)
                        for n in range(2):
                            for k in range(KE):
                                mm = pe.matmul(py[:, n, :], h[u][:, k, :], wo[u][:, k, n * BANK:(n + 1) * BANK], start=k == 0, stop=k == KE - 1)
                        mm.then_inc(s_y[u], 1)

            @block.vector
            def _(dve):
                with dve.Fori(0, NI) as i:
                    for u in U:
                        dve.wait_ge(s_t[u], i + 1)
                        dve.tensor_copy(xT[u][:], pt[:].rearrange("p a b t -> p (a b) t")).then_inc(s_xT[u], 1)
                        dve.wait_ge(s_sg[u], i + 1)
                        dve.tensor_tensor(h[u][:], sg[u][:], pg[u][:, 1], ALU.mult).then_inc(s_h[u], 1)

            @block.scalar
            def _(act):
                with act.Fori(0, NI) as i:
                    for u in U:
                        act.wait_ge(s_up[u], i + 1)
                        act.activation(sg[u][:], pg[u][:, 0], ACT.Silu).then_inc(s_sg[u], 1)
                        act.wait_ge(s_y[u], i + 1)
                        act.wait_ge(s_st[u], i * 16)
                        act.activation(y[u][:], py[:].rearrange("p a b -> p (a b)"), ACT.Copy).then_inc(s_ye[u], 1)
                        act.wait_ge(s_ye[u], i + 1)
                        act.dma_start(yb[bass.ds(i * 2 * P + u * P, P), :], y[u][:]).then_inc(s_st[u], 16)
                for u in U:
                    act.wait_ge(s_st[u], NI * 16)


def stage_combine(K, gcol):
    nc = K.nc
    yb = K.scratch["moe_y"]
    NT = T // P
    with K.stage() as st:
        U = range(2)
        a = [[K.sb(f"comb_{k}_{u}", [P, D], stack=st) for u in U] for k in range(2)]
        pt = [K.ps(f"comb_ps{u}", [P, 2, 4, P], st) for u in U]
        s_g = [[K.sem(f"comb_in{k}{u}") for u in U] for k in range(2)]
        s_w, s_t, s_h = K.sem("comb_sum"), K.sem("comb_turned"), K.sem("comb_added")
        with nc.Block() as block:
            @block.gpsimd
            def _(pool):
                for i in range(NT):
                    if i >= 2:
                        pool.wait_ge(s_t, i - 1)
                    for k in range(2):
                        pool.indirect_dma_start(a[k][i % 2][:], None, yb, bass.IndirectOffsetOnAxis(
                            ap=K.moe_dest[:, k * NT + i:k * NT + i + 1], axis=0)).then_inc(s_g[k][i % 2], 16)

            @block.vector
            def _(dve):
                for i in range(NT):
                    u = i % 2
                    for k in range(2):
                        dve.wait_ge(s_g[k][u], 16 * (i // 2 + 1))
                    dve.tensor_scalar(a[1][u][:], a[1][u][:], K.moe_w[:, 1, i:i + 1], None, ALU.mult).then_inc(s_w, 1)
                    dve.wait_ge(s_w, 2 * i + 1)
                    dve.scalar_tensor_tensor(a[0][u][:], a[0][u][:], K.moe_w[:, 0, i:i + 1], a[1][u][:], ALU.mult, ALU.add).then_inc(s_w, 1)
                    dve.wait_ge(s_t, i + 1)
                    for k in range(KT):
                        h = K.hF[:, k, i * P:(i + 1) * P]
                        ins = dve.scalar_tensor_tensor(h, pt[u][:, k // 4, k % 4, :], gcol[:, k:k + 1], h, ALU.mult, ALU.add)
                    ins.then_inc(s_h, 1)

            @block.tensor
            def _(pe):
                for i in range(NT):
                    u = i % 2
                    pe.wait_ge(s_w, 2 * i + 2)
                    if i >= 2:
                        pe.wait_ge(s_h, i - 1)
                    for k in range(KT):
                        mm = pe.transpose(pt[u][:, k // 4, k % 4, :], a[0][u][:, k * P:(k + 1) * P], K.c("ident"))
                    mm.then_inc(s_t, 1)


def moe(K):
    mc = K.modcols
    g = lambda n: K.cols[:, K.col_at[n]:K.col_at[n] + 8]
    with ExitStack() as plan:
        K.moe_w = K.sb("moe_w", [P, 2, T // P], stack=plan)
        K.moe_dest = K.sb("moe_dest", [P, 2 * T // P], I32, stack=plan)
        K.blk_e = K.sb("blk_expert", [P, NBLK], I32, stack=plan)
        K.nblk = K.sb("blk_count", [P, 1], I32, stack=plan)
        with ExitStack() as norm:
            K.hN = K.sb("hN2", [P, KT, T], stack=norm)
            stage_norm(K, "n2", K.hF, K.hN, T, g("norm2_g"), shift=mc[:, 24:32], scale=mc[:, 32:40])
            stage_route(K)
        stage_experts(K)
        stage_combine(K, mc[:, 40:48])
    stage_norm(K, "nf1", K.hF, K.hF, T, g("final_norm_g"))


HQ, HF_, HI, HG, BQ, BK, BV, CIN = 0, 512, 1024, 1536, 2048, 2304, 2560, 2816
LEVELS = (8, 16, 32, 64)
DIAG = 8


def stage_hgrn(K):
    nc = K.nc
    qF, fF, iF, vT = (K.scratch[n] for n in ("hq", "hf", "hi", "viT"))
    out = K.dram("hgrn_o", [512, T])
    NC = T // P
    NL = len(LEVELS)
    with K.stage() as st:
        sb = lambda n, shape: K.sb(f"hg_{n}", shape, stack=st)
        q, x, vi, vt = sb("q", [P, T]), sb("f_raw", [P, T]), sb("i", [P, T]), sb("iT", [P, NC, P])
        ex, f, k, b, reset = sb("exp", [P, T]), sb("f", [P, T]), sb("k", [P, T]), sb("b", [P, T]), sb("reset", [P, T])
        lev = sb("levels", [P, NL, T])
        eb, ee, qb, ke, keT = sb("e_cum", [P, T]), sb("e_end", [P, T]), sb("qb", [P, T]), sb("ke", [P, T]), sb("keT", [P, NC, P])
        kf = [sb(f"kf{n}", [P, T]) for n in range(2)]
        pr = [sb(f"prod{n}", [P, T]) for n in range(2)]
        dt, od = sb("diag_term", [P, T]), sb("o", [P, T])
        att, S = [sb(f"att{n}", [P, NL, P]) for n in range(2)], sb("S", [P, P])
        pd = K.ps("hg_diag", [P, 2, BANK], st)
        pa = [K.ps(f"hg_att{n}", [P, NL, P], st) for n in range(2)]
        po = K.ps("hg_o", [P, 2, BANK], st)
        psu = K.ps("hg_su", [P, P], st)
        s_in, s_ls, s_lf, s_f, s_b, s_d, s_e, s_t, s_kt, s_ktc, s_pr, s_dg, s_dt, s_lv, s_m, s_su, s_S, s_o, s_fin, s_st, s_kf, s_z = (
            K.sem(f"hg_{n}") for n in ("in", "logsig", "logf", "f", "b", "diff", "exp", "scaled", "turned", "keT",
                                       "prod", "diag", "term", "levels", "att", "su", "S", "o", "done", "stored", "kf", "zero"))
        span = lambda t, L: t.rearrange("p (n h l) -> p n h l", h=2, l=L)
        blocks = lambda t: t.rearrange("p (n l) -> p n l", l=DIAG)
        chunks = lambda t: t.rearrange("p (c t) -> p c t", t=P)
        masks = K.const[:, K.const_at["level8"][0]:K.const_at["level8"][0] + NL * P].rearrange("p (l t) -> p l t", l=NL)
        NT_ = 2 * NL + 2
        with nc.Block() as block:
            @block.sync
            def _(sp):
                with sp.Fori(0, 4) as i:
                    rows = bass.ds(i * P, P)
                    sp.wait_ge(s_fin, i)
                    sp.dma_start(x[:], fF[rows, :]).then_inc(s_in, 16)
                    sp.dma_start(q[:], qF[rows, :]).then_inc(s_in, 16)
                    sp.dma_start(vi[:], iF[rows, :]).then_inc(s_in, 16)
                    sp.dma_start(vt[:], vT[:, rows].rearrange("(c t) v -> t c v", t=P)).then_inc(s_in, 16)

            @block.gpsimd
            def _(pool):
                pool.memset(reset[:], 1.0).then_inc(s_z, 1)
                pool.wait_ge(s_z, 1)
                pool.memset(chunks(reset[:])[:, :, 0:1], 0.0).then_inc(s_z, 1)

            @block.scalar
            def _(act):
                with act.Fori(0, 4) as i:
                    act.wait_ge(s_in, (i + 1) * 64)
                    act.wait_ge(s_fin, i)
                    step = Count(act, s_ls, i * 3)
                    step(act.activation(ex[:], x[:], ACT.Abs))
                    step(act.activation(ex[:], ex[:], ACT.Exp, scale=-1.0))
                    step.mark(act.activation(ex[:], ex[:], ACT.Ln, bias=1.0))
                    act.wait_ge(s_lf, i + 1)
                    act.activation(f[:], x[:], ACT.Exp).then_inc(s_f, 1)
                    for n in range(NL):
                        act.wait_ge(s_d, i * (2 * NL + 1) + 2 * n + 2)
                        act.activation(lev[:, n, :], lev[:, n, :], ACT.Exp).then_inc(s_e, 1)
                    act.activation(eb[:], b[:], ACT.Exp).then_inc(s_e, 1)
                    act.wait_ge(s_d, (i + 1) * (2 * NL + 1))
                    act.activation(ee[:], ee[:], ACT.Exp).then_inc(s_e, 1)
                    for n in range(2):
                        act.wait_ge(s_kt, i * 2 + n + 1)
                        act.activation(keT[:, 4 * n:4 * n + 4, :], pd[:, n, :].rearrange("p (c t) -> p c t", t=P), ACT.Copy).then_inc(s_ktc, 1)
                    act.wait_ge(s_fin, i + 1)
                    act.dma_start(out[bass.ds(i * P, P), :], od[:]).then_inc(s_st, 16)
                act.wait_ge(s_st, 64)

            @block.vector
            def _(dve):
                dve.wait_ge(s_z, 2)
                with dve.Fori(0, 4) as i:
                    dve.wait_ge(s_ls, (i + 1) * 3)
                    dve.scalar_tensor_tensor(x[:], x[:], 0.0, ex[:], ALU.min, ALU.subtract).then_inc(s_lf, 1)
                    dve.wait_ge(s_lf, i + 1)
                    dve.tensor_tensor_scan(b[:], reset[:], x[:], 0.0, ALU.mult, ALU.add).then_inc(s_b, 1)
                    dve.wait_ge(s_f, i + 1)
                    dve.tensor_scalar(k[:], f[:], -1.0, 1.0, ALU.mult, ALU.add).then_inc(s_b, 1)
                    dve.wait_ge(s_b, i * 2 + 2)
                    for n, L in enumerate(LEVELS):
                        bs, d = span(b[:], L), span(lev[:, n, :], L)
                        ref = bs[:, :, 0, L - 1:L].to_broadcast([P, T // (2 * L), L])
                        dve.tensor_tensor(d[:, :, 0, :], ref, bs[:, :, 0, :], ALU.subtract).then_inc(s_d, 1)
                        dve.tensor_tensor(d[:, :, 1, :], bs[:, :, 1, :], ref, ALU.subtract).then_inc(s_d, 1)
                    bc = chunks(b[:])
                    dve.tensor_tensor(chunks(ee[:]), bc[:, :, P - 1:P].to_broadcast([P, NC, P]), bc, ALU.subtract).then_inc(s_d, 1)
                    for n, L in enumerate(LEVELS):
                        d = span(lev[:, n, :], L)
                        dve.wait_ge(s_e, i * (NL + 2) + n + 1)
                        dve.tensor_tensor(d[:, :, 0, :], d[:, :, 0, :], span(k[:], L)[:, :, 0, :], ALU.mult).then_inc(s_t, 1)
                        dve.tensor_tensor(d[:, :, 1, :], d[:, :, 1, :], span(q[:], L)[:, :, 1, :], ALU.mult).then_inc(s_t, 1)
                    dve.wait_ge(s_e, (i + 1) * (NL + 2))
                    dve.tensor_tensor(qb[:], q[:], eb[:], ALU.mult).then_inc(s_t, 1)
                    dve.tensor_tensor(ke[:], k[:], ee[:], ALU.mult).then_inc(s_t, 1)
                    step = Count(dve, s_dt, i * (2 * DIAG - 1))
                    for n in range(DIAG):
                        W = DIAG - n
                        if n > 0:
                            src = blocks((k if n == 1 else kf[(n - 1) % 2])[:])
                            if n > 1:
                                dve.wait_ge(s_kf, i * (DIAG - 1) + n - 1)
                            dve.tensor_tensor(blocks(kf[n % 2][:])[:, :, n:], src[:, :, n - 1:DIAG - 1], blocks(f[:])[:, :, n:], ALU.mult) \
                                .then_inc(s_kf, 1)
                            dve.wait_ge(s_kf, i * (DIAG - 1) + n)
                        keys = k if n == 0 else kf[n % 2]
                        if n >= 2:
                            dve.wait_ge(s_dg, i * DIAG + n - 1)
                        prod = pr[n % 2][:, 0:P * W].rearrange("p (n l) -> p n l", l=W)
                        dve.tensor_tensor(prod, blocks(q[:])[:, :, n:], blocks(keys[:])[:, :, n:], ALU.mult).then_inc(s_pr, 1)
                        dve.wait_ge(s_dg, i * DIAG + n + 1)
                        sums = pd[:, :, 0:64 * W].rearrange("p a (n l) -> p a n l", l=W)
                        past = blocks(vi[:]).rearrange("p (a n) l -> p a n l", a=2)[:, :, :, 0:W]
                        if n == 0:
                            dve.wait_ge(s_st, i * 16)
                            o = od[:].rearrange("p (a n l) -> p a n l", a=2, l=DIAG)
                            step(dve.tensor_tensor(o, sums, past, ALU.mult))
                        else:
                            t = dt[:, 0:P * W].rearrange("p (a n l) -> p a n l", a=2, l=W)
                            step(dve.tensor_tensor(t, sums, past, ALU.mult))
                            o = blocks(od[:])[:, :, n:]
                            step(dve.tensor_tensor(o, o, dt[:, 0:P * W].rearrange("p (n l) -> p n l", l=W), ALU.add))
                    assert step.n == 2 * DIAG - 1
                    dve.memset(S[:], 0.0).then_inc(s_S, 1)
                    step = Count(dve, s_m, i * 3 * NC)
                    for c in range(NC):
                        a = att[c % 2]
                        dve.wait_ge(s_lv, i * NC + c + 1)
                        step(dve.tensor_tensor(a[:], pa[c % 2][:], masks, ALU.mult))
                        step(dve.tensor_tensor(a[:, 0:2, :], a[:, 0:2, :], a[:, 2:4, :], ALU.add))
                        step(dve.tensor_tensor(a[:, 0, :], a[:, 0, :], a[:, 1, :], ALU.add))
                        dve.wait_ge(s_o, i * NC + c + 1)
                        dve.scalar_tensor_tensor(S[:], S[:], eb[:, c * P + P - 1:c * P + P], psu[:], ALU.mult, ALU.add).then_inc(s_S, 1)
                        dve.wait_ge(s_S, i * (NC + 1) + c + 2)
                    dve.tensor_tensor(od[:], od[:], po[:].rearrange("p a t -> p (a t)"), ALU.add).then_inc(s_fin, 1)

            @block.tensor
            def _(pe):
                with pe.Fori(0, 4) as i:
                    pe.wait_ge(s_t, (i + 1) * NT_)
                    for n in range(2):
                        for c in range(4):
                            mm = pe.transpose(pd[:, n, c * P:(c + 1) * P], ke[:, (4 * n + c) * P:(4 * n + c + 1) * P], K.c("ident"))
                        mm.then_inc(s_kt, 1)

                    def levels(c):
                        if c >= 2:
                            pe.wait_ge(s_m, i * 3 * NC + 3 * (c - 2) + 1)
                        for l in range(NL):
                            o = lev[:, l, c * P:(c + 1) * P]
                            mm = pe.matmul(pa[c % 2][:, l, :], o, o, start=True, stop=True)
                        mm.then_inc(s_lv, 1)
                    levels(0)
                    levels(1)
                    for n in range(DIAG):
                        W = DIAG - n
                        pe.wait_ge(s_pr, i * DIAG + n + 1)
                        if n == 0:
                            pe.wait_ge(s_ktc, i * 2 + 2)
                        else:
                            pe.wait_ge(s_dt, i * (2 * DIAG - 1) + max(1, 2 * n - 2))
                        for h in range(2):
                            mm = pe.matmul(pd[:, h, 0:64 * W], K.c("ones"), pr[n % 2][:, h * 64 * W:(h + 1) * 64 * W], start=True, stop=True)
                        mm.then_inc(s_dg, 1)
                    pe.wait_ge(s_fin, i)
                    for c in range(NC):
                        if c >= 2:
                            levels(c)
                        pe.wait_ge(s_S, i * (NC + 1) + c + 1)
                        pe.matmul(psu[:], keT[:, c, :], vt[:, c, :], start=True, stop=True)
                        pe.wait_ge(s_m, i * 3 * NC + 3 * c + 3)
                        o = po[:, c // 4, (c % 4) * P:(c % 4 + 1) * P]
                        pe.matmul(o, vt[:, c, :], att[c % 2][:, 0, :], start=True, stop=False)
                        pe.matmul(o, S[:], qb[:, c * P:(c + 1) * P], start=False, stop=True).then_inc(s_o, 1)


def stage_windows(K):
    nc = K.nc
    qk, vT = K.scratch["bqk"], K.scratch["viT"]
    out = K.dram("win_o", [256, T])
    NT = T // P
    SC = 0.125
    with K.stage() as st:
        U = range(2)
        sb2 = lambda n, shape: [K.sb(f"win_{n}{u}", shape, stack=st) for u in U]
        q, k = K.sb("win_q", [64, T], stack=st), K.sb("win_k", [64, T], stack=st)
        v = K.sb("win_v", [P, NT, 64], stack=st)
        wide = K.sb("win_mult", [P, 2, T], stack=st)
        sc, mx, zs, rz = sb2("scores", [P, T]), sb2("max", [P, 1]), sb2("sum", [P, 1]), sb2("inv", [P, 1])
        dg, pT = sb2("diag", [P, P]), sb2("probsT", [P, NT, P])
        ob = K.sb("win_out_sb", [64, T], stack=st)
        ps = [K.ps(f"win_s{u}", [P, 2, BANK], st) for u in U]
        pt = K.ps("win_t", [P, 2, 4, P], st)
        po = K.ps("win_out", [64, 2, BANK], st)
        s_in, s_c, s_s, s_pt, s_pc, s_o, s_ob, s_st = (K.sem(f"win_{n}") for n in (
            "in", "const", "scores", "turned", "copied", "o", "evac", "stored"))
        s_v, s_x = K.sem("win_vec"), K.sem("win_exp")
        NV = 7
        with nc.Block() as block:
            @block.sync
            def _(sp):
                sp.dma_start(wide[:], K.wide_dram.rearrange("p (a t) -> p a t", a=2)).then_inc(s_c, 16)
                with sp.Fori(0, 4) as i:
                    sp.wait_ge(s_ob, i)
                    rows = bass.ds(i * 64, 64)
                    sp.dma_start(q[:], qk[rows, :]).then_inc(s_in, 16)
                    sp.dma_start(k[:], qk[bass.ds(i * 64 + 256, 64), :]).then_inc(s_in, 16)
                    sp.dma_start(v[:], vT[:, bass.ds(i * 64 + 512, 64)].rearrange("(c t) v -> t c v", t=P)).then_inc(s_in, 16)

            @block.tensor
            def _(pe):
                with pe.Fori(0, 4) as i:
                    pe.wait_ge(s_in, (i + 1) * 48)

                    def scores(n):
                        W = (n + 1) * P
                        pe.wait_ge(s_v, i * (NT * NV) + NV * (n - 2) + 1 if n >= 2 else i * (NT * NV))
                        pe.wait_ge(s_c, 16)
                        for h in range(-(-W // BANK)):
                            w = min(BANK, W - h * BANK)
                            mm = pe.matmul(ps[n % 2][:, h, 0:w], q[:, n * P:(n + 1) * P], k[:, h * BANK:h * BANK + w], start=True, stop=True)
                        mm.then_inc(s_s, 1)
                    scores(0)
                    for n in range(NT):
                        if n + 1 < NT:
                            scores(n + 1)
                        pe.wait_ge(s_v, i * (NT * NV) + NV * (n + 1))
                        pe.wait_ge(s_pc, i * NT + n)
                        for c in range(n + 1):
                            mm = pe.matmul(pt[:, c // 4, c % 4, :], sc[n % 2][:, c * P:(c + 1) * P], dg[n % 2][:], start=True, stop=True)
                        mm.then_inc(s_pt, 1)
                        pe.wait_ge(s_pc, i * NT + n + 1)
                        if n == 0:
                            pe.wait_ge(s_ob, i)
                        for c in range(n + 1):
                            mm = pe.matmul(po[:, n // 4, (n % 4) * P:(n % 4 + 1) * P], v[:, c, :], pT[n % 2][:, c, :],
                                           start=c == 0, stop=c == n)
                        mm.then_inc(s_o, 1)

            @block.vector
            def _(dve):
                dve.wait_ge(s_c, 16)
                with dve.Fori(0, 4) as i:
                    for n in range(NT):
                        W = (n + 1) * P
                        u = n % 2
                        step = Count(dve, s_v, i * (NT * NV) + n * NV)
                        dve.wait_ge(s_s, i * NT + n + 1)
                        if n >= 2:
                            dve.wait_ge(s_pt, i * NT + n - 1)
                        s = sc[u][:, 0:W]
                        flat = ps[u][:].rearrange("p a t -> p (a t)")[:, 0:W]
                        step(dve.tensor_tensor(s, flat, wide[:, 1, T - W:T], ALU.add))
                        step(dve.tensor_reduce(mx[u][:], s, AX.X, ALU.max))
                        step(dve.tensor_scalar(mx[u][:], mx[u][:], -SC, None, ALU.mult))
                        dve.wait_ge(s_x, i * NT + n + 1)
                        step(dve.tensor_tensor(s, s, wide[:, 0, T - W:T], ALU.mult))
                        step(dve.tensor_reduce(zs[u][:], s, AX.X, ALU.add))
                        step(dve.reciprocal(rz[u][:], zs[u][:]))
                        step(dve.tensor_scalar(dg[u][:], K.c("ident"), rz[u][:], None, ALU.mult))
                    dve.wait_ge(s_o, (i + 1) * NT)
                    dve.wait_ge(s_st, i * 16)
                    dve.tensor_copy(ob[:], po[:].rearrange("p a t -> p (a t)")).then_inc(s_ob, 1)

            @block.scalar
            def _(act):
                with act.Fori(0, 4) as i:
                    def turned(n):
                        act.wait_ge(s_pt, i * NT + n + 1)
                        if n >= 2:
                            act.wait_ge(s_o, i * NT + n - 1)
                        act.activation(pT[n % 2][:, 0:n + 1, :], pt[:].rearrange("p a b t -> p (a b) t")[:, 0:n + 1, :], ACT.Copy).then_inc(s_pc, 1)
                    for n in range(NT):
                        act.wait_ge(s_v, i * (NT * NV) + n * NV + 3)
                        s = sc[n % 2][:, 0:(n + 1) * P]
                        act.activation(s, s, ACT.Exp, scale=SC, bias=mx[n % 2][:]).then_inc(s_x, 1)
                        if n:
                            turned(n - 1)
                    turned(NT - 1)
                    act.wait_ge(s_ob, i + 1)
                    act.dma_start(out[bass.ds(i * 64, 64), :], ob[:]).then_inc(s_st, 16)
                act.wait_ge(s_st, 64)


RK_WD = 768
RK_CH = 64
RK_ALPHA, RK_RHO, RK_K, RK_B, RK_KG, RK_BG, RK_V = range(7)


def stage_rwkv_prep(K):
    nc, A = K.nc, K.A
    cin = K.scratch["cin"]
    rk, rkG = K.dram("rk", [7, 256, T]), K.dram("rk_G", [256, T // RK_CH])
    NC, MID = T // RK_CH, RK_CH // 2 - 1
    DECAY = -float(np.exp(-0.5))
    with K.stage() as st:
        sb = lambda n, shape: K.sb(f"rp_{n}", shape, stack=st)
        raw = [sb(f"raw_{n}", [P, T + 1]) for n in ("r", "k", "v", "ranks", "gate")]
        r, k, v, ranks, gate = (sb(n, [P, T]) for n in ("r", "k", "v", "ranks", "gate"))
        w2, a2, g2 = sb("w2", [P, 256]), sb("a2", [P, 256]), sb("g2", [P, 256])
        d = [sb(f"diff{n}", [P, T]) for n in range(2)]
        lw, a, b, bm = sb("logw", [P, T]), sb("a", [P, T]), sb("cum", [P, T]), sb("cum_mid", [P, T])
        kk, sq, inv, ep, en, ea = (sb(n, [P, T]) for n in ("kk", "sq", "inv", "e_pos", "e_neg", "e_alpha"))
        reset, emid, G = sb("reset", [P, T]), sb("e_mid", [P, NC + 1]), sb("G", [P, NC])
        outs = [sb(f"out{n}", [P, T]) for n in range(6)]
        pw, pa, pg, pn = (K.ps(f"rp_{n}", [P, 2, BANK], st) for n in ("w", "a", "g", "sum"))
        s_z, s_w, s_lo, s_in, s_mix, s_low, s_z3, s_sig, s_gc, s_v, s_kk, s_sq, s_n, s_rt, s_e, s_bo, s_bp, s_out, s_st = (
            K.sem(f"rp_{n}") for n in ("zero", "weights", "ranks_in", "in", "mixed", "ranks", "products", "sigmoid", "gate_copied", "vec", "kk",
                                       "squares", "norm2", "root", "exp", "bonus", "bonus_sum", "out", "stored"))
        chunks = lambda t: t.rearrange("p (c t) -> p c t", t=RK_CH)
        flat = lambda t: t.rearrange("p a t -> p (a t)")
        NV = 8
        with nc.Block() as block:
            @block.gpsimd
            def _(pool):
                for x in raw:
                    pool.memset(x[:, 0:1], 0.0).then_inc(s_z, 1)
                pool.memset(reset[:], 1.0).then_inc(s_z, 1)
                pool.memset(emid[:, NC:NC + 1], 1.0).then_inc(s_z, 1)
                pool.memset(w2[:], 0.0).then_inc(s_z, 1)
                pool.memset(a2[:], 0.0).then_inc(s_z, 1)
                pool.wait_ge(s_z, 9)
                pool.memset(chunks(reset[:])[:, :, 0:1], 0.0).then_inc(s_z, 1)
                pool.dma_start(w2[0:64, :], A["rwkv_w2_2"][0]).then_inc(s_w, 16)
                pool.dma_start(a2[64:P, :], A["rwkv_a2_2"][0]).then_inc(s_w, 16)
                pool.dma_start(g2[:], A["rwkv_g2_2"][0]).then_inc(s_w, 16)

            @block.sync
            def _(sp):
                sp.dma_start(raw[3][:, 1:T + 1], cin[RK_WD:RK_WD + P, :]).then_inc(s_lo, 16)
                sp.dma_start(raw[4][:, 1:T + 1], cin[RK_WD + P:RK_WD + 2 * P, :]).then_inc(s_lo, 16)
                with sp.Fori(0, 2) as i:
                    sp.wait_ge(s_mix, i * 3 + 2)
                    for n in range(3):
                        sp.dma_start(raw[n][:, 1:T + 1], cin[bass.ds(i * P + n * 256, P), :]).then_inc(s_in, 16)
                    rows = bass.ds(i * P, P)
                    for n in range(6):
                        sp.wait_ge(s_out, i * 7 + n + 1)
                        sp.dma_start(rk[n, rows, :], outs[n][:]).then_inc(s_st, 16)
                    sp.dma_start(rk[RK_V, rows, :], v[:]).then_inc(s_st, 16)
                    sp.wait_ge(s_out, i * 7 + 7)
                    sp.dma_start(rkG[rows, :], G[:]).then_inc(s_st, 16)
                sp.wait_ge(s_st, 2 * 8 * 16)

            @block.vector
            def _(dve):
                def mixed(x, dst, mu, n):
                    dve.tensor_tensor(d[n % 2][:], x[:, 0:T], x[:, 1:T + 1], ALU.subtract).then_inc(s_kk, 1)
                    return dve.scalar_tensor_tensor, (dst[:], d[n % 2][:], mu, x[:, 1:T + 1], ALU.mult, ALU.add)
                dve.wait_ge(s_z, 10)
                dve.wait_ge(s_lo, 2 * 16)
                for n, (x, dst) in enumerate(((raw[3], ranks), (raw[4], gate))):
                    op, args = mixed(x, dst, K.col("rwkv_mu_2", 6 + n), n)
                    dve.wait_ge(s_kk, n + 1)
                    op(*args).then_inc(s_mix, 1)
                NK = 8
                pcol = lambda name, i: K.cols[:, bass.ds(i + K.col_at[name], 1)]
                with dve.Fori(0, 2) as i:
                    dve.wait_ge(s_in, (i + 1) * 48)
                    dve.wait_ge(s_st, i * (8 * 16))
                    step = Count(dve, s_kk, i * NK, 2)
                    for n, (x, dst) in enumerate(((raw[0], r), (raw[1], k), (raw[2], v))):
                        op, args = mixed(x, dst, pcol("rwkv_mu_2", i + 2 * n), n)
                        step.n += 1
                        dve.wait_ge(s_kk, i * NK + step.n)
                        op(*args).then_inc(s_mix, 1)
                    dve.wait_ge(s_mix, i * 3 + 5)
                    step(dve.tensor_scalar(kk[:], k[:], pcol("rwkv_k_k_2", i), None, ALU.mult))
                    vec = Count(dve, s_v, i * NV)
                    dve.wait_ge(s_sig, i * 2 + 2)
                    vec(dve.tensor_scalar(lw[:], lw[:], DECAY, None, ALU.mult))
                    vec(dve.tensor_tensor_scan(b[:], reset[:], lw[:], 0.0, ALU.mult, ALU.add))
                    mid = chunks(b[:])[:, :, MID:MID + 1]
                    vec(dve.tensor_tensor(chunks(bm[:]), chunks(b[:]), mid.to_broadcast([P, NC, RK_CH]), ALU.subtract))
                    vec.mark(dve.tensor_tensor(ea[:], bm[:], lw[:], ALU.subtract))
                    step(dve.tensor_scalar(d[0][:], a[:], -1.0, pcol("rwkv_k_a_2", i), ALU.add, ALU.mult))
                    step(dve.scalar_tensor_tensor(k[:], d[0][:], 1.0, k[:], ALU.add, ALU.mult))
                    step(dve.scalar_tensor_tensor(d[1][:], r[:], pcol("rwkv_r_k_2", i), k[:], ALU.mult, ALU.mult))
                    dve.wait_ge(s_rt, i + 1)
                    step(dve.tensor_scalar(inv[:], inv[:], 1e-12, None, ALU.max))
                    vec(dve.reciprocal(inv[:], inv[:]))
                    vec(dve.tensor_tensor(kk[:], kk[:], inv[:], ALU.mult))
                    dve.wait_ge(s_e, i * 4 + 4)
                    dve.scalar_tensor_tensor(outs[RK_ALPHA][:], kk[:], -1.0, ea[:], ALU.mult, ALU.mult).then_inc(s_out, 1)
                    dve.tensor_tensor(outs[RK_RHO][:], r[:], ep[:], ALU.mult).then_inc(s_out, 1)
                    dve.tensor_tensor(outs[RK_K][:], k[:], en[:], ALU.mult).then_inc(s_out, 1)
                    vec(dve.tensor_tensor(kk[:], kk[:], a[:], ALU.mult))
                    dve.tensor_tensor(outs[RK_B][:], kk[:], en[:], ALU.mult).then_inc(s_out, 1)
                    vec(dve.tensor_tensor(G[:], chunks(ep[:])[:, :, RK_CH - 1], emid[:, 1:NC + 1], ALU.mult))
                    dve.wait_ge(s_out, i * 7 + 4)
                    g = G[:].unsqueeze(2).to_broadcast([P, NC, RK_CH])
                    dve.tensor_tensor(chunks(outs[RK_KG][:]), chunks(outs[RK_K][:]), g, ALU.mult).then_inc(s_out, 1)
                    dve.tensor_tensor(chunks(outs[RK_BG][:]), chunks(outs[RK_B][:]), g, ALU.mult).then_inc(s_out, 1)
                    dve.wait_ge(s_bp, i + 1)
                    bonus = flat(K.rk_bonus[:])[:, bass.ds(i * T, T)]
                    dve.tensor_tensor(bonus, flat(pn[:]), v[:], ALU.mult).then_inc(s_out, 1)
                    assert step.n == 2 + NK and vec.n == NV

            @block.scalar
            def _(act):
                pcol = lambda name, i: K.cols[:, bass.ds(i + K.col_at[name], 1)]
                act.wait_ge(s_mix, 2)
                act.activation(ranks[0:64, :], ranks[0:64, :], ACT.Tanh).then_inc(s_low, 1)
                act.activation(gate[:], gate[:], ACT.Sigmoid).then_inc(s_low, 1)
                with act.Fori(0, 2) as i:
                    act.wait_ge(s_z3, i + 1)
                    act.wait_ge(s_out, i * 7)
                    act.activation(lw[:], flat(pw[:]), ACT.Sigmoid, bias=pcol("rwkv_w0_2", i)).then_inc(s_sig, 1)
                    act.activation(a[:], flat(pa[:]), ACT.Sigmoid, bias=pcol("rwkv_a0_2", i)).then_inc(s_sig, 1)
                    act.activation(flat(K.rk_gate[:])[:, bass.ds(i * T, T)], flat(pg[:]), ACT.Copy).then_inc(s_gc, 1)
                    act.wait_ge(s_kk, i * 8 + 6)
                    act.activation(sq[:], kk[:], ACT.Square).then_inc(s_sq, 1)
                    act.wait_ge(s_n, i + 1)
                    act.activation(inv[:], flat(pn[:]), ACT.Sqrt).then_inc(s_rt, 1)
                    act.wait_ge(s_v, i * NV + 4)
                    act.activation(emid[:, 0:NC], chunks(b[:])[:, :, MID], ACT.Exp).then_inc(s_e, 1)
                    act.activation(ep[:], bm[:], ACT.Exp).then_inc(s_e, 1)
                    act.activation(en[:], bm[:], ACT.Exp, scale=-1.0).then_inc(s_e, 1)
                    act.activation(ea[:], ea[:], ACT.Exp).then_inc(s_e, 1)

            @block.tensor
            def _(pe):
                pe.wait_ge(s_low, 2)
                pe.wait_ge(s_w, 3 * 16)
                for i in range(2):
                    if i:
                        pe.wait_ge(s_sig, 2)
                        pe.wait_ge(s_gc, 1)
                    for h in range(2):
                        t = slice(h * BANK, (h + 1) * BANK)
                        pe.matmul(pw[:, h, :], w2[:, i * P:(i + 1) * P], ranks[:, t], start=True, stop=True)
                        pe.matmul(pa[:, h, :], a2[:, i * P:(i + 1) * P], ranks[:, t], start=True, stop=True)
                        mm = pe.matmul(pg[:, h, :], g2[:, i * P:(i + 1) * P], gate[:, t], start=True, stop=True)
                    mm.then_inc(s_z3, 1)
                    pe.wait_ge(s_sq, i + 1)
                    if i:
                        pe.wait_ge(s_out, 7)
                    for h in range(2):
                        mm = pe.matmul(pn[:, h, :], K.c("ones64"), sq[:, h * BANK:(h + 1) * BANK], start=True, stop=True)
                    mm.then_inc(s_n, 1)
                    pe.wait_ge(s_kk, i * 8 + 9)
                    pe.wait_ge(s_rt, i + 1)
                    for h in range(2):
                        mm = pe.matmul(pn[:, h, :], K.c("ones64"), d[1][:, h * BANK:(h + 1) * BANK], start=True, stop=True)
                    mm.then_inc(s_bp, 1)


def stage_rwkv(K):
    nc = K.nc
    rk, rkG = K.scratch["rk"], K.scratch["rk_G"]
    out = K.dram("rk_y", [256, T])
    H, HD, NC = 4, 64, T // RK_CH
    LV = (2, 4, 8, 16, 32)
    with K.stage() as st:
        sb = lambda n, shape: K.sb(f"rks_{n}", shape, stack=st)
        f = sb("in", [HD, 7, H, P])
        Gc, diagG = sb("Gcol", [HD, H, NC]), sb("diagG", [HD, NC, H, HD])
        v, RA, KBz = sb("vT", [P, H, HD]), sb("KAv_alpha", [P, H, 2, HD]), sb("KG_BG", [P, H, 2, 2, HD])
        AB, KK = sb("A_BR", [P, H, 2, P]), sb("KA_KR", [P, H, 2, P])
        X, XT, W = sb("X", [P, H, P]), sb("XT", [P, H, P]), sb("AX", [P, H, P])
        SX = sb("SA_Xalpha", [P, H, 2, HD])
        Ms, Ns = sb("M", [HD, 2, H, HD]), sb("N", [HD, H, 2, HD])
        rho = sb("rho", [HD, H, P])
        S = [sb(f"S{n}", [HD, H, HD]) for n in range(2)]
        yb = sb("y", [HD, H, P])
        pT = K.ps("rk_turned", [P, 2, BANK], st)
        pB = K.ps("rk_AB", [P, H, 2, P], st)
        pK = K.ps("rk_KK", [P, H, 2, P], st)
        pA = K.ps("rk_A", [P, H, P], st)
        pY = K.ps("rk_Y", [HD, H, P], st)
        s_c, s_d, s_S0, s_in, s_t, s_tok, s_sc, s_msk, s_x, s_w, s_wm, s_xx, s_r, s_rc, s_xr, s_xrc, s_mn, s_ms, s_ns, s_up, s_S, s_y, s_yc, s_st = (
            K.sem(f"rk_{n}") for n in ("G", "diag", "init", "in", "turned", "tokens", "scores", "masked", "X", "AX", "AX_masked", "X_more",
                                       "KAv", "KAv_copied", "SA", "SA_copied", "MN", "M_copied", "N_copied", "update", "S", "y",
                                       "y_copied", "stored"))
        pTr = pT[:].rearrange("p a (h q e) -> p (a h) q e", h=2, q=4)
        pX = [pT[:, n, :].rearrange("p (h t) -> p h t", h=H) for n in range(2)]
        pM = pB[0:HD, 0:2].rearrange("p a b t -> p (a b) t").rearrange("p h (c e) -> p h c e", c=2)
        pN = pB[0:HD, 2:4].rearrange("p a b t -> p (a b) t").rearrange("p h (c e) -> p h c e", c=2)
        pR = pK[:, 0:2].rearrange("p a b t -> p (a b) t")
        pSX = pK[:, 2:4].rearrange("p a b t -> p (a b) t")
        o_lt = K.const_at["lt_half"][0]
        strict = K.const[:, o_lt:o_lt + 2 * P].unsqueeze(1).to_broadcast([P, H, 2 * P])
        both = lambda name: K.c(name).unsqueeze(1).to_broadcast([P, H, P])
        NX = 3 + 2 * len(LV) - 1
        with nc.Block() as block:
            @block.sync
            def _(sp):
                sp.dma_start(Gc[:], rkG.rearrange("(h p) c -> p h c", p=HD)).then_inc(s_c, 16)
                with sp.Fori(0, T // P) as i:
                    sp.wait_ge(s_ms, i * 2)
                    for n in range(7):
                        sp.dma_start(f[:, n], rk[n, :, bass.ds(i * P, P)].rearrange("(h p) t -> p h t", p=HD)).then_inc(s_in, 16)

            @block.tensor
            def _(pe):
                pe.wait_ge(s_S0, 1)
                with pe.Fori(0, T // P) as i:
                    pe.wait_ge(s_in, (i + 1) * 112)
                    pe.wait_ge(s_S, i * 2)
                    for h in range(H):
                        mm = pe.matmul(pA[:, h, :], f[:, RK_ALPHA, h, :], f[:, RK_B, h, :], start=True, stop=True)
                    mm.then_inc(s_sc, 1)
                    for h in range(H):
                        for q, n in enumerate((RK_V, RK_ALPHA, RK_KG, RK_BG)):
                            mm = pe.transpose(pTr[:, h, q, :], f[:, n, h, :], K.c("ident")[0:HD, 0:HD])
                    mm.then_inc(s_t, 1)
                    pe.wait_ge(s_ms, i * 2)
                    pe.wait_ge(s_ns, i)
                    for h in range(H):
                        mm = pe.matmul(pB[:, h], f[:, RK_B, h, :], f[:, 0:2, h, :], start=True, stop=True)
                    mm.then_inc(s_sc, 1)
                    for h in range(H):
                        mm = pe.matmul(pK[:, h], f[:, RK_K, h, :], f[:, 0:2, h, :], start=True, stop=True)
                    mm.then_inc(s_sc, 1)
                    pe.wait_ge(s_tok, i * 4 + 4)
                    for n in range(len(LV)):
                        pe.wait_ge(s_x, i * NX + 3 + 2 * n)
                        for h in range(H):
                            mm = pe.matmul(pA[:, h, :], AB[:, h, 0, :], X[:, h, :], start=True, stop=True)
                        mm.then_inc(s_w, 1)
                        pe.wait_ge(s_wm, i * len(LV) + n + 1)
                        for h in range(H):
                            mm = pe.matmul(pX[1][:, h, :], W[:, h, :], XT[:, h, :], start=True, stop=True)
                        mm.then_inc(s_xx, 1)
                        if n < len(LV) - 1:
                            for h in range(H):
                                mm = pe.matmul(pX[0][:, h, :], XT[:, h, :], W[:, h, :], start=True, stop=True)
                            mm.then_inc(s_xx, 1)
                    pe.wait_ge(s_msk, i * 2 + 2)
                    for h in range(H):
                        mm = pe.matmul(pR[:, h, 0:HD], KK[:, h, 0, :], v[:, h, :], start=True, stop=True)
                    mm.then_inc(s_r, 1)
                    pe.wait_ge(s_rc, i + 1)
                    pe.wait_ge(s_x, (i + 1) * NX)
                    for h in range(H):
                        mm = pe.matmul(pSX[:, h, :], XT[:, h, :], RA[:, h], start=True, stop=True)
                    mm.then_inc(s_xr, 1)
                    pe.wait_ge(s_xrc, i + 1)
                    for h in range(H):
                        pe.matmul(pM[:, h], SX[:, h, 1, :], KBz[:, h, 1], start=True, stop=True)
                        pe.matmul(pR[0:HD, h, :], SX[:, h, 1, :], AB[:, h, 1, :], start=True, stop=True)
                        for c in range(2):
                            pe.matmul(pN[:, h, c, :], KBz[:, h, 0, c, :], v[:, h, :], start=True, stop=False)
                            mm = pe.matmul(pN[:, h, c, :], KBz[:, h, 1, c, :], SX[:, h, 0, :], start=False, stop=True)
                    mm.then_inc(s_mn, 1)
                    pe.wait_ge(s_ms, i * 2 + 2)
                    pe.wait_ge(s_yc, i)
                    for c in range(2):
                        pe.wait_ge(s_S, i * 2 + c)
                        t = slice(c * HD, (c + 1) * HD)
                        o = [pY[:, h, t] for h in range(H)]
                        pe.matmul(o[0], v[:, 0, :], KK[:, 0, 1, t], start=True, stop=False)
                        for h in range(H):
                            mm = pe.matmul(pA[0:HD, h, 0:HD], Ms[:, c, h, :], S[c][:, h, :], start=True, stop=True)
                        mm.then_inc(s_up, 1)
                        for h in range(H):
                            if h:
                                pe.matmul(o[h], v[:, h, :], KK[:, h, 1, t], start=True, stop=False)
                            pe.matmul(o[h], SX[:, h, 0, :], AB[:, h, 1, t], start=False, stop=False)
                            mm = pe.matmul(o[h], S[c][:, h, :], rho[:, h, t], start=False, stop=True)
                        mm.then_inc(s_y, 1)

            @block.scalar
            def _(act):
                with act.Fori(0, T // P) as i:
                    act.wait_ge(s_t, i + 1)
                    act.wait_ge(s_y, i * 2)
                    act.activation(v[:], pTr[:, :, 0, :], ACT.Copy).then_inc(s_tok, 1)
                    act.activation(RA[:, :, 1, :], pTr[:, :, 1, :], ACT.Copy).then_inc(s_tok, 1)
                    for c in range(2):
                        half = K.c("halves")[:, c:c + 1]
                        act.activation(KBz[:, :, :, c, :], pTr[:, :, 2:4, :], ACT.Copy, scale=half).then_inc(s_tok, 1)
                    act.wait_ge(s_r, i + 1)
                    act.activation(RA[:, :, 0, :], pR[:, :, 0:HD], ACT.Copy).then_inc(s_rc, 1)
                    act.wait_ge(s_xr, i + 1)
                    act.activation(SX[:].rearrange("p h a e -> p h (a e)"), pSX, ACT.Copy).then_inc(s_xrc, 1)
                    act.wait_ge(s_mn, i + 1)
                    act.activation(Ns[:], pN, ACT.Copy).then_inc(s_ns, 1)
                    act.wait_ge(s_y, i * 2 + 2)
                    act.wait_ge(s_st, i * 16)
                    act.activation(yb[:], pY[:], ACT.Copy).then_inc(s_yc, 1)
                    act.wait_ge(s_yc, i + 1)
                    act.dma_start(out[:, bass.ds(i * P, P)].rearrange("(h p) t -> p h t", p=HD), yb[:]).then_inc(s_st, 16)
                act.wait_ge(s_st, T // P * 16)

            @block.vector
            def _(dve):
                dve.memset(S[0][:], 0.0).then_inc(s_S0, 1)
                dve.wait_ge(s_c, 16)
                for h in range(H):
                    one = K.c("ident")[0:HD, 0:HD].unsqueeze(1).to_broadcast([HD, NC, HD])
                    dve.tensor_tensor(diagG[:, :, h, :], one, Gc[:, h, :].unsqueeze(2).to_broadcast([HD, NC, HD]), ALU.mult).then_inc(s_d, 1)
                dve.wait_ge(s_d, H)
                with dve.Fori(0, T // P) as i:
                    step = Count(dve, s_x, i * NX)
                    dve.wait_ge(s_sc, i * 3 + 1)
                    step(dve.tensor_tensor(X[:], pA[:], both("pairT1"), ALU.mult))
                    step.mark(dve.tensor_tensor(X[:], X[:], both("ident"), ALU.add))
                    dve.wait_ge(s_y, i * 2)
                    dve.wait_ge(s_sc, i * 3 + 2)
                    dve.tensor_tensor(AB[:].rearrange("p h a t -> p h (a t)"), pB[:].rearrange("p h a t -> p h (a t)"), strict, ALU.mult) \
                        .then_inc(s_msk, 1)
                    dve.wait_ge(s_msk, i * 2 + 1)
                    dve.tensor_tensor(XT[:], AB[:, :, 0, :], both("pair1"), ALU.mult).then_inc(s_d, 1)
                    dve.wait_ge(s_d, H + i + 1)
                    step.mark(dve.tensor_tensor(XT[:], XT[:], both("ident"), ALU.add))
                    dve.wait_ge(s_sc, i * 3 + 3)
                    dve.tensor_tensor(KK[:].rearrange("p h a t -> p h (a t)"), pK[:].rearrange("p h a t -> p h (a t)"), strict, ALU.mult) \
                        .then_inc(s_msk, 1)
                    for n, l in enumerate(LV):
                        dve.wait_ge(s_w, i * len(LV) + n + 1)
                        dve.tensor_tensor(W[:], pA[:], both(f"pairT{l}"), ALU.mult).then_inc(s_wm, 1)
                        dve.wait_ge(s_xx, i * (2 * len(LV) - 1) + 2 * n + 1)
                        last = n == len(LV) - 1
                        if not last:
                            dve.wait_ge(s_xx, i * (2 * len(LV) - 1) + 2 * n + 2)
                        step.mark(dve.tensor_tensor(XT[:], XT[:], pX[1], ALU.add))
                        if not last:
                            step.mark(dve.tensor_tensor(X[:], X[:], pX[0], ALU.add))
                    assert step.n == NX
                    dve.wait_ge(s_mn, i + 1)
                    g = diagG[:].rearrange("p c h e -> p (c h e)")[:, bass.ds(i * (2 * H * HD), 2 * H * HD)]
                    dve.tensor_tensor(Ms[:], pM.rearrange("p h c e -> p c h e"), g.rearrange("p (c h e) -> p c h e", c=2, h=H), ALU.add) \
                        .then_inc(s_ms, 1)
                    dve.tensor_tensor(rho[:], f[:, RK_RHO], pR[0:HD], ALU.add).then_inc(s_ms, 1)
                    dve.wait_ge(s_ns, i + 1)
                    for c in range(2):
                        dve.wait_ge(s_up, i * 2 + c + 1)
                        if c:
                            dve.wait_ge(s_y, i * 2 + c)
                        dve.tensor_tensor(S[1 - c][:], pA[0:HD, :, 0:HD], Ns[:, :, c, :], ALU.add).then_inc(s_S, 1)


def stage_rwkv_out(K, mixF, tile):
    nc = K.nc
    y_in = K.scratch["rk_y"]
    with K.stage() as st:
        U = range(2)
        sb2 = lambda n: [K.sb(f"ro_{n}{u}", [P, T], stack=st) for u in U]
        y, sq, rs = sb2("y"), sb2("sq"), sb2("rstd")
        pm, pv = ([K.ps(f"ro_{n}{u}", [P, 2, BANK], st) for u in U] for n in ("mean", "var"))
        s_in, s_mm, s_v, s_a = (K.sem(f"ro_{n}") for n in ("in", "means", "vec", "act"))
        flat = lambda t: t.rearrange("p a t -> p (a t)")
        NV = 5
        with nc.Block() as block:
            @block.sync
            def _(sp):
                for u in U:
                    sp.dma_start(y[u][:], y_in[u * P:(u + 1) * P, :]).then_inc(s_in, 16)

            @block.tensor
            def _(pe):
                pe.wait_ge(s_in, 32)
                for u in U:
                    for h in range(2):
                        mm = pe.matmul(pm[u][:, h, :], K.c("mean64"), y[u][:, h * BANK:(h + 1) * BANK], start=True, stop=True)
                    mm.then_inc(s_mm, 1)
                for u in U:
                    pe.wait_ge(s_a, u + 1)
                    for h in range(2):
                        mm = pe.matmul(pv[u][:, h, :], K.c("mean64"), sq[u][:, h * BANK:(h + 1) * BANK], start=True, stop=True)
                    mm.then_inc(s_mm, 1)

            @block.scalar
            def _(act):
                for u in U:
                    act.wait_ge(s_v, u + 1)
                    act.activation(sq[u][:], y[u][:], ACT.Square).then_inc(s_a, 1)
                for u in U:
                    act.wait_ge(s_v, 2 + u * NV + 1)
                    act.activation(rs[u][:], rs[u][:], ACT.Sqrt).then_inc(s_a, 1)

            @block.vector
            def _(dve):
                for u in U:
                    dve.wait_ge(s_mm, u + 1)
                    dve.tensor_tensor(y[u][:], y[u][:], flat(pm[u][:]), ALU.subtract).then_inc(s_v, 1)
                for u in U:
                    step = Count(dve, s_v, 2 + u * NV)
                    dve.wait_ge(s_mm, 3 + u)
                    step(dve.tensor_scalar(rs[u][:], flat(pv[u][:]), RK_GN_EPS, None, ALU.add))
                    dve.wait_ge(s_a, 3 + u)
                    step(dve.reciprocal(rs[u][:], rs[u][:]))
                    step(dve.scalar_tensor_tensor(y[u][:], y[u][:], K.col("rwkv_ln_w_2", u), rs[u][:], ALU.mult, ALU.mult))
                    step(dve.scalar_tensor_tensor(y[u][:], y[u][:], K.col("rwkv_ln_b_2", u), K.rk_bonus[:, u, :], ALU.add, ALU.add))
                    step(dve.tensor_tensor(mixF[:, tile + u, :], y[u][:], K.rk_gate[:, u, :], ALU.mult))
                    assert step.n == NV


def stage_load_rows(K, name, src, dst, tile):
    with K.stage():
        s_in = K.sem(f"{name}_in")
        with K.nc.Block() as block:
            @block.sync
            def _(sp):
                for k in range(src.shape[0] // P):
                    sp.dma_start(dst[:, tile + k, :], src[k * P:(k + 1) * P, :]).then_inc(s_in, 16)
                sp.wait_ge(s_in, src.shape[0] // P * 16)


def mixer_two(K):
    A = K.A
    w_in = A["w_in_2"][0]
    with ExitStack() as norm:
        K.hN = K.sb("hN3", [P, KT, T], stack=norm)
        stage_norm(K, "nm", K.hF, K.hN, T, K.cols[:, K.col_at["norm_mix_g_2"]:K.col_at["norm_mix_g_2"] + 8])
        for name, c0, n, func in (("hq", HQ, 512, ACT.Silu), ("hf", HF_, 512, ACT.Copy), ("hi", HI, 512, ACT.Copy),
                                  ("hg", HG, 512, ACT.Silu), ("bqk", BQ, 512, ACT.Copy), ("cin", CIN, 1024, ACT.Copy)):
            stage_gemm_f(K, name, w_in[:, c0:c0 + n], n, K.hN, T, K.dram(name, [n, T]), func)
        viT = K.dram("viT", [T, 768])
        stage_gemm_t(K, "viT", [(w_in[:, HI:HI + 512], viT, 0), (w_in[:, BV:BV + 256], viT, 512)],
                     [(K.hN, i * P, (i * P,)) for i in range(T // P)])
    stage_hgrn(K)
    stage_windows(K)
    with ExitStack() as mixed:
        K.rk_bonus, K.rk_gate = K.sb("rk_bonus", [P, 2, T], stack=mixed), K.sb("rk_gate", [P, 2, T], stack=mixed)
        stage_rwkv_prep(K)
        stage_rwkv(K)
        mixF = K.sb("mixF2", [P, KT, T], stack=mixed)
        stage_join(K, "join2", [(K.scratch["hgrn_o"], "hgrn_gnorm_g_2", K.scratch["hg"], 0)], mixF)
        stage_load_rows(K, "win_rows", K.scratch["win_o"], mixF, 4)
        stage_rwkv_out(K, mixF, 6)
        stage_gemm_f(K, "wout2", A["w_out_2"][0], D, mixF, T, None, residual=K.hF)


def stage_ffn_up(K, hN, actT):
    nc = K.nc
    up = K.A["ffn_up_2"][0]
    NJ = NFF // P
    with K.stage() as st:
        U = range(2)
        wt = [[K.sb(f"up_w{u}{g}", [P, KT, P], stack=st) for g in range(2)] for u in U]
        c = [[K.sb(f"up_conv{u}{g}", [P, T], stack=st) for g in range(2)] for u in U]
        pm = [[K.ps(f"up_ps{u}{g}", [P, 2, BANK], st) for g in range(2)] for u in U]
        s_w, s_mm, s_tap, s_vec, s_silu = ([K.sem(f"up_{n}{u}") for u in U] for n in ("w", "mm", "tap", "vec", "silu"))
        flat = lambda t: t.rearrange("p a t -> p (a t)")
        taps = lambda j, g, n: K.cols[:, bass.ds(j + (K.col_at["ffn_conv_w_2"] + n * 2 * NJ + g * NJ), 1)]
        bias = lambda j, g: K.cols[:, bass.ds(j + (K.col_at["ffn_conv_b_2"] + g * NJ), 1)]
        NV = 5
        with nc.Block() as block:
            @block.sync
            def _(sp):
                with sp.Fori(0, NJ // 2) as i:
                    for u in U:
                        sp.wait_ge(s_mm[u], i * 2)
                        for g in range(2):
                            sp.dma_start(wt[u][g][:], up[:, bass.ds(i * 2 * P + (u * P + g * NFF), P)].rearrange("(k p) n -> p k n", p=P)) \
                                .then_inc(s_w[u], 16)

            @block.tensor
            def _(pe):
                with pe.Fori(0, NJ // 2) as i:
                    for u in U:
                        pe.wait_ge(s_w[u], i * 32 + 32)
                        pe.wait_ge(s_vec[u], i * NV)
                        for g in range(2):
                            for h in range(2):
                                for k in range(KT):
                                    mm = pe.matmul(pm[u][g][:, h, :], wt[u][g][:, k, :], hN[:, k, h * BANK:(h + 1) * BANK],
                                                   start=k == 0, stop=k == KT - 1)
                            mm.then_inc(s_mm[u], 1)

            @block.scalar
            def _(act):
                with act.Fori(0, NJ // 2) as i:
                    for u in U:
                        j = i * 2 + u
                        act.wait_ge(s_vec[u], i * NV)
                        for g in range(2):
                            act.wait_ge(s_mm[u], i * 2 + g + 1)
                            act.activation(c[u][g][:], flat(pm[u][g][:]), ACT.Identity, bias=bias(j, g), scale=taps(j, g, 2)).then_inc(s_tap[u], 1)
                        act.wait_ge(s_vec[u], i * NV + 2)
                        act.activation(c[u][0][:], c[u][0][:], ACT.Silu).then_inc(s_silu[u], 1)

            @block.vector
            def _(dve):
                with dve.Fori(0, NJ // 2) as i:
                    for u in U:
                        j = i * 2 + u
                        step = Count(dve, s_vec[u], i * NV)
                        for g in range(2):
                            dve.wait_ge(s_tap[u], i * 2 + g + 1)
                            for n in (1, 2):
                                o, x = c[u][g][:, n:], flat(pm[u][g][:])[:, 0:T - n]
                                step(dve.scalar_tensor_tensor(o, x, taps(j, g, 2 - n), o, ALU.mult, ALU.add))
                        dve.wait_ge(s_silu[u], i + 1)
                        a = actT[:].rearrange("p k t -> p (k t)")[:, bass.ds(i * 2 * T + u * T, T)]
                        step.mark(dve.tensor_tensor(a, c[u][0][:], c[u][1][:], ALU.mult))
                        assert step.n == NV


def ffn(K):
    with ExitStack() as st:
        actT = K.sb("ffn_act", [P, NFF // P, T], stack=st)
        with ExitStack() as norm:
            hN = K.sb("hN4", [P, KT, T], stack=norm)
            stage_norm(K, "nf", K.hF, hN, T, K.cols[:, K.col_at["norm_ffn_g_2"]:K.col_at["norm_ffn_g_2"] + 8])
            stage_ffn_up(K, hN, actT)
        stage_gemm_f(K, "down", K.A["ffn_down_2"][0], D, actT, T, None, residual=K.hF, kt=NFF // P)


def stage_embed(K, hN):
    nc, A = K.nc, K.A
    NP = 2
    with K.stage() as st:
        U = range(2)
        p_in, pF = K.sb("ple_rows", [P, T // P, NP * P], stack=st), K.sb("ple_F", [P, NP, T], stack=st)
        wg, wp = ([K.sb(f"ple_{n}{u}", [P, k, P], stack=st) for u in U] for n, k in (("wg", KT), ("wp", NP)))
        g = [K.sb(f"ple_gate{u}", [P, T], stack=st) for u in U]
        pg, pp = ([K.ps(f"ple_{n}{u}", [P, 2, BANK], st) for u in U] for n in ("g", "p"))
        s_p, s_t, s_pc = (K.sem(f"ple_{n}") for n in ("in", "turned", "copied"))
        s_w, s_mm, s_sig, s_h = ([K.sem(f"ple_{n}{u}") for u in U] for n in ("w", "mm", "sigmoid", "added"))
        flat = lambda t: t.rearrange("p a t -> p (a t)")
        cols = lambda w, i, u: w[:, bass.ds(i * 2 * P + u * P, P)].rearrange("(k p) n -> p k n", p=P)
        with nc.Block() as block:
            @block.sync
            def _(sp):
                sp.dma_start(p_in[:], A["p_2"][0, 0].rearrange("(c t) f -> t c f", t=P)).then_inc(s_p, 16)
                with sp.Fori(0, KT // 2) as i:
                    for u in U:
                        sp.wait_ge(s_mm[u], i)
                        sp.dma_start(wg[u][:], cols(A["ple_gate_2"][0], i, u)).then_inc(s_w[u], 16)
                        sp.dma_start(wp[u][:], cols(A["ple_proj_2"][0], i, u)).then_inc(s_w[u], 16)

            @block.tensor
            def _(pe):
                pe.wait_ge(s_p, 16)
                for k in range(NP):
                    for c in range(T // P):
                        mm = pe.transpose(pp[k][:, c // 4, (c % 4) * P:(c % 4 + 1) * P], p_in[:, c, k * P:(k + 1) * P], K.c("ident"))
                    mm.then_inc(s_t, 1)
                pe.wait_ge(s_pc, NP)
                with pe.Fori(0, KT // 2) as i:
                    for u in U:
                        pe.wait_ge(s_w[u], i * 32 + 32)
                        pe.wait_ge(s_h[u], i * 2)
                        for h in range(2):
                            t = slice(h * BANK, (h + 1) * BANK)
                            for k in range(KT):
                                pe.matmul(pg[u][:, h, :], wg[u][:, k, :], hN[:, k, t], start=k == 0, stop=k == KT - 1)
                            for k in range(NP):
                                mm = pe.matmul(pp[u][:, h, :], wp[u][:, k, :], pF[:, k, t], start=k == 0, stop=k == NP - 1)
                        mm.then_inc(s_mm[u], 1)

            @block.scalar
            def _(act):
                with act.Fori(0, KT // 2) as i:
                    for u in U:
                        act.wait_ge(s_mm[u], i + 1)
                        act.wait_ge(s_h[u], i * 2)
                        act.activation(g[u][:], flat(pg[u][:]), ACT.Sigmoid).then_inc(s_sig[u], 1)

            @block.vector
            def _(dve):
                for k in range(NP):
                    dve.wait_ge(s_t, k + 1)
                    dve.tensor_copy(pF[:, k, :], flat(pp[k][:])).then_inc(s_pc, 1)
                with dve.Fori(0, KT // 2) as i:
                    for u in U:
                        dve.wait_ge(s_sig[u], i + 1)
                        step = Count(dve, s_h[u], i * 2)
                        step(dve.tensor_tensor(g[u][:], g[u][:], flat(pp[u][:]), ALU.mult))
                        h = flat(K.hF[:])[:, bass.ds(i * 2 * T + u * T, T)]
                        step.mark(dve.tensor_tensor(h, h, g[u][:], ALU.add))


def stage_turn_out(K, src):
    nc = K.nc
    NT = T // P
    with K.stage() as st:
        pt = [K.ps(f"out_ps{u}", [P, 2, BANK], st) for u in range(2)]
        ob = [K.sb(f"out_rows{u}", [P, D], stack=st) for u in range(2)]
        s_t, s_c, s_o = K.sem("out_turned"), K.sem("out_copied"), [K.sem(f"out_stored{u}") for u in range(2)]
        with nc.Block() as block:
            @block.tensor
            def _(pe):
                for n in range(NT):
                    if n >= 2:
                        pe.wait_ge(s_c, n - 1)
                    for k in range(KT):
                        mm = pe.transpose(pt[n % 2][:, k // 4, (k % 4) * P:(k % 4 + 1) * P], src[:, k, n * P:(n + 1) * P], K.c("ident"))
                    mm.then_inc(s_t, 1)

            @block.vector
            def _(dve):
                for n in range(NT):
                    dve.wait_ge(s_t, n + 1)
                    if n >= 2:
                        dve.wait_ge(s_o[n % 2], n // 2 * 16)
                    dve.tensor_copy(ob[n % 2][:], pt[n % 2][:].rearrange("p a t -> p (a t)")).then_inc(s_c, 1)

            @block.sync
            def _(sp):
                for n in range(NT):
                    sp.wait_ge(s_c, n + 1)
                    sp.dma_start(K.out[0, n * P:(n + 1) * P, :], ob[n % 2][:]).then_inc(s_o[n % 2], 16)
                for u in range(2):
                    sp.wait_ge(s_o[u], NT // 2 * 16)


def tail(K):
    gain = lambda name: K.cols[:, K.col_at[name]:K.col_at[name] + 8]
    with ExitStack() as st:
        hN = K.sb("hN5", [P, KT, T], stack=st)
        stage_norm(K, "np", K.hF, hN, T, gain("norm_ple_g_2"))
        stage_embed(K, hN)
        stage_norm(K, "no", K.hF, hN, T, gain("final_norm_g_2"))
        stage_turn_out(K, hN)


def program(nc, A, const_at, const, wide, out):
    with ExitStack() as stack:
        K = Core(nc, A, const_at, const, wide, out, stack)
        K.hF = K.sb("hF", [P, KT, T])
        stage_setup(K)
        mixer_one(K)
        moe(K)
        mixer_two(K)
        ffn(K)
        tail(K)


def kernel(**inputs):
    import concourse.bacc as bacc
    from concourse.bass_utils import run_bass_kernel_spmd

    nc = bacc.Bacc("TRN2", target_bir_lowering=False, num_devices=1)
    at, const, wide = constants()
    arrays, A = {}, {}
    for name, a in inputs.items():
        a = np.ascontiguousarray(a)
        if a.size:
            arrays[f"in_{name}"] = a
            A[name] = nc.dram_tensor(f"in_{name}", a.shape, mybir.dt.from_np(a.dtype), kind="ExternalInput").ap()
    tables = []
    for name, a in (("masks", const), ("window_masks", wide)):
        arrays[name] = a
        tables.append(nc.dram_tensor(name, a.shape, F32, kind="ExternalInput").ap())
    out = nc.dram_tensor("out", (1, T, D), F32, kind="ExternalOutput").ap()
    program(nc, A, at, *tables, out)
    return run_bass_kernel_spmd(nc, [arrays], core_ids=[0]).results[0]["out"]
```

```python
from contextlib import ExitStack, contextmanager

import numpy as np

import concourse.bass as bass
from concourse import mybir

F32 = mybir.dt.float32
I32 = mybir.dt.int32
F32R = mybir.dt.float32r
ALU = mybir.AluOpType
ACT = mybir.ActivationFunctionType
AX = mybir.AxisListType

P = 128
D = 1024
KT = D // P
T = 1024
NCTX = 256
TALL = NCTX + T
TSCAN = TALL + NCTX
NCH = TALL // P
BANK = 512
EPS = 1e-6
RK_GN_EPS = 64e-5

GQ, GK, GV, GG, GLR, MQK, MV, MO, MI, MF = 0, 256, 512, 1024, 1536, 1568, 2592, 3104, 3616, 3624
NE, EPG, NG, DE = 32, 8, 4, 512
BR = 64
NBLK = 2 * T // BR + NE
NSORT = (NBLK + 2) * BR
NFF = 2816


def constants():
    s, t = np.arange(P)[:, None], np.arange(P)[None, :]
    one = lambda m: m.astype(np.float32)
    mid = one(s < 64)
    parts = {
        "ident": one(s == t), "ones": np.ones((P, P), np.float32),
        "tri0": one(s <= t), "tri1": one(s >= t),
        "mid0": one(s <= t) - mid, "mid1": one(s >= t) - one(s >= 64),
        "after0": one(s > t), "after1": one(s < t),
        "neg0": -1e30 * one(s > t), "neg1": -1e30 * one(s < t),
        "selrow": one(np.arange(4 * P)[None, :] // P == s),
        "mean1024": np.full((P, P), 1.0 / 1024, np.float32),
        "mean128": np.full((P, P), 1.0 / 128, np.float32),
        "mean64": one(s // 64 == t // 64) / 64, "ones64": one(s // 64 == t // 64),
        "lt_half": one((s // 64 == t // 64) & (s < t)), "le_half": one((s // 64 == t // 64) & (s <= t)),
        "halves": one(np.arange(P)[:, None] // 64 == np.arange(2)[None, :]),
        "lt64": one((s < t) & (t < 64)), "le64": one((s <= t) & (t < 64)),
        "before": one(s < t), "iota": np.broadcast_to(np.arange(64, dtype=np.float32), (P, 64)),
    }
    for lv in (8, 16, 32, 64):
        parts[f"level{lv}"] = one((s // (2 * lv) == t // (2 * lv)) & (s % (2 * lv) < lv) & (t % (2 * lv) >= lv))
    for lv in (1, 2, 4, 8, 16, 32):
        parts[f"pair{lv}"] = one((s // (2 * lv) == t // (2 * lv)) & (s % (2 * lv) < lv) & (t % (2 * lv) >= lv))
        parts[f"pairT{lv}"] = parts[f"pair{lv}"].T
    q, k = np.arange(P)[:, None], np.arange(T)[None, :]
    dist = q + T - P - k
    mult = one((dist >= 0) & (dist <= 128)) + one((dist >= 0) & (dist % 4 == 0) & (dist <= 512)) \
        + one((dist >= 0) & (dist % 16 == 0) & (dist <= 2048))
    wide = {"mult": mult, "multneg": np.where(mult > 0, 0, -1e30)}

    def pack(parts):
        at, n = {}, 0
        for name, a in parts.items():
            at[name] = (n, a.shape[1])
            n += a.shape[1]
        return at, np.ascontiguousarray(np.concatenate(list(parts.values()), 1).astype(np.float32))
    at, const = pack(parts)
    return at, const, pack(wide)[1]


class Count:

    def __init__(self, eng, sem, base=0, n=0):
        self.eng, self.sem, self.base, self.n = eng, sem, base, n

    def __call__(self, ins):
        self.n += 1
        ins.then_inc(self.sem, 1)
        self.eng.wait_ge(self.sem, self.base + self.n)

    def mark(self, ins):
        self.n += 1
        ins.then_inc(self.sem, 1)


class Core:

    def __init__(self, nc, A, const_at, const, wide, out, stack):
        self.nc, self.A, self.out, self.stack = nc, A, out, stack
        self.const_at, self.const_dram, self.wide_dram = const_at, const, wide
        self.scratch = {}
        self.nsem = 0

    def sb(self, name, shape, dt=F32, stack=None):
        return (stack or self.stack).enter_context(self.nc.sbuf_tensor(name, shape, dt))

    def ps(self, name, shape, stack, dt=F32):
        return stack.enter_context(self.nc.psum_tensor(name + "_psum", shape, dt))

    @contextmanager
    def stage(self):
        with ExitStack() as st:
            self.held = []
            yield st
            self.nc.clear_and_free_semaphores(self.held)
            self.nc.all_engine_barrier()

    def sem(self, name):
        self.held.append(self.nc.alloc_semaphore(name))
        return self.held[-1]

    def dram(self, name, shape, dt=F32):
        self.scratch[name] = self.nc.dram_tensor(name, shape, dt, kind="Internal").ap()
        return self.scratch[name]

    def c(self, name):
        o, n = self.const_at[name]
        return self.const[:, o:o + n]

    def col(self, name, j=0):
        return self.cols[:, self.col_at[name] + j:self.col_at[name] + j + 1]


VECS = [("norm1_g", 8), ("gla_norm_g", 4), ("ml_norm_g", 4), ("ml_conv_b", 8), ("norm2_g", 8),
        ("final_norm_g", 8), ("norm_mix_g_2", 8), ("norm_ffn_g_2", 8), ("norm_ple_g_2", 8),
        ("final_norm_g_2", 8), ("hgrn_gnorm_g_2", 4), ("hgrn_lower_bounds_2", 4), ("rwkv_mu_2", 8),
        ("ml_conv_w", 72), ("ffn_conv_w_2", 132), ("ffn_conv_b_2", 44),
        ("rwkv_w0_2", 2), ("rwkv_a0_2", 2), ("rwkv_k_k_2", 2), ("rwkv_k_a_2", 2), ("rwkv_r_k_2", 2),
        ("rwkv_ln_w_2", 2), ("rwkv_ln_b_2", 2)]


def flat_rows(ap, w):
    while len(ap.shape) > 1:
        names = " ".join("abcdef"[:len(ap.shape)])
        ap = ap.rearrange(f"{names} -> ({names})")
    return ap.rearrange("(r w) -> r w", w=w)


def stage_setup(K):
    nc, A = K.nc, K.A
    nconst = K.const_dram.shape[1]
    K.const = K.sb("const", [P, nconst])
    total = sum(n for _, n in VECS)
    ntile = -(-total // P)
    K.cols = K.sb("cols", [P, ntile * P])
    K.modcols = K.sb("modcols", [P, 64])
    K.col_at, at = {}, 0
    for name, n in VECS:
        K.col_at[name] = at
        at += n
    mod = K.dram("mod", [2, 6 * D])
    with K.stage() as st:
        rows = [K.sb(f"vec_rows{i}", [P, P], stack=st) for i in range(ntile)]
        mrows = K.sb("mod_rows", [64, P], stack=st)
        crow = K.sb("cond_rows", [16, P], stack=st)
        csil = K.sb("cond_silu", [P, 8, 2], stack=st)
        brow = K.sb("ada_bias", [2, 6 * D], stack=st)
        mout = K.sb("mod_out", [2, 6 * D], stack=st)
        NW = 3
        aw = [K.sb(f"ada_w{i}", [P, 8, 512], stack=st) for i in range(NW)]
        pt = K.ps("vec_ps", [P, ntile * P], st)
        pm = [K.ps(f"mod_ps{i}", [2, 512], st) for i in range(2)]
        s_const, s_rows, s_cond, s_bias = (K.sem(f"setup_{x}") for x in ("const", "rows", "cond", "bias"))
        s_aw = [K.sem(f"setup_ada{i}") for i in range(NW)]
        s_mm, s_ev, s_t, s_tc, s_zero, s_mod, s_modrows, s_sil = (
            K.sem(f"setup_{x}") for x in ("mod_mm", "mod_ev", "turned", "copied", "zero", "mod_out", "mod_rows", "silu"))
        pieces = []
        for name, n in VECS:
            src, r = flat_rows(A[name], P), 0
            while r < n:
                g = K.col_at[name] + r
                k = min(n - r, P - g % P)
                pieces.append((g // P, g % P, k, src[r:r + k, :]))
                r += k
        last = total % P
        with nc.Block() as block:
            @block.sync
            def _(sp):
                sp.dma_start(K.const[:], K.const_dram).then_inc(s_const, 16)
                sp.dma_start(crow[0:8, :], flat_rows(A["c"], P)).then_inc(s_cond, 16)
                sp.dma_start(crow[8:16, :], flat_rows(A["c_ctx"], P)).then_inc(s_cond, 16)
                for r in range(2):
                    sp.dma_start(brow[r:r + 1, :], A["ada_b"]).then_inc(s_bias, 16)
                for n in range(12):
                    if n >= NW:
                        sp.wait_ge(s_mm, n - NW + 1)
                    sp.dma_start(aw[n % NW][:], A["ada_w"][0, :, n * 512:(n + 1) * 512].rearrange("(k p) n -> p k n", p=P)) \
                        .then_inc(s_aw[n % NW], 16)
                sp.wait_ge(s_ev, 12)
                sp.dma_start(mod, mout[:]).then_inc(s_mod, 16)
                sp.wait_ge(s_mod, 16)
                sp.dma_start(mrows[0:48, :], flat_rows(mod[0:1, :], P)).then_inc(s_modrows, 16)
                sp.dma_start(mrows[48:64, :], flat_rows(mod[1:2, 0:2 * D], P)).then_inc(s_modrows, 16)

            @block.gpsimd
            def _(pool):
                if last:
                    nc.gpsimd.memset(rows[-1][:], 0.0).then_inc(s_zero, 1)
                    pool.wait_ge(s_zero, 1)
                for i, r, k, src in pieces:
                    pool.dma_start(rows[i][r:r + k, :], src).then_inc(s_rows, 16)

            @block.scalar
            def _(act):
                act.wait_ge(s_t, 1)
                act.activation(csil[:].rearrange("p k r -> p r k"), pt[:, 0:16].rearrange("p (r k) -> p r k", r=2),
                               ACT.Silu).then_inc(s_sil, 1)

            @block.tensor
            def _(pe):
                pe.wait_ge(s_const, 16)
                pe.wait_ge(s_cond, 32)
                pe.transpose(pt[:, 0:16], crow[:], K.c("ident")[0:16, 0:16]).then_inc(s_t, 1)
                pe.wait_ge(s_sil, 1)
                for n in range(12):
                    pe.wait_ge(s_aw[n % NW], 16 * (n // NW + 1))
                    if n >= 2:
                        pe.wait_ge(s_ev, n - 1)
                    for k in range(8):
                        mm = pe.matmul(pm[n % 2][:], csil[:, k, :], aw[n % NW][:, k, :], start=k == 0, stop=k == 7)
                    mm.then_inc(s_mm, 1)
                pe.wait_ge(s_rows, 16 * len(pieces))
                for i in range(ntile):
                    mm = pe.transpose(pt[:, i * P:(i + 1) * P], rows[i][:], K.c("ident"))
                mm.then_inc(s_t, 1)
                pe.wait_ge(s_tc, 1)
                pe.wait_ge(s_modrows, 32)
                pe.transpose(pt[:, 0:64], mrows[:], K.c("ident")[0:64, 0:64]).then_inc(s_t, 1)

            @block.vector
            def _(dve):
                dve.wait_ge(s_bias, 32)
                for n in range(12):
                    dve.wait_ge(s_mm, n + 1)
                    dve.tensor_tensor(mout[:, n * 512:(n + 1) * 512], pm[n % 2][:], brow[:, n * 512:(n + 1) * 512],
                                      ALU.add).then_inc(s_ev, 1)
                dve.wait_ge(s_t, 2)
                dve.tensor_copy(K.cols[:], pt[:]).then_inc(s_tc, 1)
                dve.wait_ge(s_t, 3)
                dve.tensor_copy(K.modcols[:], pt[:, 0:64]).then_inc(s_tc, 1)
                dve.wait_ge(s_tc, 2)
                for o in (8, 32, 56):
                    dve.tensor_scalar(K.modcols[:, o:o + 8], K.modcols[:, o:o + 8], 1.0, None, ALU.add)


def stage_turn_in(K):
    nc, A = K.nc, K.A
    ctxF = K.ctxF
    with K.stage() as st:
        xin = [K.sb(f"x_rows{i}", [P, D], stack=st) for i in range(4)]
        pt = [K.ps(f"turn_ps{i}", [P, 2, 512], st) for i in range(3)]
        s_x = [K.sem(f"turn_x{i}") for i in range(4)]
        s_t, s_c = K.sem("turn_done"), K.sem("turn_copied")
        tiles = [("c", i) for i in range(NCTX // P)] + [("x", i) for i in range(T // P)]
        with nc.Block() as block:
            @block.sync
            def _(sp):
                for n, (w, i) in enumerate(tiles):
                    if n >= 4:
                        sp.wait_ge(s_t, n - 3)
                    src = A["x" if w == "x" else "ctx"][0, i * P:(i + 1) * P, :]
                    sp.dma_start(xin[n % 4][:], src).then_inc(s_x[n % 4], 16)

            @block.tensor
            def _(pe):
                for n in range(len(tiles)):
                    pe.wait_ge(s_x[n % 4], 16 * (n // 4 + 1))
                    if n >= 3:
                        pe.wait_ge(s_c, n - 2)
                    for k in range(8):
                        mm = pe.transpose(pt[n % 3][:, k // 4, (k % 4) * P:(k % 4 + 1) * P],
                                          xin[n % 4][:, k * P:(k + 1) * P], K.c("ident"))
                    mm.then_inc(s_t, 1)

            @block.vector
            def _(dve):
                for n, (w, i) in enumerate(tiles):
                    dve.wait_ge(s_t, n + 1)
                    dst = (K.hF if w == "x" else ctxF)[:, :, i * P:(i + 1) * P]
                    dve.tensor_copy(dst, pt[n % 3][:].rearrange("p a (b t) -> p (a b) t", b=4)).then_inc(s_c, 1)


def split(dve, x, hi, lo, s_hi, n):
    dve.tensor_copy(hi.bitcast(F32R), x).then_inc(s_hi, 1)
    dve.wait_ge(s_hi, n)
    return dve.tensor_tensor(lo.bitcast(F32R), x, hi, ALU.subtract)


def matmul3(pe, out, w, x, start, stop):
    r = lambda ap: ap.bitcast(F32R)
    pe.matmul(out, r(w[0]), r(x[0]), start=start, stop=False)
    pe.matmul(out, r(w[0]), r(x[1]), start=False, stop=False)
    return pe.matmul(out, r(w[1]), r(x[0]), start=False, stop=stop)


def stage_norm(K, name, src, dst, ntok, gain, shift=None, scale=None):
    W = min(512, ntok)
    parts = isinstance(dst, tuple)
    with K.stage() as st:
        NB = 4
        sq = [K.sb(f"{name}_sq{i}", [P, W], stack=st) for i in range(NB)]
        tmp = [K.sb(f"{name}_tmp{i}", [P, W], stack=st) for i in range(NB)] if parts else None
        rstd = [K.sb(f"{name}_rstd{i}", [P, W], stack=st) for i in range(2)]
        gm = K.sb(f"{name}_gain", [P, 8], stack=st)
        pm = [K.ps(f"{name}_ps{i}", [P, W], st) for i in range(2)]
        s_sq, s_used, s_v, s_rt, s_n, s_g, s_out, s_hi = (
            K.sem(f"{name}_{x}") for x in ("sq", "sq_used", "var", "root", "normed", "gain", "out", "hi"))
        nh = ntok // W
        at = lambda t, h, k: t[:, k, h * W:(h + 1) * W]
        to = lambda h, k: tmp[k % NB][:] if parts else at(dst, h, k)
        with K.nc.Block() as block:
            @block.scalar
            def _(act):
                for h in range(nh):
                    for k in range(8):
                        n = 8 * h + k
                        if n >= NB:
                            act.wait_ge(s_used, n - NB + 1)
                        act.activation(sq[n % NB][:], at(src, h, k), ACT.Square).then_inc(s_sq, 1)
                for h in range(nh):
                    act.wait_ge(s_v, h + 1)
                    act.activation(rstd[h][:], rstd[h][:], ACT.Sqrt).then_inc(s_rt, 1)
                    if shift is not None:
                        act.wait_ge(s_g, 1)
                        for k in range(8):
                            act.wait_ge(s_n, 8 * h + k + 1)
                            act.activation(to(h, k), to(h, k), ACT.Identity, bias=shift[:, k:k + 1], scale=gm[:, k:k + 1]).then_inc(s_out, 1)

            @block.tensor
            def _(pe):
                for h in range(nh):
                    for k in range(8):
                        pe.wait_ge(s_sq, 8 * h + k + 1)
                        mm = pe.matmul(pm[h][:], K.c("mean1024"), sq[(8 * h + k) % NB][:], start=k == 0, stop=k == 7)
                        mm.then_inc(s_used, 1)

            @block.vector
            def _(dve):
                def cut(h, k):
                    n = 8 * h + k + 1
                    dve.wait_ge(s_out if shift is not None else s_n, n)
                    split(dve, to(h, k), at(dst[0], h, k), at(dst[1], h, k), s_hi, n)
                if shift is not None:
                    dve.tensor_tensor(gm[:], gain, scale, ALU.mult).then_inc(s_g, 1)
                for h in range(nh):
                    dve.wait_ge(s_used, 8 * h + 8)
                    dve.tensor_scalar(rstd[h][:], pm[h][:], EPS, None, ALU.add).then_inc(s_v, 1)
                for h in range(nh):
                    dve.wait_ge(s_rt, h + 1)
                    dve.reciprocal(rstd[h][:], rstd[h][:]).then_inc(s_v, 1)
                    dve.wait_ge(s_v, nh + h + 1)
                    for k in range(8):
                        if shift is not None:
                            dve.tensor_tensor(to(h, k), at(src, h, k), rstd[h][:], ALU.mult).then_inc(s_n, 1)
                        else:
                            dve.scalar_tensor_tensor(to(h, k), at(src, h, k), gain[:, k:k + 1], rstd[h][:], ALU.mult, ALU.mult).then_inc(s_n, 1)
                        if parts and k:
                            cut(h, k - 1)
                    if parts:
                        cut(h, 7)


def stage_gemm_f(K, name, groups, src, ntok, whole=None, residual=None, gcol=None, ctx=None):
    npair = sum(g[1] for g in groups) // (2 * P)
    NT = ntok // BANK
    with K.stage() as st:
        U = range(2)
        wt, wh, wl = ([K.sb(f"{name}_{x}{u}", [P, KT, P], stack=st) for u in U] for x in ("w", "wh", "wl"))
        nps = NT + (1 if ctx is not None else 0)
        pm = [K.ps(f"{name}_ps{u}", [P, nps, BANK], st) for u in U]
        ob = [K.sb(f"{name}_out{u}", [P, nps * BANK], stack=st) for u in U] if residual is None else None
        s_src, s_srch = K.sem(f"{name}_src"), K.sem(f"{name}_srch")
        s_w, s_wh, s_wl, s_o, s_mm, s_ev = ([K.sem(f"{name}_{x}{u}") for u in U] for x in ("w", "wh", "wl", "o", "mm", "ev"))
        with K.nc.Block() as block:
            @block.sync
            def _(sp):
                base = 0
                for w, ncol, _, _, _ in groups:
                    with sp.Fori(0, ncol // (2 * P)) as i:
                        for u in U:
                            sp.wait_ge(s_wl[u], i + base)
                            sp.dma_start(wt[u][:], w[:, bass.ds(i * 2 * P + u * P, P)].rearrange("(k p) n -> p k n", p=P)) \
                                .then_inc(s_w[u], 16)
                    base += ncol // (2 * P)

            @block.vector
            def _(dve):
                flat = residual[:].rearrange("p k t -> p (k t)") if residual is not None else None

                def weights(u, n):
                    dve.wait_ge(s_w[u], n * 16 + 16)
                    split(dve, wt[u][:], wh[u][:], wl[u][:], s_wh[u], n + 1).then_inc(s_wl[u], 1)

                def added(u, i):
                    dve.wait_ge(s_mm[u], i + 1)
                    h = flat[:, bass.ds(i * 2 * ntok + u * ntok, ntok)]
                    x = pm[u][:].rearrange("p a b -> p (a b)")
                    if gcol is None:
                        dve.tensor_tensor(h, x, h, ALU.add).then_inc(s_ev[u], 1)
                    else:
                        dve.scalar_tensor_tensor(h, x, gcol[:, bass.ds(i * 2 + u, 1)], h, ALU.mult, ALU.add).then_inc(s_ev[u], 1)
                weights(0, 0)
                if whole is not None:
                    for k in range(KT):
                        split(dve, whole[:, k, :], src[0][:, k, :], src[1][:, k, :], s_srch, k + 1).then_inc(s_src, 1)
                weights(1, 0)
                with dve.Fori(0, npair - 1) as i:
                    for u in U:
                        if residual is not None:
                            added(u, i)
                        dve.wait_ge(s_mm[u], i + 1)
                        weights(u, i + 1)
                if residual is not None:
                    for u in U:
                        added(u, npair - 1)

            @block.tensor
            def _(pe):
                with pe.Fori(0, npair) as i:
                    for u in U:
                        pe.wait_ge(s_wl[u], i + 1)
                        pe.wait_ge(s_ev[u], i)
                        for k in range(KT):
                            if whole is not None:
                                pe.wait_ge(s_src, k + 1)
                            for h in range(NT):
                                t = slice(h * BANK, (h + 1) * BANK)
                                mm = matmul3(pe, pm[u][:, h, :], (wh[u][:, k, :], wl[u][:, k, :]), (src[0][:, k, t], src[1][:, k, t]),
                                             start=k == 0, stop=k == KT - 1)
                        if ctx is not None:
                            for k in range(KT):
                                mm = matmul3(pe, pm[u][:, NT, 0:NCTX], (wh[u][:, k, :], wl[u][:, k, :]), (ctx[0][:, k, :], ctx[1][:, k, :]),
                                             start=k == 0, stop=k == KT - 1)
                        mm.then_inc(s_mm[u], 1)

            if residual is None:
                @block.scalar
                def _(act):
                    base, stored = 0, 0
                    for w, ncol, dst, func, scale in groups:
                        scan = dst.shape[1] == TSCAN
                        n, ndma = (T + NCTX, 3) if scan else (ntok, 1)
                        with act.Fori(0, ncol // (2 * P)) as i:
                            for u in U:
                                act.wait_ge(s_mm[u], i + (base + 1))
                                act.wait_ge(s_o[u], i * (16 * ndma) + stored)
                                act.activation(ob[u][:, 0:n], pm[u][:].rearrange("p a b -> p (a b)")[:, 0:n], func, scale=scale) \
                                    .then_inc(s_ev[u], 1)
                                act.wait_ge(s_ev[u], i + (base + 1))
                                rows = bass.ds(i * 2 * P + u * P, P)
                                if scan:
                                    act.dma_start(dst[rows, NCTX:NCTX + T], ob[u][:, 0:T]).then_inc(s_o[u], 16)
                                    act.dma_start(dst[rows, 0:NCTX], ob[u][:, T:n]).then_inc(s_o[u], 16)
                                    act.dma_start(dst[rows, NCTX + T:TSCAN], ob[u][:, T:n]).then_inc(s_o[u], 16)
                                else:
                                    act.dma_start(dst[rows, :], ob[u][:, 0:n]).then_inc(s_o[u], 16)
                        base += ncol // (2 * P)
                        stored += ncol // (2 * P) * 16 * ndma
                    for u in U:
                        act.wait_ge(s_o[u], stored)


def stage_gemm_t(K, name, groups, toks, bufs=2):
    NB = 4
    with K.stage() as st:
        wt = K.sb(f"{name}_w", [P, KT, BANK], stack=st)
        wh, wl = ([K.sb(f"{name}_{x}{u}", [P, KT, BANK], stack=st) for u in range(bufs)] for x in ("wh", "wl"))
        pm = [K.ps(f"{name}_ps{i}", [P, BANK], st) for i in range(NB)]
        ob = [K.sb(f"{name}_out{i}", [P, BANK], stack=st) for i in range(NB)]
        s_o = [K.sem(f"{name}_o{i}") for i in range(NB)]
        s_w, s_wh, s_wl, s_mm, s_ev = (K.sem(f"{name}_{x}") for x in ("w", "wh", "wl", "mm", "ev"))
        nt = len(toks)
        stored = [0] * NB
        with K.nc.Block() as block:
            @block.sync
            def _(sp):
                for g, (w, dst, c0) in enumerate(groups):
                    n = w.shape[1]
                    sp.wait_ge(s_wl, KT * g)
                    for k in range(KT):
                        sp.dma_start(wt[:, k, 0:n], w[k * P:(k + 1) * P, :]).then_inc(s_w, 16)

            @block.vector
            def _(dve):
                for g, (w, dst, c0) in enumerate(groups):
                    n = w.shape[1]
                    if g >= bufs:
                        dve.wait_ge(s_mm, nt * (g - bufs + 1))
                    dve.wait_ge(s_w, 16 * KT * (g + 1))
                    for k in range(KT):
                        split(dve, wt[:, k, 0:n], wh[g % bufs][:, k, 0:n], wl[g % bufs][:, k, 0:n], s_wh, g * KT + k + 1).then_inc(s_wl, 1)

            @block.tensor
            def _(pe):
                for g, (w, dst, c0) in enumerate(groups):
                    n = w.shape[1]
                    for i, (src, t0, _) in enumerate(toks):
                        m = g * nt + i
                        if m >= NB:
                            pe.wait_ge(s_ev, m - NB + 1)
                        t = slice(t0, t0 + P)
                        for k in range(KT):
                            if i == 0:
                                pe.wait_ge(s_wl, g * KT + k + 1)
                            mm = matmul3(pe, pm[m % NB][:, 0:n], (src[0][:, k, t], src[1][:, k, t]),
                                         (wh[g % bufs][:, k, 0:n], wl[g % bufs][:, k, 0:n]), start=k == 0, stop=k == KT - 1)
                        mm.then_inc(s_mm, 1)

            @block.scalar
            def _(act):
                for g, (w, dst, c0) in enumerate(groups):
                    n = w.shape[1]
                    for i, (_, _, rows) in enumerate(toks):
                        m = g * nt + i
                        b = m % NB
                        act.wait_ge(s_mm, m + 1)
                        if stored[b]:
                            act.wait_ge(s_o[b], stored[b])
                        act.activation(ob[b][:, 0:n], pm[b][:, 0:n], ACT.Copy).then_inc(s_ev, 1)
                        act.wait_ge(s_ev, m + 1)
                        for r in rows:
                            act.dma_start(dst[r:r + P, c0:c0 + n], ob[b][:, 0:n]).then_inc(s_o[b], 16)
                            stored[b] += 16
                for b in range(NB):
                    act.wait_ge(s_o[b], stored[b])


def stage_misc(K):
    nc, A = K.nc, K.A
    misc = K.dram("miscF", [P, TALL])
    with K.stage() as st:
        wm, wh, wl = (K.sb(f"misc_{x}", [P, KT, P], stack=st) for x in ("w", "wh", "wl"))
        ob = K.sb("misc_out", [P, TALL], stack=st)
        pm = K.ps("misc_ps", [P, 3, BANK], st)
        s_z, s_w, s_wh, s_wl, s_mm, s_cp, s_st = (K.sem(f"misc_{x}") for x in ("zero", "w", "w_hi", "w_lo", "mm", "copied", "stored"))
        with nc.Block() as block:
            @block.gpsimd
            def _(pool):
                pool.memset(wm[:], 0.0).then_inc(s_z, 1)

            @block.sync
            def _(sp):
                sp.wait_ge(s_z, 1)
                w = A["w_in"][0].rearrange("(k p) n -> p k n", p=P)
                for o, c, n in ((0, GLR, 16), (32, GLR + 16, 16), (64, MI, 8), (96, MF, 8)):
                    sp.dma_start(wm[:, :, o:o + n], w[:, :, c:c + n]).then_inc(s_w, 16)
                sp.wait_ge(s_cp, 2)
                sp.dma_start(misc, ob[:]).then_inc(s_st, 16)
                sp.wait_ge(s_st, 16)

            @block.tensor
            def _(pe):
                pe.wait_ge(s_wl, 1)
                for h in range(3):
                    for k in range(KT):
                        t = slice(0, NCTX) if h == 2 else slice(h * BANK, (h + 1) * BANK)
                        x = [s[:, k, t] for s in (K.ctx if h == 2 else K.x)]
                        mm = matmul3(pe, pm[:, h, 0:x[0].shape[1]], (wh[:, k, :], wl[:, k, :]), x, start=k == 0, stop=k == KT - 1)
                mm.then_inc(s_mm, 1)

            @block.vector
            def _(dve):
                dve.wait_ge(s_w, 64)
                split(dve, wm[:], wh[:], wl[:], s_wh, 1).then_inc(s_wl, 1)
                dve.wait_ge(s_mm, 1)
                flat = pm[:].rearrange("p a b -> p (a b)")
                dve.tensor_copy(ob[:, NCTX:TALL], flat[:, 0:T]).then_inc(s_cp, 1)
                dve.tensor_copy(ob[:, 0:NCTX], flat[:, T:TALL]).then_inc(s_cp, 1)


def stage_gates(K):
    nc, A = K.nc, K.A
    misc = K.scratch["miscF"]
    la_dram = K.dram("laT", [TSCAN, 512])
    K.rows5 = [K.sb(f"ml_rows{d}", [4, NCH, 5, P], stack=K.mixstack) for d in range(2)]
    K.kwcol = [K.sb(f"ml_kwcol{d}", [P, NCH, 4], stack=K.mixstack) for d in range(2)]
    U_, W_, M_, C_, G_ = range(5)
    with K.stage() as st:
        glr = [K.sb(f"glr{d}", [16, TALL], stack=st) for d in range(2)]
        upw = [K.sb(f"gla_up{d}", [16, 256], stack=st) for d in range(2)]
        upb = K.sb("gla_up_b", [P, 512], stack=st)
        gate = [[K.sb(f"gate{n}_{d}", [4, TALL], stack=st) for d in range(2)] for n in range(2)]
        bias = [[K.sb(f"gbias{n}_{d}", [4, 1], stack=st) for d in range(2)] for n in range(2)]
        reset = K.sb("reset", [4, TALL], stack=st)
        tmp = [K.sb(f"gtmp{d}", [4, TALL], stack=st) for d in range(2)]
        acum = tmp
        mrun = [K.sb(f"mrun{d}", [4, TALL], stack=st) for d in range(2)]
        mprev = [K.sb(f"mprev{d}", [4, NCH], stack=st) for d in range(2)]
        lx = K.sb("gla_logit", [P, NCH, 512], stack=st)
        le = K.sb("gla_exp", [P, NCH, 512], stack=st)
        pl = [K.ps(f"logit_ps{i}", [P, 512], st) for i in range(2)]
        pg = K.ps("kwcol_ps", [P, 2, NCH, 4], st)
        s_z, s_8, s_in, s_lg, s_lb, s_a, s_la, s_g, s_ge, s_row, s_col, s_st = (
            K.sem(f"gates_{x}") for x in ("zero", "rows", "in", "logits", "biased", "act",
                                          "logsig", "row", "rowact", "rowdone", "col", "stored"))
        with nc.Block() as block:
            @block.gpsimd
            def _(pool):
                pool.memset(reset[:], 1.0).then_inc(s_z, 1)
                pool.wait_ge(s_z, 1)
                pool.memset(reset[:].rearrange("r (c t) -> r c t", t=P)[:, :, 0:1], 0.0).then_inc(s_z, 1)

            @block.sync
            def _(sp):
                for d in range(2):
                    sp.dma_start(upw[d][:], A["gla_up_w"][0, d]).then_inc(s_in, 16)
                    sp.dma_start(upb[:, d * 256:(d + 1) * 256], A["gla_up_b"][0, d].partition_broadcast(P)).then_inc(s_in, 16)
                    sp.dma_start(bias[0][d][:], A["ml_i_b"][0, d].rearrange("(h a) -> h a", a=1)).then_inc(s_in, 16)
                    sp.dma_start(bias[1][d][:], A["ml_f_b"][0, d].rearrange("(h a) -> h a", a=1)).then_inc(s_in, 16)
                for d in range(2):
                    sp.dma_start(glr[d][:], misc[32 * d:32 * d + 16, :]).then_inc(s_in, 16)
                    for n in range(2):
                        r = misc[64 + 32 * n + 4 * d:64 + 32 * n + 4 * d + 4, :]
                        if d == 0:
                            sp.dma_start(gate[n][d][:], r).then_inc(s_8, 16)
                        else:
                            sp.dma_start(gate[n][d][:, 0:T], r[:, NCTX:TALL]).then_inc(s_8, 16)
                            sp.dma_start(gate[n][d][:, T:TALL], r[:, 0:NCTX]).then_inc(s_8, 16)
                sp.wait_ge(s_la, 1)
                tok = lambda ap: ap.rearrange("(c p) n -> p c n", p=P)
                sp.dma_start(tok(la_dram[0:TALL, :]), lx[:]).then_inc(s_st, 16)
                sp.dma_start(tok(la_dram[TALL:TSCAN, :]), lx[:, 0:2, :]).then_inc(s_st, 16)
                sp.wait_ge(s_st, 32)

            @block.tensor
            def _(pe):
                pe.wait_ge(s_in, 160)
                for n in range(NCH):
                    if n >= 2:
                        pe.wait_ge(s_lb, n - 1)
                    for d in range(2):
                        mm = pe.matmul(pl[n % 2][:, d * 256:(d + 1) * 256], glr[d][:, n * P:(n + 1) * P], upw[d][:],
                                       start=True, stop=True)
                    mm.then_inc(s_lg, 1)
                pe.wait_ge(s_row, 2)
                for d in range(2):
                    for n in range(NCH):
                        mm = pe.transpose(pg[:, d, n, :], K.rows5[d][:, n, G_, :], K.c("ident")[0:4, 0:4])
                mm.then_inc(s_col, 1)

            @block.vector
            def _(dve):
                dve.wait_ge(s_in, 160)
                for n in range(NCH):
                    dve.wait_ge(s_lg, n + 1)
                    dve.tensor_tensor(lx[:, n, :], pl[n % 2][:], upb[:], ALU.add).then_inc(s_lb, 1)
                dve.wait_ge(s_a, 3)
                dve.scalar_tensor_tensor(lx[:], lx[:], 0.0, le[:], ALU.min, ALU.subtract).then_inc(s_la, 1)
                dve.wait_ge(s_8, 96)
                dve.wait_ge(s_z, 2)
                step = Count(dve, s_g)
                for d in range(2):
                    gi, gf, r5 = gate[0][d], gate[1][d], K.rows5[d]
                    run = (lambda t: t[:]) if d == 0 else (lambda t: backwards(t, 4, TALL))
                    chunks = lambda t: t[:].rearrange("r (c t) -> r c t", t=P)
                    end = P - 1 if d == 0 else 0
                    step(dve.tensor_scalar(gi[:], gi[:], bias[0][d][:], None, ALU.add))
                    step(dve.tensor_scalar(gf[:], gf[:], bias[1][d][:], None, ALU.add))
                    dve.wait_ge(s_ge, 4 * d + 3)
                    step(dve.scalar_tensor_tensor(gf[:], gf[:], 0.0, tmp[d][:], ALU.min, ALU.subtract))
                    step(dve.tensor_tensor_scan(run(acum[d]), reset[:], run(gf), 0.0, ALU.mult, ALU.add))
                    step(dve.tensor_tensor_scan(run(mrun[d]), run(gf), run(gi), 0.0, ALU.add, ALU.max))
                    step(dve.memset(mprev[d][:], 0.0))
                    m = chunks(mrun[d])
                    if d == 0:
                        step(dve.tensor_copy(mprev[d][:, 1:NCH], m[:, 0:NCH - 1, end]))
                    else:
                        step(dve.tensor_copy(mprev[d][:, 0:NCH - 1], m[:, 1:NCH, end]))
                    step(dve.tensor_tensor(r5[:, :, U_, :], chunks(acum[d]), m, ALU.subtract))
                    step(dve.tensor_tensor(r5[:, :, C_, :], chunks(gi), chunks(acum[d]), ALU.subtract))
                    step(dve.tensor_scalar(r5[:, :, M_, :], m, -1.0, None, ALU.mult))
                    step(dve.tensor_tensor(r5[:, :, W_, :], r5[:, :, U_, :], mprev[d][:].unsqueeze(2).to_broadcast([4, NCH, P]), ALU.add))
                    step(dve.tensor_tensor(r5[:, :, G_, :], r5[:, :, C_, :],
                                           r5[:, :, U_, end:end + 1].to_broadcast([4, NCH, P]), ALU.add))
                dve.wait_ge(s_col, 1)
                for d in range(2):
                    dve.tensor_copy(K.kwcol[d][:], pg[:, d])

            @block.scalar
            def _(act):
                act.wait_ge(s_lb, NCH)
                act.activation(le[:], lx[:], ACT.Abs).then_inc(s_a, 1)
                act.wait_ge(s_a, 1)
                act.activation(le[:], le[:], ACT.Exp, scale=-1.0).then_inc(s_a, 1)
                act.wait_ge(s_a, 2)
                act.activation(le[:], le[:], ACT.Ln, bias=1.0).then_inc(s_a, 1)
                for d in range(2):
                    act.wait_ge(s_g, 12 * d + 2)
                    act.activation(tmp[d][:], gate[1][d][:], ACT.Abs).then_inc(s_ge, 1)
                    act.wait_ge(s_ge, 4 * d + 1)
                    act.activation(tmp[d][:], tmp[d][:], ACT.Exp, scale=-1.0).then_inc(s_ge, 1)
                    act.wait_ge(s_ge, 4 * d + 2)
                    act.activation(tmp[d][:], tmp[d][:], ACT.Ln, bias=1.0).then_inc(s_ge, 1)
                    act.wait_ge(s_g, 12 * d + 12)
                    g = K.rows5[d][:, :, G_, :]
                    act.activation(g, g, ACT.Exp).then_inc(s_ge, 1)
                    act.wait_ge(s_ge, 4 * d + 4)
                    act.sem_inc(s_row, 1)


def backwards(t, parts, n):
    a = t[:]
    return bass.AP(a.tensor, a.offset + n - 1, [a.ap[0], [-1, n]])


def stage_conv(K):
    nc = K.nc
    raw, out = K.scratch["mqk_raw"], K.dram("mqkF", [1024, TSCAN])
    R, W = 16, 64
    with K.stage() as st:
        img = [K.sb(f"img{u}", [P, R + 2, W + 2], stack=st) for u in range(2)]
        row = [K.sb(f"ctxrow{u}", [P, NCTX + 2], stack=st) for u in range(2)]
        acc = [K.sb(f"conv_acc{u}", [P, TALL], stack=st) for u in range(2)]
        s_z = K.sem("conv_zero")
        s_in, s_tap, s_act, s_out = ([K.sem(f"conv_{x}{u}") for u in range(2)] for x in ("in", "taps", "act", "out"))
        cw, cb = K.col_at["ml_conv_w"], K.col_at["ml_conv_b"]
        NTAP = 12
        with nc.Block() as block:
            @block.gpsimd
            def _(pool):
                for u in range(2):
                    pool.memset(img[u][:], 0.0).then_inc(s_z, 1)
                    pool.memset(row[u][:], 0.0).then_inc(s_z, 1)

            @block.sync
            def _(sp):
                sp.wait_ge(s_z, 4)
                with sp.Fori(0, 4) as i:
                    for u in range(2):
                        sp.wait_ge(s_tap[u], i * NTAP)
                        rows = bass.ds(i * 2 * P + u * P, P)
                        sp.dma_start(img[u][:, 1:R + 1, 1:W + 1],
                                     raw[rows, NCTX:NCTX + T].rearrange("p (r w) -> p r w", w=W)).then_inc(s_in[u], 16)
                        sp.dma_start(row[u][:, 1:NCTX + 1], raw[rows, 0:NCTX]).then_inc(s_in[u], 16)

            @block.vector
            def _(dve):
                with dve.Fori(0, 4) as i:
                    for u in range(2):
                        dve.wait_ge(s_in[u], (i + 1) * 32)
                        dve.wait_ge(s_out[u], i * 32)
                        step = Count(dve, s_tap[u], i * NTAP)
                        ax = acc[u][:, NCTX:TALL].rearrange("p (r w) -> p r w", w=W)
                        ac = acc[u][:, 0:NCTX]
                        for n in range(9):
                            dy, dx = n // 3, n % 3
                            wcol = K.cols[:, bass.ds(i * 2 + (cw + 8 * n + u), 1)]
                            src = img[u][:, dy:dy + R, dx:dx + W]
                            if n == 0:
                                step(dve.tensor_scalar(ax, src, wcol, None, ALU.mult))
                            else:
                                step(dve.scalar_tensor_tensor(ax, src, wcol, ax, ALU.mult, ALU.add))
                        for dx in range(3):
                            wcol = K.cols[:, bass.ds(i * 2 + (cw + 8 * (3 + dx) + u), 1)]
                            src = row[u][:, dx:dx + NCTX]
                            if dx == 0:
                                step(dve.tensor_scalar(ac, src, wcol, None, ALU.mult))
                            else:
                                step(dve.scalar_tensor_tensor(ac, src, wcol, ac, ALU.mult, ALU.add))
                        assert step.n == NTAP

            @block.scalar
            def _(act):
                with act.Fori(0, 4) as i:
                    for u in range(2):
                        act.wait_ge(s_tap[u], (i + 1) * NTAP)
                        act.activation(acc[u][:], acc[u][:], ACT.Silu,
                                       bias=K.cols[:, bass.ds(i * 2 + (cb + u), 1)]).then_inc(s_act[u], 1)
                        act.wait_ge(s_act[u], i + 1)
                        rows = bass.ds(i * 2 * P + u * P, P)
                        act.dma_start(out[rows, 0:TALL], acc[u][:]).then_inc(s_out[u], 16)
                        act.dma_start(out[rows, TALL:TSCAN], acc[u][:, 0:NCTX]).then_inc(s_out[u], 16)
                for u in range(2):
                    act.wait_ge(s_out[u], 4 * 32)


def stage_turn_rows(K, name, src, ncols, dst, src0=0):
    nc = K.nc
    nt = ncols // P
    with K.stage() as st:
        f = K.sb(f"{name}_f", [P, nt, TSCAN], stack=st)
        t = [K.sb(f"{name}_t{u}", [P, nt, P], stack=st) for u in range(2)]
        pt = [K.ps(f"{name}_ps{u}", [P, nt, P], st) for u in range(2)]
        s_in, s_t = K.sem(f"{name}_in"), K.sem(f"{name}_turned")
        s_c = K.sem(f"{name}_copied")
        s_o = [K.sem(f"{name}_out{u}") for u in range(2)]
        n_ch = TSCAN // P
        with nc.Block() as block:
            @block.sync
            def _(sp):
                sp.dma_start(f[:], src[src0:src0 + ncols, :].rearrange("(k p) t -> p k t", p=P)).then_inc(s_in, 16)
                for n in range(n_ch):
                    sp.wait_ge(s_c, n + 1)
                    sp.dma_start(dst[n * P:(n + 1) * P, :].rearrange("t (k p) -> t k p", p=P), t[n % 2][:]).then_inc(s_o[n % 2], 16)
                for u in range(2):
                    sp.wait_ge(s_o[u], n_ch // 2 * 16)

            @block.tensor
            def _(pe):
                pe.wait_ge(s_in, 16)
                for n in range(n_ch):
                    if n >= 2:
                        pe.wait_ge(s_c, n - 1)
                    for k in range(nt):
                        mm = pe.transpose(pt[n % 2][:, k, :], f[:, k, n * P:(n + 1) * P], K.c("ident"))
                    mm.then_inc(s_t, 1)

            @block.vector
            def _(dve):
                for n in range(n_ch):
                    dve.wait_ge(s_t, n + 1)
                    if n >= 2:
                        dve.wait_ge(s_o[n % 2], n // 2 * 16)
                    dve.tensor_copy(t[n % 2][:], pt[n % 2][:]).then_inc(s_c, 1)


def stage_gla(K):
    nc = K.nc
    qk, vT, kT, la = K.scratch["gqkF"], K.scratch["vT"], K.scratch["gkT"], K.scratch["laT"]
    out = K.dram("gla_o", [2, 512, TALL])
    TAU = 1.0 / 16
    with K.stage() as st:
        D2 = range(2)
        sb2 = lambda n, shape: [K.sb(f"gla_{n}{d}", shape, stack=st) for d in D2]
        q, k = sb2("q", [P, 2, P]), sb2("k", [P, 2, P])
        kt, v, lat = sb2("kT", [P, 256]), sb2("v", [P, 4, P]), sb2("la", [P, 256])
        e1, e2, e3, e4 = sb2("e_mid", [P, 2, P]), sb2("e_inv", [P, 2, P]), sb2("e_cum", [P, 2, P]), sb2("e_end", [P, 256])
        qa, qs, ke = sb2("qa", [P, 2, P]), sb2("qs", [P, 2, P]), sb2("ke", [P, 256])
        ka, S = sb2("ka", [P, 4, P]), sb2("S", [P, 4, P])
        att, ob = sb2("att", [P, 4, P]), sb2("o", [P, 4, P])
        mask = [K.sb(f"gla_mask{d}", [P, 4, P], mybir.dt.int32, stack=st) for d in D2]
        pb = [K.ps(f"gla_decay{d}", [P, 2, 2, P], st) for d in D2]
        pe_ = [K.ps(f"gla_end{d}", [P, 256], st) for d in D2]
        pa = [K.ps(f"gla_att{d}", [P, 4, P], st) for d in D2]
        po = [K.ps(f"gla_out{d}", [P, 4, P], st) for d in D2]
        sem2 = lambda n: [K.sem(f"gla_{n}{d}") for d in D2]
        s_in, s_dec, s_exp, s_q, s_att, s_m, s_o, s_su, s_S, s_ob, s_st = (
            sem2(x) for x in ("in", "decay", "exp", "scaled", "att", "masked", "o", "su", "S", "evac", "stored"))
        s_init = K.sem("gla_init")
        with nc.Block() as block:
            @block.sync
            def _(sp):
                with sp.Fori(0, NCH) as j:
                    for d in D2:
                        at = j * P if d == 0 else (TSCAN // P - 1) * P - j * P
                        sp.wait_ge(s_init, 8)
                        sp.wait_ge(s_o[d], j)
                        f = qk[:, bass.ds(at, P)].rearrange("(a p) t -> p a t", p=P)
                        sp.dma_start(q[d][:], f[:, 0:2, :]).then_inc(s_in[d], 16)
                        sp.dma_start(k[d][:], f[:, 2:4, :]).then_inc(s_in[d], 16)
                        sp.dma_start(kt[d][:], kT[bass.ds(at, P), :]).then_inc(s_in[d], 16)
                        sp.dma_start(v[d][:], vT[bass.ds(at, P), 0:512].rearrange("t (h p) -> t h p", p=P)).then_inc(s_in[d], 16)
                        sp.dma_start(lat[d][:], la[bass.ds(at, P), d * 256:(d + 1) * 256]).then_inc(s_in[d], 16)

            @block.tensor
            def _(pe):
                pe.wait_ge(s_init, 8)
                with pe.Fori(0, NCH) as j:
                    for d in D2:
                        pe.wait_ge(s_in[d], (j + 1) * 80)
                        pe.wait_ge(s_S[d], j * 4)
                        for p in range(2):
                            for m, w in enumerate((f"mid{d}", f"tri{d}")):
                                pe.matmul(pb[d][:, p, m, :], lat[d][:, p * P:(p + 1) * P], K.c(w), start=True, stop=True)
                        pe.matmul(pe_[d][:], K.c(f"after{d}"), lat[d][:], start=True, stop=True).then_inc(s_dec[d], 1)
                    for d in D2:
                        pe.wait_ge(s_q[d], (j + 1) * 5)
                        pe.wait_ge(s_m[d], j)
                        for h in range(4):
                            mm = pe.matmul(pa[d][:, h, :], ka[d][:, h, :], qa[d][:, h // 2, :], start=True, stop=True)
                        mm.then_inc(s_att[d], 1)
                        for h in range(4):
                            p = h // 2
                            mm = pe.matmul(pb[d][:, p, h % 2, :], ke[d][:, p * P:(p + 1) * P], v[d][:, h, :], start=True, stop=True)
                        mm.then_inc(s_su[d], 1)
                    for d in D2:
                        pe.wait_ge(s_m[d], j + 1)
                        pe.wait_ge(s_ob[d], j)
                        for h in range(4):
                            pe.matmul(po[d][:, h, :], v[d][:, h, :], att[d][:, h, :], start=True, stop=False)
                            mm = pe.matmul(po[d][:, h, :], S[d][:, h, :], qs[d][:, h // 2, :], start=False, stop=True)
                        mm.then_inc(s_o[d], 1)

            @block.scalar
            def _(act):
                with act.Fori(0, NCH) as j:
                    for d in D2:
                        act.wait_ge(s_dec[d], j + 1)
                        act.wait_ge(s_o[d], j)
                        act.activation(e1[d][:], pb[d][:, :, 0, :], ACT.Exp, scale=TAU).then_inc(s_exp[d], 1)
                        act.activation(e2[d][:], pb[d][:, :, 0, :], ACT.Exp, scale=-TAU).then_inc(s_exp[d], 1)
                        act.activation(e3[d][:], pb[d][:, :, 1, :], ACT.Exp, scale=TAU).then_inc(s_exp[d], 1)
                        act.activation(e4[d][:], pe_[d][:], ACT.Exp, scale=TAU).then_inc(s_exp[d], 1)
                    for d in D2:
                        act.wait_ge(s_o[d], j + 1)
                        act.wait_ge(s_st[d], j * 16)
                        act.activation(ob[d][:], po[d][:], ACT.Copy).then_inc(s_ob[d], 1)
                        act.wait_ge(s_ob[d], j + 1)
                        at = j * P if d == 0 else (NCH - 1) * P - j * P
                        act.dma_start(out[d, :, bass.ds(at, P)].rearrange("(h p) t -> p h t", p=P), ob[d][:]).then_inc(s_st[d], 16)
                for d in D2:
                    act.wait_ge(s_st[d], NCH * 16)

            @block.vector
            def _(dve):
                for d in D2:
                    dve.memset(S[d][:], 0.0).then_inc(s_init, 1)
                    dve.memset(att[d][:], 0.0).then_inc(s_init, 1)
                    dve.memset(ka[d][:], 0.0).then_inc(s_init, 1)
                    m = K.c(f"tri{d}").unsqueeze(1).to_broadcast([P, 4, P])
                    dve.tensor_copy(mask[d][:], m).then_inc(s_init, 1)
                dve.wait_ge(s_init, 8)
                with dve.Fori(0, NCH) as j:
                    for d in D2:
                        dve.wait_ge(s_exp[d], (j + 1) * 4)
                        dve.tensor_tensor(qa[d][:], q[d][:], e1[d][:], ALU.mult).then_inc(s_q[d], 1)
                        for r in (slice(0, 64), slice(64, P)):
                            own = ka[d][r].rearrange("p (a b) t -> p a b t", b=2)[:, :, r.start // 64, :]
                            dve.tensor_tensor(own, k[d][r], e2[d][r], ALU.mult).then_inc(s_q[d], 1)
                        dve.tensor_tensor(qs[d][:], q[d][:], e3[d][:], ALU.mult).then_inc(s_q[d], 1)
                        dve.tensor_tensor(ke[d][:], kt[d][:], e4[d][:], ALU.mult).then_inc(s_q[d], 1)
                    for d in D2:
                        dve.wait_ge(s_init, 8)
                        dve.wait_ge(s_att[d], j + 1)
                        dve.copy_predicated(att[d][:], mask[d][:], pa[d][:]).then_inc(s_m[d], 1)
                    for d in D2:
                        dve.wait_ge(s_su[d], j + 1)
                        dve.wait_ge(s_o[d], j + 1)
                        end = P - 1 if d == 0 else 0
                        for h in range(4):
                            p, r = h // 2, slice(64 * (h % 2), 64 * (h % 2) + 64)
                            dve.scalar_tensor_tensor(S[d][r, h, :], S[d][r, h, :], e3[d][r, p, end:end + 1],
                                                     pb[d][r, p, h % 2, :], ALU.mult, ALU.add).then_inc(s_S[d], 1)


def stage_mlstm(K):
    nc = K.nc
    qk, vT, kT = K.scratch["mqkF"], K.scratch["vT"], K.scratch["mkT"]
    out = K.dram("ml_o", [2, 512, TALL])
    QS = float(P) ** -0.5
    U_, W_, M_, C_, G_ = range(5)
    with K.stage() as st:
        D2 = range(2)
        sb2 = lambda n, shape: [K.sb(f"ml_{n}{d}", shape, stack=st) for d in D2]
        q, k, kt, va = sb2("q", [P, 4, P]), sb2("k", [P, 4, P]), sb2("kT", [P, 4, P]), sb2("v_ones", [P, 4, 2 * P])
        rb = sb2("rows_now", [4, 5, P])
        dx, wx, mx = sb2("exp_pair", [P, 4, P]), sb2("exp_inter", [P, 4, P]), sb2("exp_negm", [P, 4, P])
        pr, qw, kw = sb2("probs", [P, 4, P]), sb2("qw", [P, 4, P]), sb2("kw", [P, 4, P])
        den, ob, S = sb2("den", [P, 4, P]), sb2("o", [P, 4, P]), sb2("S", [P, 4, 2 * P])
        b0 = [K.ps(f"ml_exp_num{d}", [P, 4, P], st) for d in D2]
        b1 = [K.ps(f"ml_inter_den{d}", [P, 4, P], st) for d in D2]
        b23 = [K.ps(f"ml_m_qk_state{d}", [P, 2, 4, P], st) for d in D2]
        sem2 = lambda n: [K.sem(f"ml_{n}{d}") for d in D2]
        s_in, s_rb, s_e, s_x, s_p, s_nd, s_su, s_S, s_dn, s_h, s_st = (sem2(x) for x in (
            "in", "rows", "exponents", "exp", "weighted", "num_den", "su", "S", "den", "h", "stored"))
        s_init = K.sem("ml_init")
        with nc.Block() as block:
            @block.sync
            def _(sp):
                sp.wait_ge(s_init, 4)
                with sp.Fori(0, NCH) as j:
                    for d in D2:
                        at = j * P if d == 0 else (TSCAN // P - 1) * P - j * P
                        sp.wait_ge(s_init, 4)
                        sp.wait_ge(s_su[d], j)
                        f = qk[:, bass.ds(at, P)].rearrange("(a p) t -> p a t", p=P)
                        sp.dma_start(q[d][:], f[:, 0:4, :]).then_inc(s_in[d], 16)
                        sp.dma_start(k[d][:], f[:, 4:8, :]).then_inc(s_in[d], 16)
                        sp.dma_start(kt[d][:], kT[bass.ds(at, P), :].rearrange("t (h p) -> t h p", p=P)).then_inc(s_in[d], 16)
                        sp.dma_start(va[d][:, :, 0:P], vT[bass.ds(at, P), 512:1024].rearrange("t (h p) -> t h p", p=P)) \
                            .then_inc(s_in[d], 16)

            @block.gpsimd
            def _(pool):
                for d in D2:
                    pool.memset(S[d][:], 0.0).then_inc(s_init, 1)
                    pool.memset(va[d][:, :, P:2 * P], 1.0).then_inc(s_init, 1)
                with pool.Fori(0, NCH) as j:
                    for d in D2:
                        at = j * (5 * P) if d == 0 else (NCH - 1) * (5 * P) - j * (5 * P)
                        pool.wait_ge(s_init, 4)
                        pool.wait_ge(s_e[d], j)
                        pool.tensor_copy(rb[d][:].rearrange("r a t -> r (a t)"),
                                         K.rows5[d][:].rearrange("r c a t -> r (c a t)")[:, bass.ds(at, 5 * P)]).then_inc(s_rb[d], 1)

            @block.tensor
            def _(pe):
                pe.wait_ge(s_init, 4)
                with pe.Fori(0, NCH) as j:
                    for d in D2:
                        sel = K.c("selrow")
                        pe.wait_ge(s_in[d], (j + 1) * 64)
                        pe.wait_ge(s_h[d], j)
                        pe.wait_ge(s_S[d], j * 4)
                        neg = K.c(f"neg{d}").unsqueeze(1).to_broadcast([P, 4, P])
                        pe.matmul(b0[d][:], K.c("ident"), neg, start=True, stop=False)
                        pe.wait_ge(s_rb[d], j + 1)
                        pe.matmul(b0[d][:], rb[d][:, C_, :], sel[0:4, :], start=False, stop=False)
                        for h in range(4):
                            one = sel[0:4, h * P:(h + 1) * P]
                            pe.matmul(b0[d][:, h, :], one, rb[d][:, U_, :], start=False, stop=h == 3)
                        for h in range(4):
                            one = sel[0:4, h * P:(h + 1) * P]
                            pe.matmul(b1[d][:, h, :], one, rb[d][:, W_, :], start=True, stop=True)
                            pe.matmul(b23[d][:, 0, h, :], one, rb[d][:, M_, :], start=True, stop=True)
                        for h in range(4):
                            mm = pe.matmul(b23[d][:, 1, h, :], k[d][:, h, :], q[d][:, h, :], start=True, stop=True)
                        mm.then_inc(s_e[d], 1)
                    for d in D2:
                        pe.wait_ge(s_p[d], (j + 1) * 3)
                        for h in range(4):
                            pe.matmul(b0[d][:, h, :], va[d][:, h, 0:P], pr[d][:, h, :], start=True, stop=False)
                            pe.matmul(b0[d][:, h, :], S[d][:, h, 0:P], qw[d][:, h, :], start=False, stop=True)
                        for h in range(4):
                            pe.matmul(b1[d][:, h, :], K.c("ones"), pr[d][:, h, :], start=True, stop=False)
                            mm = pe.matmul(b1[d][:, h, :], S[d][:, h, P:2 * P], qw[d][:, h, :], start=False, stop=True)
                        mm.then_inc(s_nd[d], 1)
                        for h in range(4):
                            o = b23[d][:, h // 2, 2 * (h % 2):2 * (h % 2) + 2, :].rearrange("p a b -> p (a b)")
                            mm = pe.matmul(o, kw[d][:, h, :], va[d][:, h, :], start=True, stop=True)
                        mm.then_inc(s_su[d], 1)

            @block.scalar
            def _(act):
                with act.Fori(0, NCH) as j:
                    for d in D2:
                        act.wait_ge(s_e[d], j + 1)
                        act.wait_ge(s_S[d], j * 4)
                        act.activation(dx[d][:], b0[d][:], ACT.Exp).then_inc(s_x[d], 1)
                        act.activation(wx[d][:], b1[d][:], ACT.Exp).then_inc(s_x[d], 1)
                        act.activation(mx[d][:], b23[d][:, 0], ACT.Exp).then_inc(s_x[d], 1)
                    for d in D2:
                        act.wait_ge(s_h[d], j + 1)
                        at = j * P if d == 0 else (NCH - 1) * P - j * P
                        act.dma_start(out[d, :, bass.ds(at, P)].rearrange("(h p) t -> p h t", p=P), ob[d][:]).then_inc(s_st[d], 16)
                for d in D2:
                    act.wait_ge(s_st[d], NCH * 16)

            @block.vector
            def _(dve):
                with dve.Fori(0, NCH) as j:
                    for d in D2:
                        at = j * 4 if d == 0 else (NCH - 1) * 4 - j * 4
                        dve.wait_ge(s_x[d], (j + 1) * 3)
                        dve.scalar_tensor_tensor(pr[d][:], b23[d][:, 1], QS, dx[d][:], ALU.mult, ALU.mult).then_inc(s_p[d], 1)
                        dve.scalar_tensor_tensor(qw[d][:], q[d][:], QS, wx[d][:], ALU.mult, ALU.mult).then_inc(s_p[d], 1)
                        kc = K.kwcol[d][:].rearrange("p c h -> p (c h)")[:, bass.ds(at, 4)].unsqueeze(2).to_broadcast([P, 4, P])
                        dve.tensor_tensor(kw[d][:], kt[d][:], kc, ALU.mult).then_inc(s_p[d], 1)
                    for d in D2:
                        dve.wait_ge(s_nd[d], j + 1)
                        step = Count(dve, s_dn[d], j * 3)
                        step(dve.scalar_tensor_tensor(den[d][:], b1[d][:], -1.0, mx[d][:], ALU.mult, ALU.max))
                        step(dve.tensor_tensor(den[d][:], b1[d][:], den[d][:], ALU.max))
                        step(dve.reciprocal(den[d][:], den[d][:]))
                        dve.wait_ge(s_st[d], j * 16)
                        dve.tensor_tensor(ob[d][:], b0[d][:], den[d][:], ALU.mult).then_inc(s_h[d], 1)
                        dve.wait_ge(s_su[d], j + 1)
                        end = P - 1 if d == 0 else 0
                        for h in range(4):
                            o = b23[d][:, h // 2, 2 * (h % 2):2 * (h % 2) + 2, :].rearrange("p a b -> p (a b)")
                            dve.scalar_tensor_tensor(S[d][:, h, :], S[d][:, h, :], wx[d][:, h, end:end + 1], o,
                                                     ALU.mult, ALU.add).then_inc(s_S[d], 1)


def stage_join(K, name, parts, mixF):
    nc = K.nc
    with K.stage() as st:
        a, b, g = ([K.sb(f"{name}_{x}{u}", [P, T], stack=st) for u in range(2)] for x in ("fwd", "bwd", "gate"))
        sq, rs = ([K.sb(f"{name}_{x}{u}", [P, T], stack=st) for u in range(2)] for x in ("sq", "rstd"))
        pm = [K.ps(f"{name}_ps{u}", [P, 2, BANK], st) for u in range(2)]
        s_in, s_a, s_mm, s_v, s_x = ([K.sem(f"{name}_{x}{u}") for u in range(2)] for x in ("in", "act", "mean", "vec", "sum"))
        mix = mixF[:].rearrange("p k t -> p (k t)")
        two = len(parts[0][0].shape) == 3
        nin = 48 if two else 32
        with nc.Block() as block:
            @block.sync
            def _(sp):
                for r, (src, _, gate, _) in enumerate(parts):
                    with sp.Fori(0, 2) as i:
                        for u in range(2):
                            n = i + 2 * r
                            sp.wait_ge(s_v[u], n * 4)
                            rows = bass.ds(i * 2 * P + u * P, P)
                            if two:
                                sp.dma_start(a[u][:], src[0, rows, NCTX:TALL]).then_inc(s_in[u], 16)
                                sp.dma_start(b[u][:], src[1, rows, 0:T]).then_inc(s_in[u], 16)
                            else:
                                sp.dma_start(a[u][:], src[rows, :]).then_inc(s_in[u], 16)
                            sp.dma_start(g[u][:], gate[rows, :]).then_inc(s_in[u], 16)

            @block.vector
            def _(dve):
                for r, (_, gain, _, tile) in enumerate(parts):
                    with dve.Fori(0, 2) as i:
                        for u in range(2):
                            n = i + 2 * r
                            if two:
                                dve.wait_ge(s_in[u], (n + 1) * nin)
                                dve.tensor_tensor(a[u][:], a[u][:], b[u][:], ALU.add).then_inc(s_x[u], 1)
                            dve.wait_ge(s_mm[u], n + 1)
                            step = Count(dve, s_v[u], n * 4)
                            step(dve.tensor_scalar(rs[u][:], pm[u][:].rearrange("p a b -> p (a b)"), EPS, None, ALU.add))
                            dve.wait_ge(s_a[u], n * 2 + 2)
                            step(dve.reciprocal(rs[u][:], rs[u][:]))
                            gc = K.cols[:, bass.ds(i * 2 + (K.col_at[gain] + u), 1)]
                            step(dve.scalar_tensor_tensor(rs[u][:], rs[u][:], gc, g[u][:], ALU.mult, ALU.mult))
                            step(dve.tensor_tensor(mix[:, bass.ds(i * 2 * T + (tile + u) * T, T)], a[u][:], rs[u][:], ALU.mult))

            @block.scalar
            def _(act):
                for r in range(len(parts)):
                    with act.Fori(0, 2) as i:
                        for u in range(2):
                            n = i + 2 * r
                            act.wait_ge(s_x[u] if two else s_in[u], n + 1 if two else (n + 1) * nin)
                            act.activation(sq[u][:], a[u][:], ACT.Square).then_inc(s_a[u], 1)
                            act.wait_ge(s_v[u], n * 4 + 1)
                            act.activation(rs[u][:], rs[u][:], ACT.Sqrt).then_inc(s_a[u], 1)

            @block.tensor
            def _(pe):
                for r in range(len(parts)):
                    with pe.Fori(0, 2) as i:
                        for u in range(2):
                            n = i + 2 * r
                            pe.wait_ge(s_a[u], n * 2 + 1)
                            for h in range(2):
                                mm = pe.matmul(pm[u][:, h, :], K.c("mean128"), sq[u][:, h * BANK:(h + 1) * BANK], start=True, stop=True)
                            mm.then_inc(s_mm[u], 1)


def mixer_one(K):
    nc, A = K.nc, K.A
    w_in = A["w_in"][0]
    mc = K.modcols
    with ExitStack() as norm:
        pair = lambda n, t: tuple(K.sb(f"{n}_{x}", [P, KT, t], stack=norm) for x in ("hi", "lo"))
        K.x, K.ctx = pair("hN", T), pair("ctxN", NCTX)
        g1 = K.cols[:, K.col_at["norm1_g"]:K.col_at["norm1_g"] + 8]
        with ExitStack() as c:
            K.ctxF = K.sb("ctxF", [P, KT, NCTX], stack=c)
            stage_turn_in(K)
            stage_norm(K, "n1x", K.hF, K.x, T, g1, shift=mc[:, 0:8], scale=mc[:, 8:16])
            stage_norm(K, "n1c", K.ctxF, K.ctx, NCTX, g1, shift=mc[:, 48:56], scale=mc[:, 56:64])
        gqk, mqk = K.dram("gqkF", [512, TSCAN]), K.dram("mqk_raw", [1024, TSCAN])
        ggF, moF = K.dram("ggF", [512, T]), K.dram("moF", [512, T])
        vT, gkT = K.dram("vT", [TSCAN, 1024]), K.dram("gkT", [TSCAN, 256])
        part = lambda c, n: w_in[:, c:c + n]
        stage_gemm_f(K, "in1", [
            (part(GQ, 256), 256, gqk[0:256], ACT.Copy, 0.125), (part(GK, 256), 256, gqk[256:512], ACT.Copy, 1.0),
            (part(MQK, 1024), 1024, mqk, ACT.Copy, 1.0), (part(GG, 512), 512, ggF, ACT.Silu, 1.0),
            (part(MO, 512), 512, moF, ACT.Sigmoid, 1.0)], K.x, T, ctx=K.ctx)
        toks = [(K.ctx, i * P, (i * P, TALL + i * P)) for i in range(NCTX // P)] + \
               [(K.x, i * P, (NCTX + i * P,)) for i in range(T // P)]
        stage_gemm_t(K, "vT", [(part(GV, 512), vT, 0), (part(MV, 512), vT, 512), (part(GK, 256), gkT, 0)], toks, bufs=1)
        stage_misc(K)
    K.mixstack = K.stack.enter_context(ExitStack())
    stage_gates(K)
    stage_conv(K)
    stage_turn_rows(K, "mkT", K.scratch["mqkF"], 512, K.dram("mkT", [TSCAN, 512]), src0=512)
    stage_gla(K)
    stage_mlstm(K)
    K.mixstack.close()
    with ExitStack() as st:
        mixF = K.sb("mixF", [P, KT, T], stack=st)
        stage_join(K, "join1", [(K.scratch["gla_o"], "gla_norm_g", ggF, 0), (K.scratch["ml_o"], "ml_norm_g", moF, 4)], mixF)
        parts = tuple(K.sb(f"mixF_{x}", [P, KT, T], stack=st) for x in ("hi", "lo"))
        stage_gemm_f(K, "wout1", [(A["w_out"][0], D, None, None, 1.0)], parts, T, whole=mixF, residual=K.hF, gcol=mc[:, 16:24])


def stage_route(K):
    nc, A = K.nc, K.A
    rows = K.dram("moe_rows", [NSORT, D])
    NT, NU = T // P, 2 * T // P
    NL = NG + NE
    with K.stage() as st:
        sb = lambda n, shape, dt=F32: K.sb(f"route_{n}", shape, dt, stack=st)
        rw, rb, lg = sb("w", [P, KT, NL]), sb("b", [P, NL]), sb("logits", [P, NT, NL])
        trow = [sb(f"rows{i}", [P, D]) for i in range(NT)]
        zero = sb("zero", [P, D])
        gmax, ge, gsum, idx = sb("gmax", [P, NT]), sb("gexp", [P, NT, NG]), sb("gsum", [P, NT]), sb("idx", [P, NT])
        oh4, em, cand = sb("group", [P, NT, NG]), sb("masked", [P, NT, NE]), sb("cand", [P, NT, NE])
        v = sb("top", [P, 2, NT])
        oh, pre = sb("onehot", [P, NU, NE]), sb("prefix", [P, NU, NE])
        cnt, cnti = sb("count", [P, NE]), sb("count_i", [P, NE], I32)
        nb, bend, base = sb("blocks", [P, NE]), sb("blk_end", [P, NE]), sb("base", [P, NE])
        dest = sb("dest", [P, NU])
        pt = [K.ps(f"route_turn{i}", [P, 2, BANK], st) for i in range(2)]
        pl = K.ps("route_logits", [P, NT, NL], st)
        pr = K.ps("route_rank", [P, NU, NE], st)
        pc = K.ps("route_count", [P, NE], st)
        s_in, s_lg, s_t, s_tc, s_step, s_ex, s_oh, s_rank, s_tot, s_cleared, s_zero, s_dest, s_sc = (
            K.sem(f"route_{x}") for x in ("in", "logits", "turned", "copied", "step", "exp", "onehot", "rank",
                                          "count", "cleared", "zero", "dest", "scattered"))
        iota32 = K.c("iota")[:, 0:NE]
        bc = lambda ap, n: ap.unsqueeze(2).to_broadcast([P, ap.shape[1], n])
        with nc.Block() as block:
            @block.sync
            def _(sp):
                gw, ew = A["router_group_w"][0], A["router_expert_w"][0]
                sp.dma_start(rw[:, :, 0:NG], gw.rearrange("(k p) n -> p k n", p=P)).then_inc(s_in, 16)
                sp.dma_start(rw[:, :, NG:NL], ew.rearrange("(k p) n -> p k n", p=P)).then_inc(s_in, 16)
                sp.dma_start(rb[:, 0:NG], A["router_group_b"][0].partition_broadcast(P)).then_inc(s_in, 16)
                sp.dma_start(rb[:, NG:NL], A["router_expert_b"][0].partition_broadcast(P)).then_inc(s_in, 16)
                sp.wait_ge(s_cleared, 1)
                for i in range(NSORT // P):
                    sp.dma_start(rows[i * P:(i + 1) * P, :], zero[:]).then_inc(s_zero, 16)

            @block.gpsimd
            def _(pool):
                pool.memset(zero[:], 0.0).then_inc(s_cleared, 1)
                pool.wait_ge(s_zero, 16 * (NSORT // P))
                pool.wait_ge(s_tc, NT)
                pool.wait_ge(s_dest, 1)
                for u in range(NU):
                    pool.indirect_dma_start(rows, bass.IndirectOffsetOnAxis(ap=K.moe_dest[:, u:u + 1], axis=0),
                                            trow[u % NT][:], None).then_inc(s_sc, 16)
                pool.wait_ge(s_sc, 16 * NU)

            @block.tensor
            def _(pe):
                pe.wait_ge(s_in, 64)
                for i in range(NT):
                    for k in range(KT):
                        mm = pe.matmul(pl[:, i, :], K.hN[:, k, i * P:(i + 1) * P], rw[:, k, :], start=k == 0, stop=k == KT - 1)
                mm.then_inc(s_lg, 1)
                for i in range(NT):
                    if i >= 2:
                        pe.wait_ge(s_tc, i - 1)
                    for k in range(KT):
                        mm = pe.transpose(pt[i % 2][:, k // 4, (k % 4) * P:(k % 4 + 1) * P], K.hN[:, k, i * P:(i + 1) * P], K.c("ident"))
                    mm.then_inc(s_t, 1)
                pe.wait_ge(s_oh, 2)
                pe.matmul(pr[:].rearrange("p u e -> p (u e)"), K.c("before"), oh[:].rearrange("p u e -> p (u e)"), start=True, stop=False)
                pe.matmul(pr[:].rearrange("p u e -> p (u e)"), K.c("ones"), pre[:].rearrange("p u e -> p (u e)"),
                          start=False, stop=True).then_inc(s_rank, 1)
                pe.matmul(pc[:], K.c("ones"), pre[:, NU - 1, :], start=True, stop=False)
                pe.matmul(pc[:], K.c("ones"), oh[:, NU - 1, :], start=False, stop=True).then_inc(s_tot, 1)

            @block.scalar
            def _(act):
                for i in range(NT):
                    act.wait_ge(s_t, i + 1)
                    act.activation(trow[i][:], pt[i % 2][:].rearrange("p a b -> p (a b)"), ACT.Copy).then_inc(s_tc, 1)
                    if i == 0:
                        act.wait_ge(s_step, 3)
                        act.activation(ge[:], ge[:], ACT.Exp).then_inc(s_ex, 1)
                act.wait_ge(s_ex, 2)
                act.activation(v[:, 1, :], v[:, 1, :], ACT.Exp).then_inc(s_ex, 1)

            @block.vector
            def _(dve):
                step = Count(dve, s_step)

                def first_of(hits, n, onehot):
                    io = K.c("iota")[:, 0:n].unsqueeze(1).to_broadcast([P, NT, n])
                    c = cand[:, :, 0:n]
                    step(dve.tensor_scalar(c, hits, -1e6, 1e6, ALU.mult, ALU.add))
                    step(dve.tensor_tensor(c, c, io, ALU.add))
                    step(dve.tensor_reduce(idx[:], c, AX.X, ALU.min))
                    step(dve.tensor_tensor(onehot, io, bc(idx[:], n), ALU.is_equal))

                dve.wait_ge(s_in, 64)
                dve.wait_ge(s_lg, 1)
                step(dve.tensor_tensor(lg[:], pl[:], rb[:].unsqueeze(1).to_broadcast([P, NT, NL]), ALU.add))
                gl, el = lg[:, :, 0:NG], lg[:, :, NG:NL]
                step(dve.tensor_reduce(gmax[:], gl, AX.X, ALU.max))
                step(dve.tensor_tensor(ge[:], gl, bc(gmax[:], NG), ALU.subtract))
                step(dve.tensor_tensor(oh4[:], gl, bc(gmax[:], NG), ALU.is_equal))
                first_of(oh4[:], NG, oh4[:])
                e4 = em[:].rearrange("p t (g e) -> p (t g) e", g=NG)
                ohg = oh4[:].rearrange("p t g -> p (t g)").unsqueeze(2).to_broadcast([P, NT * NG, EPG])
                step(dve.tensor_copy(em[:], el))
                step(dve.tensor_tensor(e4, e4, ohg, ALU.mult))
                step(dve.tensor_scalar(oh4[:], oh4[:], 1e30, -1e30, ALU.mult, ALU.add))
                step(dve.tensor_tensor(e4, e4, ohg, ALU.add))
                for k in range(2):
                    o = oh[:, k * NT:(k + 1) * NT, :]
                    step(dve.tensor_reduce(v[:, k, :], em[:], AX.X, ALU.max))
                    step(dve.tensor_tensor(o, em[:], bc(v[:, k, :], NE), ALU.is_equal))
                    first_of(o, NE, o)
                    if k == 0:
                        step(dve.scalar_tensor_tensor(em[:].rearrange("p t e -> p (t e)"), o.rearrange("p t e -> p (t e)"), -2e30,
                                                      em[:].rearrange("p t e -> p (t e)"), ALU.mult, ALU.add))
                step(dve.memset(pre[:, 0, :], 0.0))
                for u in range(1, NU):
                    step(dve.tensor_tensor(pre[:, u, :], pre[:, u - 1, :], oh[:, u - 1, :], ALU.add))
                dve.sem_inc(s_oh, 2)
                dve.wait_ge(s_ex, 1)
                step(dve.tensor_reduce(gsum[:], ge[:], AX.X, ALU.add))
                step(dve.reciprocal(gsum[:], gsum[:]))
                step(dve.tensor_tensor(v[:, 1, :], v[:, 1, :], v[:, 0, :], ALU.subtract))
                dve.sem_inc(s_ex, 1)
                dve.wait_ge(s_ex, 3)
                step(dve.tensor_scalar(v[:, 0, :], v[:, 1, :], 1.0, None, ALU.add))
                step(dve.reciprocal(v[:, 0, :], v[:, 0, :]))
                step(dve.tensor_tensor(K.moe_w[:, 0, :], v[:, 0, :], gsum[:], ALU.mult))
                step(dve.tensor_tensor(K.moe_w[:, 1, :], K.moe_w[:, 0, :], v[:, 1, :], ALU.mult))
                dve.wait_ge(s_tot, 1)
                step(dve.tensor_scalar(cnt[:], pc[:], float(BR - 1), None, ALU.add))
                step(dve.tensor_copy(cnti[:], cnt[:]))
                step(dve.tensor_scalar(cnti[:], cnti[:], BR.bit_length() - 1, None, ALU.arith_shift_right))
                step(dve.tensor_copy(nb[:], cnti[:]))
                step(dve.tensor_scalar(nb[:], nb[:], 1.0, None, ALU.max))
                step(dve.tensor_tensor_scan(bend[:], K.c("ones")[:, 0:NE], nb[:], 0.0, ALU.mult, ALU.add))
                step(dve.tensor_tensor(base[:], bend[:], nb[:], ALU.subtract))
                step(dve.tensor_scalar(base[:], base[:], float(BR), None, ALU.mult))
                dve.wait_ge(s_rank, 1)
                step(dve.tensor_tensor(pre[:], pr[:], base[:].unsqueeze(1).to_broadcast([P, NU, NE]), ALU.add))
                step(dve.tensor_tensor(pre[:], pre[:], oh[:], ALU.mult))
                step(dve.tensor_reduce(dest[:], pre[:], AX.X, ALU.add))
                step(dve.tensor_copy(K.moe_dest[:], dest[:]))
                dve.sem_inc(s_dest, 1)
                step(dve.memset(K.blk_at[:], 0))
                step(dve.tensor_copy(K.blk_at[:, 1:NE + 1], bend[:]))


def stage_experts(K):
    nc, A = K.nc, K.A
    rows = yb = K.scratch["moe_rows"]
    w1, w2 = A["expert_w_in"][0].rearrange("e k n -> (e k) n"), A["expert_w_out"][0].rearrange("e k n -> (e k) n")
    KE = DE // P
    with K.stage() as st:
        U = range(2)
        sb = lambda n, shape: K.sb(f"exp_{n}", shape, stack=st)
        wi, wo = [sb(f"w_in{u}", [P, KT, 2 * DE]) for u in U], [sb(f"w_out{u}", [P, KE, D]) for u in U]
        xr, xT = sb("rows", [BR, D]), sb("xT", [P, KT, BR])
        sg, h, yT, y = sb("silu", [P, KE, BR]), sb("h", [P, KE, BR]), sb("yT", [P, KT, BR]), sb("y", [BR, D])
        pt = K.ps("exp_turn", [P, KT, BR], st)
        pg = K.ps("exp_up", [P, 2, KE, BR], st)
        py = [K.ps(f"exp_down{n}", [P, KT // 2, BR], st) for n in U]
        pr = K.ps("exp_back", [BR, 2, BANK], st)
        s_wi, s_wo, s_ui, s_uo = ([K.sem(f"exp_{n}{u}") for u in U] for n in ("w_in", "w_out", "w_in_used", "w_out_used"))
        s_x, s_t, s_xT, s_up, s_sg, s_h, s_y, s_yT, s_r, s_ye, s_st = (K.sem(f"exp_{n}") for n in (
            "rows", "turned", "xT", "up", "silu", "h", "down", "yT", "back", "y", "stored"))

        def blocks(eng, e):
            first, end = (eng.value_load(K.blk_at[0:1, bass.ds(e + n, 1)], min_val=n, max_val=NBLK) for n in range(2))
            return eng.Fori(first, end)
        with nc.Block() as block:
            @block.sync
            def _(sp):
                with sp.Fori(0, NE // 2) as i:
                    for u in U:
                        sp.wait_ge(s_ui[u], i)
                        sp.dma_start(wi[u][:], w1[bass.ds(i * 2 * D + u * D, D), :].rearrange("(k p) n -> p k n", p=P)).then_inc(s_wi[u], 16)
                        sp.wait_ge(s_uo[u], i)
                        sp.dma_start(wo[u][:], w2[bass.ds(i * 2 * DE + u * DE, DE), :].rearrange("(k p) n -> p k n", p=P)).then_inc(s_wo[u], 16)

            @block.gpsimd
            def _(pool):
                n = pool.value_load(K.blk_at[0:1, NE:NE + 1], min_val=1, max_val=NBLK)
                with pool.Fori(0, n + 1) as b:
                    pool.wait_ge(s_t, b)
                    pool.dma_start(xr[:], rows[bass.ds(b * BR, BR), :]).then_inc(s_x, 16)
                pool.wait_ge(s_st, n * 16)

            @block.tensor
            def _(pe):
                def turn(b):
                    pe.wait_ge(s_x, b * 16 + 16)
                    for k in range(KT):
                        mm = pe.matmul(pt[:, k, :], xr[:, k * P:(k + 1) * P], K.c("ident")[0:BR, 0:BR], start=True, stop=True)
                    mm.then_inc(s_t, 1)
                turn(0)
                with pe.Fori(0, NE // 2) as i:
                    for u in U:
                        with blocks(pe, i * 2 + u) as b:
                            pe.wait_ge(s_xT, b + 1)
                            pe.wait_ge(s_wi[u], i * 16 + 16)
                            for g in range(2):
                                for f in range(KE):
                                    c = g * DE + f * P
                                    for k in range(KT):
                                        mm = pe.matmul(pg[:, g, f, :], wi[u][:, k, c:c + P], xT[:, k, :], start=k == 0, stop=k == KT - 1)
                            mm.then_inc(s_up, 1)
                            turn(b + 1)
                            pe.wait_ge(s_h, b + 1)
                            pe.wait_ge(s_wo[u], i * 16 + 16)
                            for n in range(KT):
                                for k in range(KE):
                                    mm = pe.matmul(py[n // 4][:, n % 4, :], wo[u][:, k, n * P:(n + 1) * P], h[:, k, :], start=k == 0, stop=k == KE - 1)
                                if n % 4 == 3:
                                    mm.then_inc(s_y, 1)
                            pe.wait_ge(s_ye, b * 2)
                            for n in range(KT):
                                if n % 4 == 0:
                                    pe.wait_ge(s_yT, b * 2 + (n // 4 + 1))
                                mm = pe.matmul(pr[:, n // 4, (n % 4) * P:(n % 4 + 1) * P], yT[:, n, :], K.c("ident"), start=True, stop=True)
                                if n % 4 == 3:
                                    mm.then_inc(s_r, 1)
                        pe.sem_inc(s_ui[u], 1)
                        pe.sem_inc(s_uo[u], 1)

            @block.vector
            def _(dve):
                def turned(b):
                    dve.wait_ge(s_t, b + 1)
                    dve.tensor_copy(xT[:], pt[:]).then_inc(s_xT, 1)
                turned(0)
                with dve.Fori(0, NE // 2) as i:
                    for u in U:
                        with blocks(dve, i * 2 + u) as b:
                            dve.wait_ge(s_sg, b + 1)
                            dve.tensor_tensor(h[:], sg[:], pg[:, 1], ALU.mult).then_inc(s_h, 1)
                            turned(b + 1)
                            dve.wait_ge(s_st, b * 16)
                            for n in range(2):
                                dve.wait_ge(s_r, b * 2 + (n + 1))
                                dve.tensor_copy(y[:, n * BANK:(n + 1) * BANK], pr[:, n, :]).then_inc(s_ye, 1)

            @block.scalar
            def _(act):
                with act.Fori(0, NE // 2) as i:
                    for u in U:
                        with blocks(act, i * 2 + u) as b:
                            act.wait_ge(s_up, b + 1)
                            act.activation(sg[:], pg[:, 0], ACT.Silu).then_inc(s_sg, 1)
                            for n in range(2):
                                act.wait_ge(s_y, b * 2 + (n + 1))
                                act.activation(yT[:, 4 * n:4 * n + 4, :], py[n][:], ACT.Copy).then_inc(s_yT, 1)
                            act.wait_ge(s_ye, b * 2 + 2)
                            act.dma_start(yb[bass.ds(b * BR, BR), :], y[:]).then_inc(s_st, 16)


def stage_combine(K, gcol):
    nc = K.nc
    yb = K.scratch["moe_rows"]
    NT = T // P
    with K.stage() as st:
        U = range(2)
        a = [[K.sb(f"comb_{k}_{u}", [P, D], stack=st) for u in U] for k in range(2)]
        pt = [K.ps(f"comb_ps{u}", [P, 2, 4, P], st) for u in U]
        s_g = [[K.sem(f"comb_in{k}{u}") for u in U] for k in range(2)]
        s_w, s_t, s_h = K.sem("comb_sum"), K.sem("comb_turned"), K.sem("comb_added")
        with nc.Block() as block:
            @block.gpsimd
            def _(pool):
                for i in range(NT):
                    if i >= 2:
                        pool.wait_ge(s_t, i - 1)
                    for k in range(2):
                        pool.indirect_dma_start(a[k][i % 2][:], None, yb, bass.IndirectOffsetOnAxis(
                            ap=K.moe_dest[:, k * NT + i:k * NT + i + 1], axis=0)).then_inc(s_g[k][i % 2], 16)

            @block.vector
            def _(dve):
                for i in range(NT):
                    u = i % 2
                    for k in range(2):
                        dve.wait_ge(s_g[k][u], 16 * (i // 2 + 1))
                    dve.tensor_scalar(a[1][u][:], a[1][u][:], K.moe_w[:, 1, i:i + 1], None, ALU.mult).then_inc(s_w, 1)
                    dve.wait_ge(s_w, 2 * i + 1)
                    dve.scalar_tensor_tensor(a[0][u][:], a[0][u][:], K.moe_w[:, 0, i:i + 1], a[1][u][:], ALU.mult, ALU.add).then_inc(s_w, 1)
                    dve.wait_ge(s_t, i + 1)
                    for k in range(KT):
                        h = K.hF[:, k, i * P:(i + 1) * P]
                        ins = dve.scalar_tensor_tensor(h, pt[u][:, k // 4, k % 4, :], gcol[:, k:k + 1], h, ALU.mult, ALU.add)
                    ins.then_inc(s_h, 1)

            @block.tensor
            def _(pe):
                for i in range(NT):
                    u = i % 2
                    pe.wait_ge(s_w, 2 * i + 2)
                    if i >= 2:
                        pe.wait_ge(s_h, i - 1)
                    for k in range(KT):
                        mm = pe.transpose(pt[u][:, k // 4, k % 4, :], a[0][u][:, k * P:(k + 1) * P], K.c("ident"))
                    mm.then_inc(s_t, 1)


def moe(K):
    mc = K.modcols
    g = lambda n: K.cols[:, K.col_at[n]:K.col_at[n] + 8]
    with ExitStack() as plan:
        K.moe_w = K.sb("moe_w", [P, 2, T // P], stack=plan)
        K.moe_dest = K.sb("moe_dest", [P, 2 * T // P], I32, stack=plan)
        K.blk_at = K.sb("blk_at", [P, NE + 1], I32, stack=plan)
        with ExitStack() as norm:
            K.hN = K.sb("hN2", [P, KT, T], stack=norm)
            stage_norm(K, "n2", K.hF, K.hN, T, g("norm2_g"), shift=mc[:, 24:32], scale=mc[:, 32:40])
            stage_route(K)
        stage_experts(K)
        stage_combine(K, mc[:, 40:48])
    stage_norm(K, "nf1", K.hF, K.hF, T, g("final_norm_g"))


HQ, HF_, HI, HG, BQ, BK, BV, CIN = 0, 512, 1024, 1536, 2048, 2304, 2560, 2816
LEVELS = (8, 16, 32, 64)
DIAG = 8


def stage_hgrn(K):
    nc = K.nc
    qF, fF, iF, vT = (K.scratch[n] for n in ("hq", "hf", "hi", "viT"))
    out = K.dram("hgrn_o", [512, T])
    NC = T // P
    NL = len(LEVELS)
    with K.stage() as st:
        sb = lambda n, shape: K.sb(f"hg_{n}", shape, stack=st)
        q, x, vi, vt = sb("q", [P, T]), sb("f_raw", [P, T]), sb("i", [P, T]), sb("iT", [P, NC, P])
        ex, f, k, b, reset = sb("exp", [P, T]), sb("f", [P, T]), sb("k", [P, T]), sb("b", [P, T]), sb("reset", [P, T])
        lev = sb("levels", [P, NL, T])
        eb, ee, qb, ke, keT = sb("e_cum", [P, T]), sb("e_end", [P, T]), sb("qb", [P, T]), sb("ke", [P, T]), sb("keT", [P, NC, P])
        kf = [sb(f"kf{n}", [P, T]) for n in range(2)]
        pr = [sb(f"prod{n}", [P, T]) for n in range(2)]
        dt, od = sb("diag_term", [P, T]), sb("o", [P, T])
        att, S = [sb(f"att{n}", [P, NL, P]) for n in range(2)], sb("S", [P, P])
        pd = K.ps("hg_diag", [P, 2, BANK], st)
        pa = [K.ps(f"hg_att{n}", [P, NL, P], st) for n in range(2)]
        po = K.ps("hg_o", [P, 2, BANK], st)
        psu = K.ps("hg_su", [P, P], st)
        s_in, s_ls, s_lf, s_f, s_b, s_d, s_e, s_t, s_kt, s_ktc, s_pr, s_dg, s_dt, s_lv, s_m, s_su, s_S, s_o, s_fin, s_st, s_kf, s_z = (
            K.sem(f"hg_{n}") for n in ("in", "logsig", "logf", "f", "b", "diff", "exp", "scaled", "turned", "keT",
                                       "prod", "diag", "term", "levels", "att", "su", "S", "o", "done", "stored", "kf", "zero"))
        span = lambda t, L: t.rearrange("p (n h l) -> p n h l", h=2, l=L)
        blocks = lambda t: t.rearrange("p (n l) -> p n l", l=DIAG)
        chunks = lambda t: t.rearrange("p (c t) -> p c t", t=P)
        masks = K.const[:, K.const_at["level8"][0]:K.const_at["level8"][0] + NL * P].rearrange("p (l t) -> p l t", l=NL)
        NT_ = 2 * NL + 2
        with nc.Block() as block:
            @block.sync
            def _(sp):
                with sp.Fori(0, 4) as i:
                    rows = bass.ds(i * P, P)
                    sp.wait_ge(s_fin, i)
                    sp.dma_start(x[:], fF[rows, :]).then_inc(s_in, 16)
                    sp.dma_start(q[:], qF[rows, :]).then_inc(s_in, 16)
                    sp.dma_start(vi[:], iF[rows, :]).then_inc(s_in, 16)
                    sp.dma_start(vt[:], vT[:, rows].rearrange("(c t) v -> t c v", t=P)).then_inc(s_in, 16)

            @block.gpsimd
            def _(pool):
                pool.memset(reset[:], 1.0).then_inc(s_z, 1)
                pool.wait_ge(s_z, 1)
                pool.memset(chunks(reset[:])[:, :, 0:1], 0.0).then_inc(s_z, 1)

            @block.scalar
            def _(act):
                with act.Fori(0, 4) as i:
                    act.wait_ge(s_in, (i + 1) * 64)
                    act.wait_ge(s_fin, i)
                    step = Count(act, s_ls, i * 3)
                    step(act.activation(ex[:], x[:], ACT.Abs))
                    step(act.activation(ex[:], ex[:], ACT.Exp, scale=-1.0))
                    step.mark(act.activation(ex[:], ex[:], ACT.Ln, bias=1.0))
                    act.wait_ge(s_lf, i + 1)
                    act.activation(f[:], x[:], ACT.Exp).then_inc(s_f, 1)
                    for n in range(NL):
                        act.wait_ge(s_d, i * (2 * NL + 1) + 2 * n + 2)
                        act.activation(lev[:, n, :], lev[:, n, :], ACT.Exp).then_inc(s_e, 1)
                    act.activation(eb[:], b[:], ACT.Exp).then_inc(s_e, 1)
                    act.wait_ge(s_d, (i + 1) * (2 * NL + 1))
                    act.activation(ee[:], ee[:], ACT.Exp).then_inc(s_e, 1)
                    for n in range(2):
                        act.wait_ge(s_kt, i * 2 + n + 1)
                        act.activation(keT[:, 4 * n:4 * n + 4, :], pd[:, n, :].rearrange("p (c t) -> p c t", t=P), ACT.Copy).then_inc(s_ktc, 1)
                    act.wait_ge(s_fin, i + 1)
                    act.dma_start(out[bass.ds(i * P, P), :], od[:]).then_inc(s_st, 16)
                act.wait_ge(s_st, 64)

            @block.vector
            def _(dve):
                dve.wait_ge(s_z, 2)
                with dve.Fori(0, 4) as i:
                    dve.wait_ge(s_ls, (i + 1) * 3)
                    dve.scalar_tensor_tensor(x[:], x[:], 0.0, ex[:], ALU.min, ALU.subtract).then_inc(s_lf, 1)
                    dve.wait_ge(s_lf, i + 1)
                    dve.tensor_tensor_scan(b[:], reset[:], x[:], 0.0, ALU.mult, ALU.add).then_inc(s_b, 1)
                    dve.wait_ge(s_f, i + 1)
                    dve.tensor_scalar(k[:], f[:], -1.0, 1.0, ALU.mult, ALU.add).then_inc(s_b, 1)
                    dve.wait_ge(s_b, i * 2 + 2)
                    for n, L in enumerate(LEVELS):
                        bs, d = span(b[:], L), span(lev[:, n, :], L)
                        ref = bs[:, :, 0, L - 1:L].to_broadcast([P, T // (2 * L), L])
                        dve.tensor_tensor(d[:, :, 0, :], ref, bs[:, :, 0, :], ALU.subtract).then_inc(s_d, 1)
                        dve.tensor_tensor(d[:, :, 1, :], bs[:, :, 1, :], ref, ALU.subtract).then_inc(s_d, 1)
                    bc = chunks(b[:])
                    dve.tensor_tensor(chunks(ee[:]), bc[:, :, P - 1:P].to_broadcast([P, NC, P]), bc, ALU.subtract).then_inc(s_d, 1)
                    for n, L in enumerate(LEVELS):
                        d = span(lev[:, n, :], L)
                        dve.wait_ge(s_e, i * (NL + 2) + n + 1)
                        dve.tensor_tensor(d[:, :, 0, :], d[:, :, 0, :], span(k[:], L)[:, :, 0, :], ALU.mult).then_inc(s_t, 1)
                        dve.tensor_tensor(d[:, :, 1, :], d[:, :, 1, :], span(q[:], L)[:, :, 1, :], ALU.mult).then_inc(s_t, 1)
                    dve.wait_ge(s_e, (i + 1) * (NL + 2))
                    dve.tensor_tensor(qb[:], q[:], eb[:], ALU.mult).then_inc(s_t, 1)
                    dve.tensor_tensor(ke[:], k[:], ee[:], ALU.mult).then_inc(s_t, 1)
                    dve.memset(S[:], 0.0).then_inc(s_S, 1)
                    step = Count(dve, s_dt, i * (2 * DIAG - 1))
                    att_step = Count(dve, s_m, i * 3 * NC)
                    for n in range(DIAG):
                        W = DIAG - n
                        if n > 0:
                            src = blocks((k if n == 1 else kf[(n - 1) % 2])[:])
                            if n > 1:
                                dve.wait_ge(s_kf, i * (DIAG - 1) + n - 1)
                            dve.tensor_tensor(blocks(kf[n % 2][:])[:, :, n:], src[:, :, n - 1:DIAG - 1], blocks(f[:])[:, :, n:], ALU.mult) \
                                .then_inc(s_kf, 1)
                            dve.wait_ge(s_kf, i * (DIAG - 1) + n)
                        keys = k if n == 0 else kf[n % 2]
                        if n >= 2:
                            dve.wait_ge(s_dg, i * DIAG + n - 1)
                        prod = pr[n % 2][:, 0:P * W].rearrange("p (n l) -> p n l", l=W)
                        dve.tensor_tensor(prod, blocks(q[:])[:, :, n:], blocks(keys[:])[:, :, n:], ALU.mult).then_inc(s_pr, 1)
                        a = att[n % 2]
                        dve.wait_ge(s_lv, i * NC + n + 1)
                        att_step(dve.tensor_tensor(a[:], pa[n % 2][:], masks, ALU.mult))
                        att_step(dve.tensor_tensor(a[:, 0:2, :], a[:, 0:2, :], a[:, 2:4, :], ALU.add))
                        att_step(dve.tensor_tensor(a[:, 0, :], a[:, 0, :], a[:, 1, :], ALU.add))
                        dve.wait_ge(s_dg, i * DIAG + n + 1)
                        sums = pd[:, :, 0:64 * W].rearrange("p a (n l) -> p a n l", l=W)
                        past = blocks(vi[:]).rearrange("p (a n) l -> p a n l", a=2)[:, :, :, 0:W]
                        if n == 0:
                            dve.wait_ge(s_st, i * 16)
                            o = od[:].rearrange("p (a n l) -> p a n l", a=2, l=DIAG)
                            step(dve.tensor_tensor(o, sums, past, ALU.mult))
                        else:
                            d = dt[:, 0:P * W].rearrange("p (a n l) -> p a n l", a=2, l=W)
                            step(dve.tensor_tensor(d, sums, past, ALU.mult))
                            o = blocks(od[:])[:, :, n:]
                            step(dve.tensor_tensor(o, o, dt[:, 0:P * W].rearrange("p (n l) -> p n l", l=W), ALU.add))
                        dve.wait_ge(s_o, i * NC + n + 1)
                        dve.scalar_tensor_tensor(S[:], S[:], eb[:, n * P + P - 1:n * P + P], psu[:], ALU.mult, ALU.add).then_inc(s_S, 1)
                    dve.wait_ge(s_S, (i + 1) * (NC + 1))
                    assert step.n == 2 * DIAG - 1 and NC == DIAG
                    dve.tensor_tensor(od[:], od[:], po[:].rearrange("p a t -> p (a t)"), ALU.add).then_inc(s_fin, 1)

            @block.tensor
            def _(pe):
                with pe.Fori(0, 4) as i:
                    pe.wait_ge(s_t, (i + 1) * NT_)
                    for n in range(2):
                        for c in range(4):
                            mm = pe.transpose(pd[:, n, c * P:(c + 1) * P], ke[:, (4 * n + c) * P:(4 * n + c + 1) * P], K.c("ident"))
                        mm.then_inc(s_kt, 1)

                    def levels(c):
                        if c >= 2:
                            pe.wait_ge(s_m, i * 3 * NC + 3 * (c - 2) + 1)
                        for l in range(NL):
                            o = lev[:, l, c * P:(c + 1) * P]
                            mm = pe.matmul(pa[c % 2][:, l, :], o, o, start=True, stop=True)
                        mm.then_inc(s_lv, 1)
                    levels(0)
                    levels(1)
                    pe.wait_ge(s_fin, i)
                    for n in range(DIAG):
                        W = DIAG - n
                        pe.wait_ge(s_pr, i * DIAG + n + 1)
                        if n == 0:
                            pe.wait_ge(s_ktc, i * 2 + 2)
                        else:
                            pe.wait_ge(s_dt, i * (2 * DIAG - 1) + max(1, 2 * n - 2))
                        for h in range(2):
                            mm = pe.matmul(pd[:, h, 0:64 * W], K.c("ones"), pr[n % 2][:, h * 64 * W:(h + 1) * 64 * W], start=True, stop=True)
                        mm.then_inc(s_dg, 1)
                        pe.wait_ge(s_S, i * (NC + 1) + n + 1)
                        pe.matmul(psu[:], keT[:, n, :], vt[:, n, :], start=True, stop=True)
                        pe.wait_ge(s_m, i * 3 * NC + 3 * n + 3)
                        o = po[:, n // 4, (n % 4) * P:(n % 4 + 1) * P]
                        pe.matmul(o, vt[:, n, :], att[n % 2][:, 0, :], start=True, stop=False)
                        pe.matmul(o, S[:], qb[:, n * P:(n + 1) * P], start=False, stop=True).then_inc(s_o, 1)
                        if n + 2 < NC:
                            levels(n + 2)


def stage_windows(K):
    nc = K.nc
    qk, vT = K.scratch["bqk"], K.scratch["viT"]
    out = K.dram("win_o", [256, T])
    NT = T // P
    SC = 0.125
    with K.stage() as st:
        U = range(2)
        sb2 = lambda n, shape: [K.sb(f"win_{n}{u}", shape, stack=st) for u in U]
        q, k = K.sb("win_q", [64, T], stack=st), K.sb("win_k", [64, T], stack=st)
        v = K.sb("win_v", [P, NT, 64], stack=st)
        wide = K.sb("win_mult", [P, 2, T], stack=st)
        sc, mx, zs, rz = sb2("scores", [P, T]), sb2("max", [P, 1]), sb2("sum", [P, 1]), sb2("inv", [P, 1])
        dg, pT = sb2("diag", [P, P]), sb2("probsT", [P, NT, P])
        ob = K.sb("win_out_sb", [64, T], stack=st)
        ps = [K.ps(f"win_s{u}", [P, 2, BANK], st) for u in U]
        pt = K.ps("win_t", [P, 2, 4, P], st)
        po = K.ps("win_out", [64, 2, BANK], st)
        s_in, s_c, s_s, s_pt, s_pc, s_o, s_ob, s_st = (K.sem(f"win_{n}") for n in (
            "in", "const", "scores", "turned", "copied", "o", "evac", "stored"))
        s_v, s_x = K.sem("win_vec"), K.sem("win_exp")
        NV = 7
        with nc.Block() as block:
            @block.sync
            def _(sp):
                sp.dma_start(wide[:], K.wide_dram.rearrange("p (a t) -> p a t", a=2)).then_inc(s_c, 16)
                with sp.Fori(0, 4) as i:
                    sp.wait_ge(s_ob, i)
                    rows = bass.ds(i * 64, 64)
                    sp.dma_start(q[:], qk[rows, :]).then_inc(s_in, 16)
                    sp.dma_start(k[:], qk[bass.ds(i * 64 + 256, 64), :]).then_inc(s_in, 16)
                    sp.dma_start(v[:], vT[:, bass.ds(i * 64 + 512, 64)].rearrange("(c t) v -> t c v", t=P)).then_inc(s_in, 16)

            @block.tensor
            def _(pe):
                with pe.Fori(0, 4) as i:
                    pe.wait_ge(s_in, (i + 1) * 48)

                    def scores(n):
                        W = (n + 1) * P
                        pe.wait_ge(s_v, i * (NT * NV) + NV * (n - 2) + 1 if n >= 2 else i * (NT * NV))
                        pe.wait_ge(s_c, 16)
                        for h in range(-(-W // BANK)):
                            w = min(BANK, W - h * BANK)
                            mm = pe.matmul(ps[n % 2][:, h, 0:w], q[:, n * P:(n + 1) * P], k[:, h * BANK:h * BANK + w], start=True, stop=True)
                        mm.then_inc(s_s, 1)
                    scores(0)
                    for n in range(NT):
                        if n + 1 < NT:
                            scores(n + 1)
                        pe.wait_ge(s_v, i * (NT * NV) + NV * (n + 1))
                        pe.wait_ge(s_pc, i * NT + n)
                        for c in range(n + 1):
                            mm = pe.matmul(pt[:, c // 4, c % 4, :], sc[n % 2][:, c * P:(c + 1) * P], dg[n % 2][:], start=True, stop=True)
                        mm.then_inc(s_pt, 1)
                        pe.wait_ge(s_pc, i * NT + n + 1)
                        if n == 0:
                            pe.wait_ge(s_ob, i)
                        for c in range(n + 1):
                            mm = pe.matmul(po[:, n // 4, (n % 4) * P:(n % 4 + 1) * P], v[:, c, :], pT[n % 2][:, c, :],
                                           start=c == 0, stop=c == n)
                        mm.then_inc(s_o, 1)

            @block.vector
            def _(dve):
                dve.wait_ge(s_c, 16)
                with dve.Fori(0, 4) as i:
                    for n in range(NT):
                        W = (n + 1) * P
                        u = n % 2
                        step = Count(dve, s_v, i * (NT * NV) + n * NV)
                        dve.wait_ge(s_s, i * NT + n + 1)
                        if n >= 2:
                            dve.wait_ge(s_pt, i * NT + n - 1)
                        s = sc[u][:, 0:W]
                        flat = ps[u][:].rearrange("p a t -> p (a t)")[:, 0:W]
                        step(dve.tensor_tensor(s, flat, wide[:, 1, T - W:T], ALU.add))
                        step(dve.tensor_reduce(mx[u][:], s, AX.X, ALU.max))
                        step(dve.tensor_scalar(mx[u][:], mx[u][:], -SC, None, ALU.mult))
                        dve.wait_ge(s_x, i * NT + n + 1)
                        step(dve.tensor_tensor(s, s, wide[:, 0, T - W:T], ALU.mult))
                        step(dve.tensor_reduce(zs[u][:], s, AX.X, ALU.add))
                        step(dve.reciprocal(rz[u][:], zs[u][:]))
                        step(dve.tensor_scalar(dg[u][:], K.c("ident"), rz[u][:], None, ALU.mult))
                    dve.wait_ge(s_o, (i + 1) * NT)
                    dve.wait_ge(s_st, i * 16)
                    dve.tensor_copy(ob[:], po[:].rearrange("p a t -> p (a t)")).then_inc(s_ob, 1)

            @block.scalar
            def _(act):
                with act.Fori(0, 4) as i:
                    def turned(n):
                        act.wait_ge(s_pt, i * NT + n + 1)
                        if n >= 2:
                            act.wait_ge(s_o, i * NT + n - 1)
                        act.activation(pT[n % 2][:, 0:n + 1, :], pt[:].rearrange("p a b t -> p (a b) t")[:, 0:n + 1, :], ACT.Copy).then_inc(s_pc, 1)
                    for n in range(NT):
                        act.wait_ge(s_v, i * (NT * NV) + n * NV + 3)
                        s = sc[n % 2][:, 0:(n + 1) * P]
                        act.activation(s, s, ACT.Exp, scale=SC, bias=mx[n % 2][:]).then_inc(s_x, 1)
                        if n:
                            turned(n - 1)
                    turned(NT - 1)
                    act.wait_ge(s_ob, i + 1)
                    act.dma_start(out[bass.ds(i * 64, 64), :], ob[:]).then_inc(s_st, 16)
                act.wait_ge(s_st, 64)


RK_WD = 768
RK_CH = 64
RK_ALPHA, RK_RHO, RK_K, RK_B, RK_KG, RK_BG, RK_V = range(7)


def stage_rwkv_prep(K):
    nc, A = K.nc, K.A
    cin = K.scratch["cin"]
    rk, rkG = K.dram("rk", [7, 256, T]), K.dram("rk_G", [256, T // RK_CH])
    NC, MID = T // RK_CH, RK_CH // 2 - 1
    DECAY = -float(np.exp(-0.5))
    with K.stage() as st:
        sb = lambda n, shape: K.sb(f"rp_{n}", shape, stack=st)
        raw = [sb(f"raw_{n}", [P, T + 1]) for n in ("r", "k", "v", "ranks", "gate")]
        r, k, v, ranks, gate = (sb(n, [P, T]) for n in ("r", "k", "v", "ranks", "gate"))
        w2, a2, g2 = sb("w2", [P, 256]), sb("a2", [P, 256]), sb("g2", [P, 256])
        d = [sb(f"diff{n}", [P, T]) for n in range(2)]
        lw, a, b, bm = sb("logw", [P, T]), sb("a", [P, T]), sb("cum", [P, T]), sb("cum_mid", [P, T])
        kk, sq, inv, ep, en, ea = (sb(n, [P, T]) for n in ("kk", "sq", "inv", "e_pos", "e_neg", "e_alpha"))
        reset, emid, G = sb("reset", [P, T]), sb("e_mid", [P, NC + 1]), sb("G", [P, NC])
        outs = [sb(f"out{n}", [P, T]) for n in range(6)]
        pw, pa, pg, pn = (K.ps(f"rp_{n}", [P, 2, BANK], st) for n in ("w", "a", "g", "sum"))
        s_z, s_w, s_lo, s_in, s_mix, s_low, s_z3, s_sig, s_gc, s_v, s_kk, s_sq, s_n, s_rt, s_e, s_bo, s_bp, s_out, s_st = (
            K.sem(f"rp_{n}") for n in ("zero", "weights", "ranks_in", "in", "mixed", "ranks", "products", "sigmoid", "gate_copied", "vec", "kk",
                                       "squares", "norm2", "root", "exp", "bonus", "bonus_sum", "out", "stored"))
        chunks = lambda t: t.rearrange("p (c t) -> p c t", t=RK_CH)
        flat = lambda t: t.rearrange("p a t -> p (a t)")
        NV = 8
        with nc.Block() as block:
            @block.gpsimd
            def _(pool):
                for x in raw:
                    pool.memset(x[:, 0:1], 0.0).then_inc(s_z, 1)
                pool.memset(reset[:], 1.0).then_inc(s_z, 1)
                pool.memset(emid[:, NC:NC + 1], 1.0).then_inc(s_z, 1)
                pool.memset(w2[:], 0.0).then_inc(s_z, 1)
                pool.memset(a2[:], 0.0).then_inc(s_z, 1)
                pool.wait_ge(s_z, 9)
                pool.memset(chunks(reset[:])[:, :, 0:1], 0.0).then_inc(s_z, 1)
                pool.dma_start(w2[0:64, :], A["rwkv_w2_2"][0]).then_inc(s_w, 16)
                pool.dma_start(a2[64:P, :], A["rwkv_a2_2"][0]).then_inc(s_w, 16)
                pool.dma_start(g2[:], A["rwkv_g2_2"][0]).then_inc(s_w, 16)

            @block.sync
            def _(sp):
                sp.dma_start(raw[3][:, 1:T + 1], cin[RK_WD:RK_WD + P, :]).then_inc(s_lo, 16)
                sp.dma_start(raw[4][:, 1:T + 1], cin[RK_WD + P:RK_WD + 2 * P, :]).then_inc(s_lo, 16)
                with sp.Fori(0, 2) as i:
                    sp.wait_ge(s_mix, i * 3 + 2)
                    for n in range(3):
                        sp.dma_start(raw[n][:, 1:T + 1], cin[bass.ds(i * P + n * 256, P), :]).then_inc(s_in, 16)
                    rows = bass.ds(i * P, P)
                    for n in range(6):
                        sp.wait_ge(s_out, i * 7 + n + 1)
                        sp.dma_start(rk[n, rows, :], outs[n][:]).then_inc(s_st, 16)
                    sp.dma_start(rk[RK_V, rows, :], v[:]).then_inc(s_st, 16)
                    sp.wait_ge(s_out, i * 7 + 7)
                    sp.dma_start(rkG[rows, :], G[:]).then_inc(s_st, 16)
                sp.wait_ge(s_st, 2 * 8 * 16)

            @block.vector
            def _(dve):
                def mixed(x, dst, mu, n):
                    dve.tensor_tensor(d[n % 2][:], x[:, 0:T], x[:, 1:T + 1], ALU.subtract).then_inc(s_kk, 1)
                    return dve.scalar_tensor_tensor, (dst[:], d[n % 2][:], mu, x[:, 1:T + 1], ALU.mult, ALU.add)
                dve.wait_ge(s_z, 10)
                dve.wait_ge(s_lo, 2 * 16)
                for n, (x, dst) in enumerate(((raw[3], ranks), (raw[4], gate))):
                    op, args = mixed(x, dst, K.col("rwkv_mu_2", 6 + n), n)
                    dve.wait_ge(s_kk, n + 1)
                    op(*args).then_inc(s_mix, 1)
                NK = 8
                pcol = lambda name, i: K.cols[:, bass.ds(i + K.col_at[name], 1)]
                with dve.Fori(0, 2) as i:
                    dve.wait_ge(s_in, (i + 1) * 48)
                    dve.wait_ge(s_st, i * (8 * 16))
                    step = Count(dve, s_kk, i * NK, 2)
                    for n, (x, dst) in enumerate(((raw[0], r), (raw[1], k), (raw[2], v))):
                        op, args = mixed(x, dst, pcol("rwkv_mu_2", i + 2 * n), n)
                        step.n += 1
                        dve.wait_ge(s_kk, i * NK + step.n)
                        op(*args).then_inc(s_mix, 1)
                    dve.wait_ge(s_mix, i * 3 + 5)
                    step(dve.tensor_scalar(kk[:], k[:], pcol("rwkv_k_k_2", i), None, ALU.mult))
                    vec = Count(dve, s_v, i * NV)
                    dve.wait_ge(s_sig, i * 2 + 2)
                    vec(dve.tensor_scalar(lw[:], lw[:], DECAY, None, ALU.mult))
                    vec(dve.tensor_tensor_scan(b[:], reset[:], lw[:], 0.0, ALU.mult, ALU.add))
                    mid = chunks(b[:])[:, :, MID:MID + 1]
                    vec(dve.tensor_tensor(chunks(bm[:]), chunks(b[:]), mid.to_broadcast([P, NC, RK_CH]), ALU.subtract))
                    vec.mark(dve.tensor_tensor(ea[:], bm[:], lw[:], ALU.subtract))
                    step(dve.tensor_scalar(d[0][:], a[:], -1.0, pcol("rwkv_k_a_2", i), ALU.add, ALU.mult))
                    step(dve.scalar_tensor_tensor(k[:], d[0][:], 1.0, k[:], ALU.add, ALU.mult))
                    step(dve.scalar_tensor_tensor(d[1][:], r[:], pcol("rwkv_r_k_2", i), k[:], ALU.mult, ALU.mult))
                    dve.wait_ge(s_rt, i + 1)
                    step(dve.tensor_scalar(inv[:], inv[:], 1e-12, None, ALU.max))
                    vec(dve.reciprocal(inv[:], inv[:]))
                    vec(dve.tensor_tensor(kk[:], kk[:], inv[:], ALU.mult))
                    dve.wait_ge(s_e, i * 4 + 4)
                    dve.scalar_tensor_tensor(outs[RK_ALPHA][:], kk[:], -1.0, ea[:], ALU.mult, ALU.mult).then_inc(s_out, 1)
                    dve.tensor_tensor(outs[RK_RHO][:], r[:], ep[:], ALU.mult).then_inc(s_out, 1)
                    dve.tensor_tensor(outs[RK_K][:], k[:], en[:], ALU.mult).then_inc(s_out, 1)
                    vec(dve.tensor_tensor(kk[:], kk[:], a[:], ALU.mult))
                    dve.tensor_tensor(outs[RK_B][:], kk[:], en[:], ALU.mult).then_inc(s_out, 1)
                    vec(dve.tensor_tensor(G[:], chunks(ep[:])[:, :, RK_CH - 1], emid[:, 1:NC + 1], ALU.mult))
                    dve.wait_ge(s_out, i * 7 + 4)
                    g = G[:].unsqueeze(2).to_broadcast([P, NC, RK_CH])
                    dve.tensor_tensor(chunks(outs[RK_KG][:]), chunks(outs[RK_K][:]), g, ALU.mult).then_inc(s_out, 1)
                    dve.tensor_tensor(chunks(outs[RK_BG][:]), chunks(outs[RK_B][:]), g, ALU.mult).then_inc(s_out, 1)
                    dve.wait_ge(s_bp, i + 1)
                    bonus = flat(K.rk_bonus[:])[:, bass.ds(i * T, T)]
                    dve.tensor_tensor(bonus, flat(pn[:]), v[:], ALU.mult).then_inc(s_out, 1)
                    assert step.n == 2 + NK and vec.n == NV

            @block.scalar
            def _(act):
                pcol = lambda name, i: K.cols[:, bass.ds(i + K.col_at[name], 1)]
                act.wait_ge(s_mix, 2)
                act.activation(ranks[0:64, :], ranks[0:64, :], ACT.Tanh).then_inc(s_low, 1)
                act.activation(gate[:], gate[:], ACT.Sigmoid).then_inc(s_low, 1)
                with act.Fori(0, 2) as i:
                    act.wait_ge(s_z3, i + 1)
                    act.wait_ge(s_out, i * 7)
                    act.activation(lw[:], flat(pw[:]), ACT.Sigmoid, bias=pcol("rwkv_w0_2", i)).then_inc(s_sig, 1)
                    act.activation(a[:], flat(pa[:]), ACT.Sigmoid, bias=pcol("rwkv_a0_2", i)).then_inc(s_sig, 1)
                    act.activation(flat(K.rk_gate[:])[:, bass.ds(i * T, T)], flat(pg[:]), ACT.Copy).then_inc(s_gc, 1)
                    act.wait_ge(s_kk, i * 8 + 6)
                    act.activation(sq[:], kk[:], ACT.Square).then_inc(s_sq, 1)
                    act.wait_ge(s_n, i + 1)
                    act.activation(inv[:], flat(pn[:]), ACT.Sqrt).then_inc(s_rt, 1)
                    act.wait_ge(s_v, i * NV + 4)
                    act.activation(emid[:, 0:NC], chunks(b[:])[:, :, MID], ACT.Exp).then_inc(s_e, 1)
                    act.activation(ep[:], bm[:], ACT.Exp).then_inc(s_e, 1)
                    act.activation(en[:], bm[:], ACT.Exp, scale=-1.0).then_inc(s_e, 1)
                    act.activation(ea[:], ea[:], ACT.Exp).then_inc(s_e, 1)

            @block.tensor
            def _(pe):
                pe.wait_ge(s_low, 2)
                pe.wait_ge(s_w, 3 * 16)
                for i in range(2):
                    if i:
                        pe.wait_ge(s_sig, 2)
                        pe.wait_ge(s_gc, 1)
                    for h in range(2):
                        t = slice(h * BANK, (h + 1) * BANK)
                        pe.matmul(pw[:, h, :], w2[:, i * P:(i + 1) * P], ranks[:, t], start=True, stop=True)
                        pe.matmul(pa[:, h, :], a2[:, i * P:(i + 1) * P], ranks[:, t], start=True, stop=True)
                        mm = pe.matmul(pg[:, h, :], g2[:, i * P:(i + 1) * P], gate[:, t], start=True, stop=True)
                    mm.then_inc(s_z3, 1)
                    pe.wait_ge(s_sq, i + 1)
                    if i:
                        pe.wait_ge(s_out, 7)
                    for h in range(2):
                        mm = pe.matmul(pn[:, h, :], K.c("ones64"), sq[:, h * BANK:(h + 1) * BANK], start=True, stop=True)
                    mm.then_inc(s_n, 1)
                    pe.wait_ge(s_kk, i * 8 + 9)
                    pe.wait_ge(s_rt, i + 1)
                    for h in range(2):
                        mm = pe.matmul(pn[:, h, :], K.c("ones64"), d[1][:, h * BANK:(h + 1) * BANK], start=True, stop=True)
                    mm.then_inc(s_bp, 1)


def stage_rwkv(K):
    nc = K.nc
    rk, rkG = K.scratch["rk"], K.scratch["rk_G"]
    out = K.dram("rk_y", [256, T])
    H, HD, NC = 4, 64, T // RK_CH
    LV = (2, 4, 8, 16, 32)
    with K.stage() as st:
        sb = lambda n, shape: K.sb(f"rks_{n}", shape, stack=st)
        f = sb("in", [HD, 7, H, P])
        Gc, diagG = sb("Gcol", [HD, H, NC]), sb("diagG", [HD, NC, H, HD])
        v, RA, KBz = sb("vT", [P, H, HD]), sb("KAv_alpha", [P, H, 2, HD]), sb("KG_BG", [P, H, 2, 2, HD])
        AB, KK = sb("A_BR", [P, H, 2, P]), sb("KA_KR", [P, H, 2, P])
        X, XT, W = sb("X", [P, H, P]), sb("XT", [P, H, P]), sb("AX", [P, H, P])
        SX = sb("SA_Xalpha", [P, H, 2, HD])
        Ms, Ns = sb("M", [HD, 2, H, HD]), sb("N", [HD, H, 2, HD])
        rho = sb("rho", [HD, H, P])
        S = [sb(f"S{n}", [HD, H, HD]) for n in range(2)]
        yb = sb("y", [HD, H, P])
        pT = K.ps("rk_turned", [P, 2, BANK], st)
        pB = K.ps("rk_AB", [P, H, 2, P], st)
        pK = K.ps("rk_KK", [P, H, 2, P], st)
        pA = K.ps("rk_A", [P, H, P], st)
        pY = K.ps("rk_Y", [HD, H, P], st)
        s_c, s_d, s_S0, s_in, s_t, s_tok, s_sc, s_msk, s_ms, s_ns, s_up, s_S, s_y, s_yc, s_st = (
            K.sem(f"rk_{n}") for n in ("G", "diag", "init", "in", "turned", "tokens", "scores", "masked", "M_copied", "N_copied",
                                       "update", "S", "y", "y_copied", "stored"))
        PAIRS = [(g, slice(2 * g, 2 * g + 2)) for g in range(2)]
        s_x, s_w, s_wm, s_xx, s_r, s_rc, s_xr, s_xrc, s_mn = ([K.sem(f"rk_{n}{g}") for g, _ in PAIRS] for n in (
            "X", "AX", "AX_masked", "X_more", "KAv", "KAv_copied", "SA", "SA_copied", "MN"))
        pTr = pT[:].rearrange("p a (h q e) -> p (a h) q e", h=2, q=4)
        heads_of = lambda bank: bank.rearrange("p (h t) -> p h t", t=P)
        pW = [pA[:, 0:2], pB[:, 0]]
        pX = [heads_of(pT[:, 0, 0:2 * P]), pK[:, 0]]
        pXT = [heads_of(pT[:, 1, :]), pB[:, 2:4].rearrange("p a b t -> p (a b) t")]
        pM = [x[0:HD, 0:2].rearrange("p h (c e) -> p h c e", c=2) for x in pXT]
        pN = [x[0:HD, 2:4].rearrange("p h (c e) -> p h c e", c=2) for x in pXT]
        o_lt = K.const_at["lt_half"][0]
        strict = K.const[:, o_lt:o_lt + 2 * P].unsqueeze(1).to_broadcast([P, H, 2 * P])
        both = lambda name: K.c(name).unsqueeze(1).to_broadcast([P, 2, P])
        NX = 3 + 2 * len(LV) - 1
        with nc.Block() as block:
            @block.sync
            def _(sp):
                sp.dma_start(Gc[:], rkG.rearrange("(h p) c -> p h c", p=HD)).then_inc(s_c, 16)
                with sp.Fori(0, T // P) as i:
                    sp.wait_ge(s_ms, i * 4)
                    for n in range(7):
                        sp.dma_start(f[:, n], rk[n, :, bass.ds(i * P, P)].rearrange("(h p) t -> p h t", p=HD)).then_inc(s_in, 16)

            @block.tensor
            def _(pe):
                pe.wait_ge(s_S0, 1)
                with pe.Fori(0, T // P) as i:
                    pe.wait_ge(s_in, (i + 1) * 112)
                    pe.wait_ge(s_S, i * 2)
                    pe.wait_ge(s_ms, i * 4)
                    pe.wait_ge(s_ns, i * 2)
                    for h in range(H):
                        mm = pe.matmul(pA[:, h, :], f[:, RK_ALPHA, h, :], f[:, RK_B, h, :], start=True, stop=True)
                    mm.then_inc(s_sc, 1)
                    for h in range(H):
                        for q, n in enumerate((RK_V, RK_ALPHA, RK_KG, RK_BG)):
                            mm = pe.transpose(pTr[:, h, q, :], f[:, n, h, :], K.c("ident")[0:HD, 0:HD])
                    mm.then_inc(s_t, 1)
                    for h in range(H):
                        mm = pe.matmul(pB[:, h], f[:, RK_B, h, :], f[:, 0:2, h, :], start=True, stop=True)
                    mm.then_inc(s_sc, 1)
                    for h in range(H):
                        mm = pe.matmul(pK[:, h], f[:, RK_K, h, :], f[:, 0:2, h, :], start=True, stop=True)
                    mm.then_inc(s_sc, 1)
                    pe.wait_ge(s_tok, i * 4 + 4)
                    for n in range(len(LV)):
                        for g, heads in PAIRS:
                            pe.wait_ge(s_x[g], i * NX + (3 + 2 * n))
                            for h in range(heads.start, heads.stop):
                                mm = pe.matmul(pW[g][:, h % 2, :], AB[:, h, 0, :], X[:, h, :], start=True, stop=True)
                            mm.then_inc(s_w[g], 1)
                        for g, heads in PAIRS:
                            pe.wait_ge(s_wm[g], i * len(LV) + (n + 1))
                            for h in range(heads.start, heads.stop):
                                mm = pe.matmul(pXT[g][:, h % 2, :], W[:, h, :], XT[:, h, :], start=True, stop=True)
                            mm.then_inc(s_xx[g], 1)
                            if n < len(LV) - 1:
                                if n == 0 and g == 1:
                                    pe.wait_ge(s_msk, i * 2 + 2)
                                for h in range(heads.start, heads.stop):
                                    mm = pe.matmul(pX[g][:, h % 2, :], XT[:, h, :], W[:, h, :], start=True, stop=True)
                                mm.then_inc(s_xx[g], 1)
                    for g, heads in PAIRS:
                        pe.wait_ge(s_x[g], (i + 1) * NX)
                        for h in range(heads.start, heads.stop):
                            mm = pe.matmul(pW[g][:, h % 2, 0:HD], KK[:, h, 0, :], v[:, h, :], start=True, stop=True)
                        mm.then_inc(s_r[g], 1)
                    for g, heads in PAIRS:
                        pe.wait_ge(s_rc[g], i + 1)
                        for h in range(heads.start, heads.stop):
                            mm = pe.matmul(pX[g][:, h % 2, :], XT[:, h, :], RA[:, h], start=True, stop=True)
                        mm.then_inc(s_xr[g], 1)
                    for g, heads in PAIRS:
                        pe.wait_ge(s_xrc[g], i + 1)
                        for h in range(heads.start, heads.stop):
                            pe.matmul(pM[g][:, h % 2], SX[:, h, 1, :], KBz[:, h, 1], start=True, stop=True)
                            pe.matmul(pW[g][0:HD, h % 2, :], SX[:, h, 1, :], AB[:, h, 1, :], start=True, stop=True)
                            for c in range(2):
                                pe.matmul(pN[g][:, h % 2, c, :], KBz[:, h, 0, c, :], v[:, h, :], start=True, stop=False)
                                mm = pe.matmul(pN[g][:, h % 2, c, :], KBz[:, h, 1, c, :], SX[:, h, 0, :], start=False, stop=True)
                        mm.then_inc(s_mn[g], 1)
                    pe.wait_ge(s_ms, i * 4 + 4)
                    pe.wait_ge(s_yc, i)
                    for c in range(2):
                        pe.wait_ge(s_S, i * 2 + c)
                        t = slice(c * HD, (c + 1) * HD)
                        o = [pY[:, h, t] for h in range(H)]
                        pe.matmul(o[0], v[:, 0, :], KK[:, 0, 1, t], start=True, stop=False)
                        for h in range(H):
                            mm = pe.matmul(pA[0:HD, h, 0:HD], Ms[:, c, h, :], S[c][:, h, :], start=True, stop=True)
                        mm.then_inc(s_up, 1)
                        for h in range(H):
                            if h:
                                pe.matmul(o[h], v[:, h, :], KK[:, h, 1, t], start=True, stop=False)
                            pe.matmul(o[h], SX[:, h, 0, :], AB[:, h, 1, t], start=False, stop=False)
                            mm = pe.matmul(o[h], S[c][:, h, :], rho[:, h, t], start=False, stop=True)
                        mm.then_inc(s_y, 1)

            @block.scalar
            def _(act):
                with act.Fori(0, T // P) as i:
                    act.wait_ge(s_t, i + 1)
                    act.wait_ge(s_y, i * 2)
                    act.activation(v[:], pTr[:, :, 0, :], ACT.Copy).then_inc(s_tok, 1)
                    act.activation(RA[:, :, 1, :], pTr[:, :, 1, :], ACT.Copy).then_inc(s_tok, 1)
                    for c in range(2):
                        half = K.c("halves")[:, c:c + 1]
                        act.activation(KBz[:, :, :, c, :], pTr[:, :, 2:4, :], ACT.Copy, scale=half).then_inc(s_tok, 1)
                    for g, heads in PAIRS:
                        act.wait_ge(s_r[g], i + 1)
                        act.activation(RA[:, heads, 0, :], pW[g][:, :, 0:HD], ACT.Copy).then_inc(s_rc[g], 1)
                    for g, heads in PAIRS:
                        act.wait_ge(s_xr[g], i + 1)
                        act.activation(SX[:, heads].rearrange("p h a e -> p h (a e)"), pX[g], ACT.Copy).then_inc(s_xrc[g], 1)
                    act.wait_ge(s_y, i * 2 + 2)
                    act.wait_ge(s_st, i * 16)
                    act.activation(yb[:], pY[:], ACT.Copy).then_inc(s_yc, 1)
                    act.wait_ge(s_yc, i + 1)
                    act.dma_start(out[:, bass.ds(i * P, P)].rearrange("(h p) t -> p h t", p=HD), yb[:]).then_inc(s_st, 16)
                act.wait_ge(s_st, T // P * 16)

            @block.vector
            def _(dve):
                dve.memset(S[0][:], 0.0).then_inc(s_S0, 1)
                dve.wait_ge(s_c, 16)
                for h in range(H):
                    one = K.c("ident")[0:HD, 0:HD].unsqueeze(1).to_broadcast([HD, NC, HD])
                    dve.tensor_tensor(diagG[:, :, h, :], one, Gc[:, h, :].unsqueeze(2).to_broadcast([HD, NC, HD]), ALU.mult).then_inc(s_d, 1)
                dve.wait_ge(s_d, H)
                with dve.Fori(0, T // P) as i:
                    steps = [Count(dve, s_x[g], i * NX) for g, _ in PAIRS]
                    dve.wait_ge(s_sc, i * 3 + 1)
                    for g, heads in PAIRS:
                        steps[g](dve.tensor_tensor(X[:, heads], pA[:, heads], both("pairT1"), ALU.mult))
                        steps[g].mark(dve.tensor_tensor(X[:, heads], X[:, heads], both("ident"), ALU.add))
                    dve.wait_ge(s_y, i * 2)
                    dve.wait_ge(s_sc, i * 3 + 2)
                    dve.tensor_tensor(AB[:].rearrange("p h a t -> p h (a t)"), pB[:].rearrange("p h a t -> p h (a t)"), strict, ALU.mult) \
                        .then_inc(s_msk, 1)
                    dve.wait_ge(s_msk, i * 2 + 1)
                    for g, heads in PAIRS:
                        dve.tensor_tensor(XT[:, heads], AB[:, heads, 0, :], both("pair1"), ALU.mult).then_inc(s_d, 1)
                        dve.wait_ge(s_d, i * 2 + (H + g + 1))
                        steps[g].mark(dve.tensor_tensor(XT[:, heads], XT[:, heads], both("ident"), ALU.add))
                    dve.wait_ge(s_sc, i * 3 + 3)
                    dve.tensor_tensor(KK[:].rearrange("p h a t -> p h (a t)"), pK[:].rearrange("p h a t -> p h (a t)"), strict, ALU.mult) \
                        .then_inc(s_msk, 1)
                    for n, l in enumerate(LV):
                        last = n == len(LV) - 1
                        for g, heads in PAIRS:
                            dve.wait_ge(s_w[g], i * len(LV) + (n + 1))
                            dve.tensor_tensor(W[:, heads], pW[g], both(f"pairT{l}"), ALU.mult).then_inc(s_wm[g], 1)
                        for g, heads in PAIRS:
                            dve.wait_ge(s_xx[g], i * (2 * len(LV) - 1) + (2 * n + (1 if last else 2)))
                            steps[g].mark(dve.tensor_tensor(XT[:, heads], XT[:, heads], pXT[g][:, 0:2], ALU.add))
                            if not last:
                                steps[g].mark(dve.tensor_tensor(X[:, heads], X[:, heads], pX[g], ALU.add))
                    assert steps[0].n == steps[1].n == NX
                    gd = diagG[:].rearrange("p c h e -> p (c h e)")[:, bass.ds(i * (2 * H * HD), 2 * H * HD)].rearrange("p (c h e) -> p c h e", c=2, h=H)
                    for g, heads in PAIRS:
                        dve.wait_ge(s_mn[g], i + 1)
                        dve.tensor_tensor(Ms[:, :, heads], pM[g].rearrange("p h c e -> p c h e"), gd[:, :, heads], ALU.add).then_inc(s_ms, 1)
                        dve.tensor_copy(Ns[:, heads], pN[g]).then_inc(s_ns, 1)
                        dve.tensor_tensor(rho[:, heads], f[:, RK_RHO, heads], pW[g][0:HD], ALU.add).then_inc(s_ms, 1)
                    dve.wait_ge(s_ns, i * 2 + 2)
                    for c in range(2):
                        dve.wait_ge(s_up, i * 2 + c + 1)
                        if c:
                            dve.wait_ge(s_y, i * 2 + c)
                        dve.tensor_tensor(S[1 - c][:], pA[0:HD, :, 0:HD], Ns[:, :, c, :], ALU.add).then_inc(s_S, 1)


def stage_rwkv_out(K, mixF, tile):
    nc = K.nc
    y_in = K.scratch["rk_y"]
    with K.stage() as st:
        U = range(2)
        sb2 = lambda n: [K.sb(f"ro_{n}{u}", [P, T], stack=st) for u in U]
        y, sq, rs = sb2("y"), sb2("sq"), sb2("rstd")
        pm, pv = ([K.ps(f"ro_{n}{u}", [P, 2, BANK], st) for u in U] for n in ("mean", "var"))
        s_in, s_mm, s_v, s_a = (K.sem(f"ro_{n}") for n in ("in", "means", "vec", "act"))
        flat = lambda t: t.rearrange("p a t -> p (a t)")
        NV = 5
        with nc.Block() as block:
            @block.sync
            def _(sp):
                for u in U:
                    sp.dma_start(y[u][:], y_in[u * P:(u + 1) * P, :]).then_inc(s_in, 16)

            @block.tensor
            def _(pe):
                pe.wait_ge(s_in, 32)
                for u in U:
                    for h in range(2):
                        mm = pe.matmul(pm[u][:, h, :], K.c("mean64"), y[u][:, h * BANK:(h + 1) * BANK], start=True, stop=True)
                    mm.then_inc(s_mm, 1)
                for u in U:
                    pe.wait_ge(s_a, u + 1)
                    for h in range(2):
                        mm = pe.matmul(pv[u][:, h, :], K.c("mean64"), sq[u][:, h * BANK:(h + 1) * BANK], start=True, stop=True)
                    mm.then_inc(s_mm, 1)

            @block.scalar
            def _(act):
                for u in U:
                    act.wait_ge(s_v, u + 1)
                    act.activation(sq[u][:], y[u][:], ACT.Square).then_inc(s_a, 1)
                for u in U:
                    act.wait_ge(s_v, 2 + u * NV + 1)
                    act.activation(rs[u][:], rs[u][:], ACT.Sqrt).then_inc(s_a, 1)

            @block.vector
            def _(dve):
                for u in U:
                    dve.wait_ge(s_mm, u + 1)
                    dve.tensor_tensor(y[u][:], y[u][:], flat(pm[u][:]), ALU.subtract).then_inc(s_v, 1)
                for u in U:
                    step = Count(dve, s_v, 2 + u * NV)
                    dve.wait_ge(s_mm, 3 + u)
                    step(dve.tensor_scalar(rs[u][:], flat(pv[u][:]), RK_GN_EPS, None, ALU.add))
                    dve.wait_ge(s_a, 3 + u)
                    step(dve.reciprocal(rs[u][:], rs[u][:]))
                    step(dve.scalar_tensor_tensor(y[u][:], y[u][:], K.col("rwkv_ln_w_2", u), rs[u][:], ALU.mult, ALU.mult))
                    step(dve.scalar_tensor_tensor(y[u][:], y[u][:], K.col("rwkv_ln_b_2", u), K.rk_bonus[:, u, :], ALU.add, ALU.add))
                    step(dve.tensor_tensor(mixF[:, tile + u, :], y[u][:], K.rk_gate[:, u, :], ALU.mult))
                    assert step.n == NV


def stage_load_rows(K, name, src, dst, tile):
    with K.stage():
        s_in = K.sem(f"{name}_in")
        with K.nc.Block() as block:
            @block.sync
            def _(sp):
                for k in range(src.shape[0] // P):
                    sp.dma_start(dst[:, tile + k, :], src[k * P:(k + 1) * P, :]).then_inc(s_in, 16)
                sp.wait_ge(s_in, src.shape[0] // P * 16)


def mixer_two(K):
    A = K.A
    w_in = A["w_in_2"][0]
    with ExitStack() as norm:
        x = tuple(K.sb(f"hN3_{x}", [P, KT, T], stack=norm) for x in ("hi", "lo"))
        stage_norm(K, "nm", K.hF, x, T, K.cols[:, K.col_at["norm_mix_g_2"]:K.col_at["norm_mix_g_2"] + 8])
        stage_gemm_f(K, "in2", [(w_in[:, c:c + n], n, K.dram(name, [n, T]), func, 1.0) for name, c, n, func in (
            ("hq", HQ, 512, ACT.Silu), ("hg", HG, 512, ACT.Silu), ("hf", HF_, 512, ACT.Copy), ("hi", HI, 512, ACT.Copy),
            ("bqk", BQ, 512, ACT.Copy), ("cin", CIN, 1024, ACT.Copy))], x, T)
        viT = K.dram("viT", [T, 768])
        stage_gemm_t(K, "viT", [(w_in[:, HI:HI + 512], viT, 0), (w_in[:, BV:BV + 256], viT, 512)],
                     [(x, i * P, (i * P,)) for i in range(T // P)])
    stage_hgrn(K)
    stage_windows(K)
    with ExitStack() as mixed:
        K.rk_bonus, K.rk_gate = K.sb("rk_bonus", [P, 2, T], stack=mixed), K.sb("rk_gate", [P, 2, T], stack=mixed)
        stage_rwkv_prep(K)
        stage_rwkv(K)
        mixF = K.sb("mixF2", [P, KT, T], stack=mixed)
        stage_join(K, "join2", [(K.scratch["hgrn_o"], "hgrn_gnorm_g_2", K.scratch["hg"], 0)], mixF)
        stage_load_rows(K, "win_rows", K.scratch["win_o"], mixF, 4)
        stage_rwkv_out(K, mixF, 6)
        parts = tuple(K.sb(f"mixF2_{x}", [P, KT, T], stack=mixed) for x in ("hi", "lo"))
        stage_gemm_f(K, "wout2", [(A["w_out_2"][0], D, None, None, 1.0)], parts, T, whole=mixF, residual=K.hF)


def stage_ffn_up(K, x, actT, halo, h):
    up = K.A["ffn_up_2"][0]
    NJ = NFF // P
    tok = slice(h * BANK, (h + 1) * BANK)
    with K.stage() as st:
        U = G = range(2)
        wt, wh, wl = ([K.sb(f"up{h}_{x}{g}", [P, KT, P], stack=st) for g in G] for x in ("w", "wh", "wl"))
        z = [[K.sb(f"up{h}_z{u}{g}", [P, BANK + 2], stack=st) for g in G] for u in U]
        c = [[K.sb(f"up{h}_conv{u}{g}", [P, BANK], stack=st) for g in G] for u in U]
        pm = [[K.ps(f"up{h}_ps{u}{g}", [P, BANK], st) for g in G] for u in U]
        s_w, s_wh, s_wl, s_mm = ([K.sem(f"up{h}_{n}{g}") for g in G] for n in ("w", "wh", "wl", "mm"))
        s_z, s_vec, s_silu = ([K.sem(f"up{h}_{n}{u}") for u in U] for n in ("z", "vec", "silu"))
        act_tile = lambda i, u: actT[:].rearrange("p k t -> p (k t)")[:, bass.ds(i * 2 * BANK + u * BANK, BANK)]
        kept = lambda i, u, g: halo[:, g].rearrange("p j t -> p (j t)")[:, bass.ds(i * 4 + 2 * u, 2)]
        taps = lambda j, g, n: K.cols[:, bass.ds(j + (K.col_at["ffn_conv_w_2"] + n * 2 * NJ + g * NJ), 1)]
        bias = lambda j, g: K.cols[:, bass.ds(j + (K.col_at["ffn_conv_b_2"] + g * NJ), 1)]
        NV = 9
        with K.nc.Block() as block:
            @block.sync
            def _(sp):
                with sp.Fori(0, NJ // 2) as i:
                    for u in U:
                        for g in G:
                            sp.wait_ge(s_wl[g], i * 2 + u)
                            sp.dma_start(wt[g][:], up[:, bass.ds(i * 2 * P + (u * P + g * NFF), P)].rearrange("(k p) n -> p k n", p=P)) \
                                .then_inc(s_w[g], 16)

            @block.tensor
            def _(pe):
                with pe.Fori(0, NJ // 2) as i:
                    for u in U:
                        for g in G:
                            pe.wait_ge(s_z[u], i * 4 + 2 * g)
                            pe.wait_ge(s_wl[g], i * 2 + (u + 1))
                            for k in range(KT):
                                mm = matmul3(pe, pm[u][g][:], (wh[g][:, k, :], wl[g][:, k, :]), (x[0][:, k, tok], x[1][:, k, tok]),
                                             start=k == 0, stop=k == KT - 1)
                            mm.then_inc(s_mm[g], 1)

            @block.scalar
            def _(act):
                with act.Fori(0, NJ // 2) as i:
                    for u in U:
                        j = i * 2 + u
                        act.wait_ge(s_vec[u], i * NV)
                        for g in G:
                            act.activation(z[u][g][:, 0:2], kept(i, u, g), ACT.Copy).then_inc(s_z[u], 1)
                            act.wait_ge(s_mm[g], i * 2 + (u + 1))
                            act.activation(z[u][g][:, 2:], pm[u][g][:], ACT.Copy).then_inc(s_z[u], 1)
                        act.wait_ge(s_vec[u], i * NV + 4)
                        act.activation(c[u][0][:], c[u][0][:], ACT.Silu, bias=bias(j, 0)).then_inc(s_silu[u], 1)

            @block.vector
            def _(dve):
                def weights(g, n):
                    dve.wait_ge(s_w[g], n * 16 + 16)
                    split(dve, wt[g][:], wh[g][:], wl[g][:], s_wh[g], n + 1).then_inc(s_wl[g], 1)

                def convolved(i, u, g):
                    j = i * 2 + u
                    o = c[u][g][:]
                    dve.wait_ge(s_z[u], i * 4 + (2 * g + 2))
                    step = Count(dve, s_vec[u], i * NV, 4 * g)
                    step.mark(dve.tensor_scalar(kept(i, u, g), z[u][g][:, BANK:], 1.0, None, ALU.mult))
                    step(dve.tensor_scalar(o, z[u][g][:, 0:BANK], taps(j, g, 0), None, ALU.mult))
                    for n in (1, 2):
                        step(dve.scalar_tensor_tensor(o, z[u][g][:, n:n + BANK], taps(j, g, n), o, ALU.mult, ALU.add))
                    if g:
                        dve.wait_ge(s_silu[u], i + 1)
                        dve.scalar_tensor_tensor(act_tile(i, u), o, bias(j, 1), c[u][0][:], ALU.add, ALU.mult).then_inc(s_vec[u], 1)

                def tile(i, u, last=False):
                    for g in G:
                        if not last:
                            dve.wait_ge(s_mm[g], i * 2 + (u + 1))
                            weights(g, i * 2 + (u + 1))
                        convolved(i, u, g)
                for g in G:
                    weights(g, 0)
                with dve.Fori(0, NJ // 2 - 1) as i:
                    for u in U:
                        tile(i, u)
                tile(NJ // 2 - 1, 0)
                tile(NJ // 2 - 1, 1, last=True)


def stage_ffn_down(K, actT, h):
    w = K.A["ffn_down_2"][0]
    NJ = NFF // P
    with K.stage() as st:
        U = range(2)
        wt, wh, wl = ([K.sb(f"down{h}_{x}{u}", [P, D], stack=st) for u in U] for x in ("w", "wh", "wl"))
        ah, al = ([K.sb(f"down{h}_{x}{u}", [P, BANK], stack=st) for u in U] for x in ("ah", "al"))
        pm = K.ps(f"down{h}_ps", [P, KT, BANK], st)
        s_w, s_wh, s_wl, s_ah, s_al, s_mm = ([K.sem(f"down{h}_{x}{u}") for u in U] for x in ("w", "wh", "wl", "ah", "al", "mm"))
        s_all = K.sem(f"down{h}_tile")
        N = NJ // 2
        with K.nc.Block() as block:
            @block.sync
            def _(sp):
                with sp.Fori(0, N) as i:
                    for u in U:
                        sp.wait_ge(s_wl[u], i)
                        sp.dma_start(wt[u][:], w[bass.ds(i * 2 * P + u * P, P), :]).then_inc(s_w[u], 16)

            @block.vector
            def _(dve):
                with dve.Fori(0, N) as i:
                    for u in U:
                        dve.wait_ge(s_w[u], i * 16 + 16)
                        dve.wait_ge(s_mm[u], i)
                        split(dve, wt[u][:], wh[u][:], wl[u][:], s_wh[u], i + 1).then_inc(s_wl[u], 1)
                        a = actT[:].rearrange("p k t -> p (k t)")[:, bass.ds(i * 2 * BANK + u * BANK, BANK)]
                        split(dve, a, ah[u][:], al[u][:], s_ah[u], i + 1).then_inc(s_al[u], 1)
                for m in range(KT):
                    dve.wait_ge(s_all, m + 1)
                    r = K.hF[:, m, h * BANK:(h + 1) * BANK]
                    dve.tensor_tensor(r, pm[:, m, :], r, ALU.add)

            @block.tensor
            def _(pe):
                def products(u, i, first, last):
                    pe.wait_ge(s_wl[u], i + 1)
                    pe.wait_ge(s_al[u], i + 1)
                    for m in range(KT):
                        c = slice(m * P, (m + 1) * P)
                        mm = matmul3(pe, pm[:, m, :], (wh[u][:, c], wl[u][:, c]), (ah[u][:], al[u][:]), start=first, stop=last)
                        if last:
                            mm.then_inc(s_all, 1)
                    if not last:
                        mm.then_inc(s_mm[u], 1)
                for u in U:
                    products(u, 0, u == 0, False)
                with pe.Fori(1, N - 1) as i:
                    for u in U:
                        products(u, i, False, False)
                for u in U:
                    products(u, N - 1, False, u == 1)


def ffn(K):
    with ExitStack() as st:
        x = tuple(K.sb(f"hN4_{x}", [P, KT, T], stack=st) for x in ("hi", "lo"))
        actT = K.sb("ffn_act", [P, NFF // P, BANK], stack=st)
        halo = K.sb("ffn_halo", [P, 2, NFF // P, 2], stack=st)
        stage_norm(K, "nf", K.hF, x, T, K.cols[:, K.col_at["norm_ffn_g_2"]:K.col_at["norm_ffn_g_2"] + 8])
        stage_clear(K, "halo0", halo)
        for h in range(T // BANK):
            stage_ffn_up(K, x, actT, halo, h)
            stage_ffn_down(K, actT, h)


def stage_clear(K, name, tile):
    with K.stage():
        with K.nc.Block() as block:
            @block.vector
            def _(dve):
                dve.memset(tile[:], 0.0)


def stage_embed(K, x):
    nc, A = K.nc, K.A
    NP = 2
    with K.stage() as st:
        U = range(2)
        p_in, pF, pF2 = K.sb("ple_rows", [P, T // P, NP * P], stack=st), K.sb("ple_F", [P, NP, T], stack=st), [K.sb(f"ple_F_{x}", [P, NP, T], stack=st) for x in ("hi", "lo")]
        wt, wh, wl = ([K.sb(f"ple_{n}{u}", [P, KT + NP, P], stack=st) for u in U] for n in ("w", "wh", "wl"))
        g = [K.sb(f"ple_gate{u}", [P, T], stack=st) for u in U]
        pg, pp = ([K.ps(f"ple_{n}{u}", [P, 2, BANK], st) for u in U] for n in ("g", "p"))
        s_p, s_t, s_pc = (K.sem(f"ple_{n}") for n in ("in", "turned", "copied"))
        s_w, s_wh, s_wl, s_mm, s_sig, s_h = ([K.sem(f"ple_{n}{u}") for u in U] for n in ("w", "w_hi", "w_lo", "mm", "sigmoid", "added"))
        s_src, s_srch = K.sem("ple_src"), K.sem("ple_src_hi")
        flat = lambda t: t.rearrange("p a t -> p (a t)")
        cols = lambda w, i, u: w[:, bass.ds(i * 2 * P + u * P, P)].rearrange("(k p) n -> p k n", p=P)
        with nc.Block() as block:
            @block.sync
            def _(sp):
                sp.dma_start(p_in[:], A["p_2"][0, 0].rearrange("(c t) f -> t c f", t=P)).then_inc(s_p, 16)
                with sp.Fori(0, KT // 2) as i:
                    for u in U:
                        sp.wait_ge(s_wl[u], i)
                        sp.dma_start(wt[u][:, 0:KT, :], cols(A["ple_gate_2"][0], i, u)).then_inc(s_w[u], 16)
                        sp.dma_start(wt[u][:, KT:, :], cols(A["ple_proj_2"][0], i, u)).then_inc(s_w[u], 16)

            @block.tensor
            def _(pe):
                pe.wait_ge(s_p, 16)
                for k in range(NP):
                    for c in range(T // P):
                        mm = pe.transpose(pp[k][:, c // 4, (c % 4) * P:(c % 4 + 1) * P], p_in[:, c, k * P:(k + 1) * P], K.c("ident"))
                    mm.then_inc(s_t, 1)
                pe.wait_ge(s_pc, NP)
                with pe.Fori(0, KT // 2) as i:
                    for u in U:
                        pe.wait_ge(s_wl[u], i + 1)
                        pe.wait_ge(s_h[u], i * 2)
                        part = lambda k: (wh[u][:, k, :], wl[u][:, k, :])
                        for k in range(KT + NP):
                            if k >= KT:
                                pe.wait_ge(s_src, k - KT + 1)
                            for h in range(2):
                                t = slice(h * BANK, (h + 1) * BANK)
                                if k < KT:
                                    matmul3(pe, pg[u][:, h, :], part(k), (x[0][:, k, t], x[1][:, k, t]), start=k == 0, stop=k == KT - 1)
                                else:
                                    mm = matmul3(pe, pp[u][:, h, :], part(k), (pF2[0][:, k - KT, t], pF2[1][:, k - KT, t]),
                                                 start=k == KT, stop=k == KT + NP - 1)
                        mm.then_inc(s_mm[u], 1)

            @block.scalar
            def _(act):
                with act.Fori(0, KT // 2) as i:
                    for u in U:
                        act.wait_ge(s_mm[u], i + 1)
                        act.wait_ge(s_h[u], i * 2)
                        act.activation(g[u][:], flat(pg[u][:]), ACT.Sigmoid).then_inc(s_sig[u], 1)

            @block.vector
            def _(dve):
                def weights(u, n):
                    dve.wait_ge(s_w[u], n * 32 + 32)
                    split(dve, wt[u][:], wh[u][:], wl[u][:], s_wh[u], n + 1).then_inc(s_wl[u], 1)

                def added(u, i):
                    dve.wait_ge(s_sig[u], i + 1)
                    step = Count(dve, s_h[u], i * 2)
                    step(dve.tensor_tensor(g[u][:], g[u][:], flat(pp[u][:]), ALU.mult))
                    h = flat(K.hF[:])[:, bass.ds(i * 2 * T + u * T, T)]
                    step.mark(dve.tensor_tensor(h, h, g[u][:], ALU.add))
                for k in range(NP):
                    dve.wait_ge(s_t, k + 1)
                    dve.tensor_copy(pF[:, k, :], flat(pp[k][:])).then_inc(s_pc, 1)
                weights(0, 0)
                dve.wait_ge(s_pc, NP)
                for k in range(NP):
                    split(dve, pF[:, k, :], pF2[0][:, k, :], pF2[1][:, k, :], s_srch, k + 1).then_inc(s_src, 1)
                weights(1, 0)
                with dve.Fori(0, KT // 2 - 1) as i:
                    for u in U:
                        dve.wait_ge(s_mm[u], i + 1)
                        weights(u, i + 1)
                        added(u, i)
                for u in U:
                    added(u, KT // 2 - 1)


def stage_turn_out(K, src):
    nc = K.nc
    NT = T // P
    with K.stage() as st:
        pt = [K.ps(f"out_ps{u}", [P, 2, BANK], st) for u in range(2)]
        ob = [K.sb(f"out_rows{u}", [P, D], stack=st) for u in range(2)]
        s_t, s_c, s_o = K.sem("out_turned"), K.sem("out_copied"), [K.sem(f"out_stored{u}") for u in range(2)]
        with nc.Block() as block:
            @block.tensor
            def _(pe):
                for n in range(NT):
                    if n >= 2:
                        pe.wait_ge(s_c, n - 1)
                    for k in range(KT):
                        mm = pe.transpose(pt[n % 2][:, k // 4, (k % 4) * P:(k % 4 + 1) * P], src[:, k, n * P:(n + 1) * P], K.c("ident"))
                    mm.then_inc(s_t, 1)

            @block.vector
            def _(dve):
                for n in range(NT):
                    dve.wait_ge(s_t, n + 1)
                    if n >= 2:
                        dve.wait_ge(s_o[n % 2], n // 2 * 16)
                    dve.tensor_copy(ob[n % 2][:], pt[n % 2][:].rearrange("p a t -> p (a t)")).then_inc(s_c, 1)

            @block.sync
            def _(sp):
                for n in range(NT):
                    sp.wait_ge(s_c, n + 1)
                    sp.dma_start(K.out[0, n * P:(n + 1) * P, :], ob[n % 2][:]).then_inc(s_o[n % 2], 16)
                for u in range(2):
                    sp.wait_ge(s_o[u], NT // 2 * 16)


def tail(K):
    gain = lambda name: K.cols[:, K.col_at[name]:K.col_at[name] + 8]
    with ExitStack() as st:
        with ExitStack() as parts:
            x = tuple(K.sb(f"hN5_{x}", [P, KT, T], stack=parts) for x in ("hi", "lo"))
            stage_norm(K, "np", K.hF, x, T, gain("norm_ple_g_2"))
            stage_embed(K, x)
        hN = K.sb("hN6", [P, KT, T], stack=st)
        stage_norm(K, "no", K.hF, hN, T, gain("final_norm_g_2"))
        stage_turn_out(K, hN)


def program(nc, A, const_at, const, wide, out):
    with ExitStack() as stack:
        K = Core(nc, A, const_at, const, wide, out, stack)
        K.hF = K.sb("hF", [P, KT, T])
        stage_setup(K)
        mixer_one(K)
        moe(K)
        mixer_two(K)
        ffn(K)
        tail(K)


def kernel(**inputs):
    import concourse.bacc as bacc
    from concourse.bass_utils import run_bass_kernel_spmd

    nc = bacc.Bacc("TRN2", target_bir_lowering=False, num_devices=1)
    at, const, wide = constants()
    arrays, A = {}, {}
    for name, a in inputs.items():
        a = np.ascontiguousarray(a)
        if a.size:
            arrays[f"in_{name}"] = a
            A[name] = nc.dram_tensor(f"in_{name}", a.shape, mybir.dt.from_np(a.dtype), kind="ExternalInput").ap()
    tables = []
    for name, a in (("masks", const), ("window_masks", wide)):
        arrays[name] = a
        tables.append(nc.dram_tensor(name, a.shape, F32, kind="ExternalInput").ap())
    out = nc.dram_tensor("out", (1, T, D), F32, kind="ExternalOutput").ap()
    program(nc, A, at, *tables, out)
    return run_bass_kernel_spmd(nc, [arrays], core_ids=[0]).results[0]["out"]
```
